# Optimizing a Trainium2 kernel written in Bass

```python
import jax, jax.numpy as jnp
from jax import lax
import numpy as np

D_MODEL = 1024
BATCH = 1
SEQ = 1024
DEPTH = 1

CTX_LEN = 256
GRID_W = 64
W_CONV = 512
W_FNO = 512
N_FGROUPS = 4
N_HEADS = 8
HEAD_DIM = 64
W_ATTN = N_HEADS * HEAD_DIM
WIN_H = 8
WIN_W = 16
Q_BLOCK_W = 16
K_BLOCK_W = 2 * WIN_W
N_BRANCH = 3
EPS = 1e-6
NEG_INF = -1e30
D_IN = 4 * W_CONV + 2 * W_FNO + 4 * W_ATTN + N_BRANCH * D_MODEL
KV_LO = 4 * W_CONV + 2 * W_FNO + W_ATTN
KV_HI = KV_LO + 2 * W_ATTN


def rmsnorm(x, g):
    xf = x.astype(jnp.float32)
    y = xf * lax.rsqrt(jnp.mean(xf * xf, axis=-1, keepdims=True) + EPS)
    return (y * g.astype(jnp.float32)).astype(x.dtype)

def split_proj(p):
    sizes = (W_CONV,) * 4 + (W_FNO,) * 2 + (W_ATTN,) * 4 + (D_MODEL,) * N_BRANCH
    points = np.cumsum(sizes)[:-1].tolist()
    return jnp.split(p, points, axis=-1)

def heads(t):
    return t.reshape(t.shape[0], t.shape[1], N_HEADS, HEAD_DIM)

def short_conv(u, w_conv, b_conv):
    up = jnp.pad(u, ((0, 0), (1, 1), (0, 0)))
    return up[:, :-2] * w_conv[0] + up[:, 1:-1] * w_conv[1] + up[:, 2:] * w_conv[2] + b_conv

def fourier_mix(u):
    b, l, w = u.shape
    ug = u.reshape(b, l, N_FGROUPS, w // N_FGROUPS).astype(jnp.float32)
    y = jnp.fft.fft2(ug, axes=(1, 3), norm='ortho').real
    return y.reshape(b, l, w).astype(u.dtype)

def context_attention(q, k, v):
    s = jnp.einsum('bqhd,bkhd->bhqk', q, k).astype(jnp.float32) * (HEAD_DIM ** -0.5)
    p = jax.nn.softmax(s, axis=-1).astype(v.dtype)
    o = jnp.einsum('bhqk,bkhd->bqhd', p, v)
    return o.reshape(o.shape[0], o.shape[1], W_ATTN)

def neighbourhood_attention(q, k, v, k_ctx, v_ctx, rpb):
    b, s, h, dh = q.shape
    rows = s // GRID_W
    kh = min(WIN_H, rows)
    n_cb = GRID_W // Q_BLOCK_W
    scale = HEAD_DIM ** -0.5
    q = q.reshape(b, rows, n_cb, Q_BLOCK_W, h, dh)
    k = k.reshape(b, rows, GRID_W, h, dh)
    v = v.reshape(b, rows, GRID_W, h, dh)
    qcol = np.arange(GRID_W).reshape(n_cb, Q_BLOCK_W)
    kcs = np.clip(np.arange(n_cb) * Q_BLOCK_W - WIN_W // 2, 0, GRID_W - K_BLOCK_W)
    kcol = kcs[:, None] + np.arange(K_BLOCK_W)[None, :]
    cs = np.clip(qcol - WIN_W // 2, 0, GRID_W - WIN_W)
    col_ok = (kcol[:, None, :] >= cs[..., None]) & (kcol[:, None, :] < cs[..., None] + WIN_W)
    dc_idx = np.clip(kcol[:, None, :] - qcol[..., None] + WIN_W - 1, 0, 2 * WIN_W - 2)
    rpb_col = rpb[:, :, dc_idx]
    mask = col_ok[:, :, None, :]

    def row_block(r):
        rs = jnp.clip(r - kh // 2, 0, rows - kh)
        qr = lax.dynamic_index_in_dim(q, r, axis=1, keepdims=False)
        kb = lax.dynamic_slice_in_dim(k, rs, kh, axis=1)[:, :, kcol]
        vb = lax.dynamic_slice_in_dim(v, rs, kh, axis=1)[:, :, kcol]
        dr_idx = rs + jnp.arange(kh) - r + (WIN_H - 1)
        bias = jnp.take(rpb_col, dr_idx, axis=1).transpose(0, 2, 3, 1, 4).astype(jnp.float32)
        s_loc = jnp.einsum('bnqhd,binchd->bhnqic', qr, kb).astype(jnp.float32) * scale + bias
        s_loc = jnp.where(mask, s_loc, NEG_INF)
        s_ctx = jnp.einsum('bnqhd,bkhd->bhnqk', qr, k_ctx).astype(jnp.float32) * scale
        n_loc = kh * K_BLOCK_W
        sc = jnp.concatenate([s_loc.reshape(b, h, n_cb, Q_BLOCK_W, n_loc), s_ctx], axis=-1)
        p = jax.nn.softmax(sc, axis=-1).astype(v.dtype)
        p_loc = p[..., :n_loc].reshape(b, h, n_cb, Q_BLOCK_W, kh, K_BLOCK_W)
        p_ctx = p[..., n_loc:]
        return (jnp.einsum('bhnqic,binchd->bnqhd', p_loc, vb)
                + jnp.einsum('bhnqk,bkhd->bnqhd', p_ctx, v_ctx))

    o = lax.map(row_block, jnp.arange(rows))
    return o.transpose(1, 0, 2, 3, 4, 5).reshape(b, s, W_ATTN)

def merge_branches(pieces, attn_o, w_conv, b_conv, w_br_a, w_br_f, w_br_c, w_out):
    a_x, a_b, a_c, a_z, f_u, f_z, _q, _k, _v, c_z, g_a, g_f, g_c = pieces
    silu, sig = jax.nn.silu, jax.nn.sigmoid
    y_a = (a_b * short_conv(a_c * a_x, w_conv, b_conv) * silu(a_z)) @ w_br_a
    y_f = (fourier_mix(f_u) * silu(f_z)) @ w_br_f
    y_c = (attn_o * silu(c_z)) @ w_br_c
    return (sig(g_a) * y_a + sig(g_f) * y_f + sig(g_c) * y_c) @ w_out

def hybrid_layer(x, ctx, c, c_ctx, norm_g, w_ada, b_ada, w_in, b_in, w_conv, b_conv,
                 rpb, w_br_a, w_br_f, w_br_c, w_out, update_ctx):
    mod_l = jax.nn.silu(c) @ w_ada + b_ada
    mod_c = jax.nn.silu(c_ctx) @ w_ada + b_ada
    sh_l, sc_l, gt_l = jnp.split(mod_l[:, None, :], 3, axis=-1)
    sh_c, sc_c, gt_c = jnp.split(mod_c, 3, axis=-1)
    h_lat = rmsnorm(x, norm_g) * (1.0 + sc_l) + sh_l
    h_ctx = rmsnorm(ctx, norm_g) * (1.0 + sc_c) + sh_c

    pl = split_proj(h_lat @ w_in + b_in)
    if update_ctx:
        pc = split_proj(h_ctx @ w_in + b_in)
        k_c, v_c = pc[7], pc[8]
    else:
        k_c, v_c = jnp.split(h_ctx @ w_in[:, KV_LO:KV_HI] + b_in[KV_LO:KV_HI], 2, axis=-1)
    k_c, v_c = heads(k_c), heads(v_c)

    o_lat = neighbourhood_attention(heads(pl[6]), heads(pl[7]), heads(pl[8]), k_c, v_c, rpb)
    x_new = x + gt_l * merge_branches(pl, o_lat, w_conv, b_conv, w_br_a, w_br_f, w_br_c, w_out)
    if update_ctx:
        o_ctx = context_attention(heads(pc[6]), k_c, v_c)
        ctx = ctx + gt_c * merge_branches(pc, o_ctx, w_conv, b_conv, w_br_a, w_br_f, w_br_c, w_out)
    return x_new, ctx

def first_inputs(seed: int = 0) -> dict:
    key = jax.random.key(seed)
    ks = jax.random.split(key, 17)
    f32 = jnp.float32
    nrm = lambda k, shape, s: jax.random.normal(k, shape, f32) * s
    return {
        'x': nrm(ks[0], (BATCH, SEQ, D_MODEL), 1.0),
        'c': nrm(ks[1], (BATCH, D_MODEL), 1.0),
        'ctx': nrm(ks[2], (BATCH, CTX_LEN, D_MODEL), 1.0),
        'c_ctx': nrm(ks[3], (D_MODEL,), 1.0),
        'norm_g': 1.0 + nrm(ks[4], (DEPTH, D_MODEL), 0.05),
        'w_ada': nrm(ks[5], (DEPTH, D_MODEL, 3 * D_MODEL), 0.5 * D_MODEL ** -0.5),
        'b_ada': nrm(ks[6], (DEPTH, 3 * D_MODEL), 0.01),
        'w_in': nrm(ks[7], (DEPTH, D_MODEL, D_IN), D_MODEL ** -0.5),
        'b_in': nrm(ks[8], (DEPTH, D_IN), 0.01),
        'w_conv': nrm(ks[9], (DEPTH, 3, W_CONV), 3 ** -0.5),
        'b_conv': nrm(ks[10], (DEPTH, W_CONV), 0.01),
        'rpb': nrm(ks[11], (DEPTH, N_HEADS, 2 * WIN_H - 1, 2 * WIN_W - 1), 0.1),
        'w_br_a': nrm(ks[12], (DEPTH, W_CONV, D_MODEL), W_CONV ** -0.5),
        'w_br_f': nrm(ks[13], (DEPTH, W_FNO, D_MODEL), W_FNO ** -0.5),
        'w_br_c': nrm(ks[14], (DEPTH, W_ATTN, D_MODEL), W_ATTN ** -0.5),
        'w_out': nrm(ks[15], (DEPTH, D_MODEL, D_MODEL), D_MODEL ** -0.5),
        'final_g': 1.0 + nrm(ks[16], (D_MODEL,), 0.05),
    }

def first_block(x, c, ctx, c_ctx, norm_g, w_ada, b_ada, w_in, b_in, w_conv, b_conv,
              rpb, w_br_a, w_br_f, w_br_c, w_out, final_g):
    for l in range(DEPTH):
        x, ctx = hybrid_layer(x, ctx, c, c_ctx, norm_g[l], w_ada[l], b_ada[l], w_in[l], b_in[l],
                              w_conv[l], b_conv[l], rpb[l], w_br_a[l], w_br_f[l], w_br_c[l],
                              w_out[l], update_ctx=(l < DEPTH - 1))
    return rmsnorm(x, final_g)


CHUNK = 64
N_BRANCH_2 = 4
BRANCH_W = D_MODEL // N_BRANCH_2
RMS_EPS = 1e-6
NEG_BIG = -1e30
LOG_FLOOR = 1e-30
HG_HEADS = 4
HG_DK = 128
HG_DV = BRANCH_W // HG_HEADS
POOL_WINDOWS = (2, 4, 8, 16)
POOL_GROUP = BRANCH_W // len(POOL_WINDOWS)
SA_HEADS = 4
SA_DH = BRANCH_W // SA_HEADS
IDX_HEADS = 8
IDX_DH = 64
TOPK_MAX = 256
Q_BLOCK = 128
N_MEM = 256
MEM_HEADS = 4
MEM_DH = BRANCH_W // MEM_HEADS
D_FF = -(-8 * D_MODEL // (3 * 256)) * 256
SPLIT_SIZES = (HG_HEADS * HG_DK, HG_HEADS * HG_DK, BRANCH_W, BRANCH_W,
               BRANCH_W,
               SA_HEADS * SA_DH, SA_DH, SA_DH,
               IDX_HEADS * IDX_DH, IDX_DH, IDX_HEADS,
               MEM_HEADS * MEM_DH)
N_IN = sum(SPLIT_SIZES)


F32 = jnp.float32

def rms_norm(x, gain, eps=RMS_EPS):
    xf = x.astype(F32)
    y = xf * lax.rsqrt(jnp.mean(xf * xf, axis=-1, keepdims=True) + eps)
    return (y * gain.astype(F32)).astype(x.dtype)

def hgrn2_mixer(q, f_logit, i, g, lb, o_gain):
    B, T, _ = q.shape
    n = T // CHUNK
    lbf = lb.astype(F32)
    sg = jax.nn.sigmoid(f_logit.astype(F32))
    f = lbf + (1.0 - lbf) * sg
    log_f = jnp.log(jnp.maximum(f, LOG_FLOOR))
    k = (1.0 - lbf) * (1.0 - sg)
    qf = jax.nn.silu(q.astype(F32))

    def to_chunks(a, d):
        return a.reshape(B, n, CHUNK, HG_HEADS, d).transpose(1, 0, 2, 3, 4)

    xs = (to_chunks(qf, HG_DK), to_chunks(k, HG_DK), to_chunks(log_f, HG_DK),
          to_chunks(i.astype(F32), HG_DV))
    causal = jnp.tril(jnp.ones((CHUNK, CHUNK), dtype=bool))[None, :, :, None, None]

    def step(S, inp):
        qc, kc, lfc, vc = inp
        b = jnp.cumsum(lfc, axis=1)
        o_inter = jnp.einsum('bthk,bhkv->bthv', qc * jnp.exp(b), S)
        diff = jnp.where(causal, b[:, :, None] - b[:, None, :], 0.0)
        decay = jnp.where(causal, jnp.exp(diff), 0.0)
        att = jnp.einsum('bthk,bshk,btshk->bhts', qc, kc, decay)
        o_intra = jnp.einsum('bhts,bshv->bthv', att, vc)
        b_last = b[:, -1]
        S = jnp.exp(b_last)[..., None] * S + jnp.einsum(
            'bshk,bshv->bhkv', kc * jnp.exp(b_last[:, None] - b), vc)
        return S, o_inter + o_intra

    S0 = jnp.zeros((B, HG_HEADS, HG_DK, HG_DV), F32)
    _, o = lax.scan(step, S0, xs)
    o = o.transpose(1, 0, 2, 3, 4).reshape(B, T, HG_HEADS, HG_DV)
    o = o * lax.rsqrt(jnp.mean(o * o, axis=-1, keepdims=True) + RMS_EPS)
    o = o.reshape(B, T, BRANCH_W) * o_gain.astype(F32) * jax.nn.silu(g.astype(F32))
    return o.astype(q.dtype)

def pool_mixer(z, pool_w, pool_scale):
    B, T, _ = z.shape
    zf = z.astype(F32).reshape(B, T, len(POOL_WINDOWS), POOL_GROUP)
    csum = jnp.cumsum(zf, axis=1)
    pos = jnp.arange(T)
    means = []
    for gi, w in enumerate(POOL_WINDOWS):
        c = csum[:, :, gi]
        lagged = jnp.pad(c, ((0, 0), (w, 0), (0, 0)))[:, :T]
        cnt = jnp.minimum(pos + 1, w).astype(F32)
        means.append((c - lagged) / cnt[None, :, None])
    pooled = jnp.stack(means, axis=2) - zf
    y = jnp.einsum('btgc,gcd->btgd', pooled, pool_w.astype(F32)).reshape(B, T, BRANCH_W)
    return (y * pool_scale.astype(F32)).astype(z.dtype)

def dsa_mixer(q, k, v, iq, ik, iw):
    B, T, _ = q.shape
    n_sel = min(TOPK_MAX, T // 4)
    nb = T // Q_BLOCK

    def blocks(a, tail):
        return jnp.moveaxis(a.reshape((B, nb, Q_BLOCK) + tail), 1, 0)

    qb_all = blocks(q, (SA_HEADS, SA_DH))
    iqb_all = blocks(iq, (IDX_HEADS, IDX_DH))
    iwb_all = blocks(iw, (IDX_HEADS,))
    key_pos = jnp.arange(T)
    gather = jax.vmap(lambda arr, idx: arr[idx])

    def block(args):
        bi, qb, iqb, iwb = args
        qpos = bi * Q_BLOCK + jnp.arange(Q_BLOCK)
        limit = (qpos // CHUNK + 1) * CHUNK
        admissible = key_pos[None, :] < limit[:, None]
        logits = jnp.einsum('bqhd,bsd->bqsh', iqb, ik).astype(F32) * (IDX_DH ** -0.5)
        score = jnp.einsum('bqsh,bqh->bqs', jax.nn.relu(logits),
                           iwb.astype(F32) * (IDX_HEADS ** -0.5))
        score = jnp.where(admissible[None], score, NEG_BIG)
        top_val, top_idx = lax.top_k(score, n_sel)
        valid = top_val > 0.5 * NEG_BIG
        k_sel = gather(k, top_idx)
        v_sel = gather(v, top_idx)
        s = jnp.einsum('bqhd,bqkd->bhqk', qb, k_sel).astype(F32) * (SA_DH ** -0.5)
        s = jnp.where(valid[:, None], s, NEG_BIG)
        p = jax.nn.softmax(s, axis=-1)
        o = jnp.einsum('bhqk,bqkd->bqhd', p.astype(v.dtype), v_sel)
        return o.reshape(B, Q_BLOCK, SA_HEADS * SA_DH)

    out = lax.map(block, (jnp.arange(nb), qb_all, iqb_all, iwb_all))
    return jnp.moveaxis(out, 0, 1).reshape(B, T, SA_HEADS * SA_DH)

def mem_attention(qm, mk, mv):
    B, T, _ = qm.shape
    qh = qm.reshape(B, T, MEM_HEADS, MEM_DH)
    kh = mk.reshape(B, N_MEM, MEM_HEADS, MEM_DH)
    vh = mv.reshape(B, N_MEM, MEM_HEADS, MEM_DH)
    s = jnp.einsum('bthd,bnhd->bhtn', qh, kh).astype(F32) * (MEM_DH ** -0.5)
    p = jax.nn.softmax(s, axis=-1)
    o = jnp.einsum('bhtn,bnhd->bthd', p.astype(vh.dtype), vh)
    return o.reshape(B, T, MEM_HEADS * MEM_DH)

def second_inputs(seed: int = 0) -> dict:
    key = jax.random.key(seed)
    ks = jax.random.split(key, 18)
    L, D = DEPTH, D_MODEL
    nrm = lambda k, shape, fan: jax.random.normal(k, shape, F32) * (fan ** -0.5)
    gain = lambda k, shape: 1.0 + 0.1 * jax.random.normal(k, shape, F32)
    return {
        "x": jax.random.normal(ks[0], (BATCH, SEQ, D), F32),
        "mem": jax.random.normal(ks[1], (BATCH, N_MEM, D), F32),
        "lb_logits": jax.random.normal(ks[2], (L, HG_HEADS * HG_DK), F32),
        "w_in": nrm(ks[3], (L, D, N_IN), D),
        "w_gate": nrm(ks[4], (L, N_BRANCH_2, D, D), D),
        "w_branch": nrm(ks[5], (L, N_BRANCH_2, BRANCH_W, D), BRANCH_W),
        "w_out": nrm(ks[6], (L, D, D), D),
        "hgrn_norm": gain(ks[7], (L, BRANCH_W)),
        "pool_w": nrm(ks[8], (L, len(POOL_WINDOWS), POOL_GROUP, POOL_GROUP), POOL_GROUP),
        "pool_scale": gain(ks[9], (L, BRANCH_W)),
        "w_mem_kv": nrm(ks[10], (L, D, 2 * MEM_HEADS * MEM_DH), D),
        "norm_mem": gain(ks[11], (L, D)),
        "norm_mix_pre": gain(ks[12], (L, D)),
        "norm_mix_post": gain(ks[13], (L, D)),
        "norm_ffn_pre": gain(ks[14], (L, D)),
        "norm_ffn_post": gain(ks[15], (L, D)),
        "w_ffn_gate_up": nrm(ks[16], (L, D, 2 * D_FF), D),
        "w_ffn_down": nrm(ks[17], (L, D_FF, D), D_FF),
    }

def second_block(x, mem, lb_logits, w_in, w_gate, w_branch, w_out, hgrn_norm, pool_w,
              pool_scale, w_mem_kv, norm_mem, norm_mix_pre, norm_mix_post,
              norm_ffn_pre, norm_ffn_post, w_ffn_gate_up, w_ffn_down):
    split_pts = [int(p) for p in np.cumsum(SPLIT_SIZES)[:-1]]
    lb_soft = jax.nn.softmax(lb_logits.astype(F32), axis=0)
    lb_all = jnp.cumsum(lb_soft, axis=0) - lb_soft[0:1]
    h = x
    for l in range(DEPTH):
        u = rms_norm(h, norm_mix_pre[l])
        z = u @ w_in[l]
        (hq, hf, hi, hg, pz, sq, sk, sv, iq, ik, iw, mq) = jnp.split(z, split_pts, axis=-1)
        y_a = hgrn2_mixer(hq, hf, hi, hg, lb_all[l], hgrn_norm[l])
        y_b = pool_mixer(pz, pool_w[l], pool_scale[l])
        y_c = dsa_mixer(sq, sk, sv, iq, ik, iw)
        mkv = rms_norm(mem, norm_mem[l]) @ w_mem_kv[l]
        mk, mv = jnp.split(mkv, 2, axis=-1)
        y_m = mem_attention(mq, mk, mv)
        merged = None
        for bi, y in enumerate((y_a, y_b, y_c, y_m)):
            term = jax.nn.sigmoid(u @ w_gate[l, bi]) * (y @ w_branch[l, bi])
            merged = term if merged is None else merged + term
        h = h + rms_norm(merged @ w_out[l], norm_mix_post[l])
        u = rms_norm(h, norm_ffn_pre[l])
        gt, up = jnp.split(u @ w_ffn_gate_up[l], 2, axis=-1)
        h = h + rms_norm((jax.nn.silu(gt) * up) @ w_ffn_down[l], norm_ffn_post[l])
    return h


def setup_inputs(seed=0):
    out = dict(first_inputs(seed))
    for name, value in second_inputs(seed + 1).items():
        if name != "x":
            out[name + "_2"] = value
    return out


def reference(
    x, c, ctx, c_ctx, norm_g, w_ada, b_ada, w_in, b_in, w_conv, b_conv, rpb, w_br_a, w_br_f,
    w_br_c, w_out, final_g, mem_2, lb_logits_2, w_in_2, w_gate_2, w_branch_2, w_out_2,
    hgrn_norm_2, pool_w_2, pool_scale_2, w_mem_kv_2, norm_mem_2, norm_mix_pre_2,
    norm_mix_post_2, norm_ffn_pre_2, norm_ffn_post_2, w_ffn_gate_up_2, w_ffn_down_2,
):
    x = first_block(
        x, c, ctx, c_ctx, norm_g, w_ada, b_ada, w_in, b_in, w_conv, b_conv, rpb, w_br_a, w_br_f,
        w_br_c, w_out, final_g,
    )
    return second_block(
        x, mem_2, lb_logits_2, w_in_2, w_gate_2, w_branch_2, w_out_2, hgrn_norm_2, pool_w_2,
        pool_scale_2, w_mem_kv_2, norm_mem_2, norm_mix_pre_2, norm_mix_post_2, norm_ffn_pre_2,
        norm_ffn_post_2, w_ffn_gate_up_2, w_ffn_down_2,
    )


_drawn_inputs = setup_inputs


def setup_inputs(seed=0):
    import zlib

    import numpy as np

    out = dict(_drawn_inputs(seed))
    spreads = {}
    factors = {'ctx': 4.244,
     'norm_g': 2.711,
     'b_ada': 5.355,
     'b_in': 8.0,
     'b_conv': 23.064,
     'rpb': 8.0,
     'norm_mem_2': 4.351,
     'hgrn_norm_2': 3.43,
     'pool_scale_2': 2.985}
    for name, (base, spread) in spreads.items():
        noise = np.random.default_rng([zlib.crc32(name.encode()), seed]).standard_normal(out[name].shape)
        drawn = base * np.exp(spread * noise) if base else spread * noise
        out[name] = __import__('jax').numpy.asarray(drawn.astype(out[name].dtype))
    for name, factor in factors.items():
        out[name] = (out[name] * factor).astype(out[name].dtype)
    return out
```

```python
from contextlib import ExitStack

import numpy as np

import concourse.bass as bass
from concourse import mybir

P = 128
T = 1024
D = 1024
KT = D // P
TT = T // P
HALF = 512
CTX = 256
NMEM = 256
WB = 512
BW = 256
DFF = 2816
FT = DFF // P
GRID = 64
ROWS = T // GRID
WIN_H, WIN_W = 8, 16
N_DR, N_DC = 2 * WIN_H - 1, 2 * WIN_W - 1
DH = 64
CHUNK = 128
TOPK = 256
EPS = 1e-6
NEG = -1e30
TAKEN = -3e38
CREDIT = 4

F32 = mybir.dt.float32
F32R = mybir.dt.float32r
U32 = mybir.dt.uint32
ACT = mybir.ActivationFunctionType
ALU = mybir.AluOpType
AX = mybir.AxisListType.X

A_X, A_B, A_C, A_Z, F_U, F_Z, Q1, K1, V1, C_Z, G_A, G_F, G_C = (
    0, 512, 1024, 1536, 2048, 2560, 3072, 3584, 4096, 4608, 5120, 6144, 7168)
H_Q, H_F, H_I, H_G, P_Z, S_Q, S_K, S_V, I_Q, I_K, I_W, M_Q = (
    0, 512, 1024, 1280, 1536, 1792, 2048, 2112, 2176, 2688, 2752, 2760)

ROWS_A = [("norm_g", 8), ("b_ada", 24), ("b_in", 64), ("w_conv", 12), ("b_conv", 4), ("final_g", 8)]
ROWS_B = [("c", 8), ("c_ctx", 8), ("lb_logits_2", 4), ("hgrn_norm_2", 2), ("pool_scale_2", 2),
          ("norm_mem_2", 8), ("norm_mix_pre_2", 8), ("norm_mix_post_2", 8), ("norm_ffn_pre_2", 8),
          ("norm_ffn_post_2", 8)]
COL = {}
for _rows, _at in ((ROWS_A, 0), (ROWS_B, P)):
    for _name, _n in _rows:
        COL[_name] = _at
        _at += _n


def constants():
    t = np.arange(HALF)[:, None].astype(np.float64)
    k = np.arange(HALF + 1)[None, :]
    norm = 1.0 / np.sqrt(T * P)
    angle = 2 * np.pi * ((t * k) % T) / T
    c = np.arange(P)[:, None] * np.arange(P)[None, :] % P
    col = np.arange(GRID)
    start = np.clip(col - WIN_W // 2, 0, GRID - WIN_W)
    inside = (col[None, :] >= start[:, None]) & (col[None, :] < start[:, None] + WIN_W)
    s, q = np.arange(CHUNK)[:, None], np.arange(CHUNK)[None, :]
    levels = []
    for b in (64, 32, 16, 8, 4, 2, 1):
        levels.append((s // (2 * b) == q // (2 * b)) & (s % (2 * b) < b) & (q % (2 * b) >= b))
    levels.append(s == q)
    pool = np.zeros((P, 2, 16))
    for tile, ws in enumerate(((2, 4), (8, 16))):
        for half, w in enumerate(ws):
            pool[half * 64:half * 64 + 64, tile] = 1.0 / np.minimum(np.arange(16) + 1, w)
    f = np.float32
    return {
        "k_ident": np.eye(P, dtype=f),
        "k_cos": (np.cos(angle) * norm).astype(f),
        "k_sin": (np.sin(angle) * norm).astype(f),
        "k_alt": (((-1.0) ** k) * norm).astype(f),
        "k_chan": np.stack([np.cos(2 * np.pi * c / P), np.sin(2 * np.pi * c / P)], 1).astype(f),
        "k_window": np.where(np.concatenate([inside[::-1]] * 2, 0), 0.0, NEG).astype(f),
        "k_levels": np.stack(levels, 1).astype(f),
        "k_pool": pool.astype(f),
        "k_blocks": np.kron(np.eye(2), np.ones((64, 64))).astype(f),
    }


class Signal:

    def __init__(self, sem, unit=1):
        self.sem, self.unit, self.base = sem, unit, CREDIT if unit == 1 else 0

    def at(self, k, i=0, per=0):
        return i * (per * self.unit) + (self.base + k * self.unit)

    def passed(self, units):
        self.base += units * self.unit


class Steps:

    def __init__(self, counted):
        self.counted, self.k, self.i, self.per = counted, 0, 0, 0

    def open(self, i, per):
        self.i, self.per, self.k = i, per, 0

    def done(self, instruction):
        instruction.then_inc(self.counted.sem, 1)
        self.k += 1

    def wait(self, engine, k=None):
        engine.wait_ge(self.counted.sem, self.counted.at(self.k if k is None else k, self.i, self.per))

    def close(self, loops=1):
        assert self.per in (0, self.k), ("steps of one iteration", self.per, self.k)
        self.counted.passed(self.k * loops)
        self.k = self.per = self.i = 0


def first_then_second_block(nc, a, out):
    ctx = ExitStack()
    with ctx:
        sem_list = []
        names = {}

        def signal(name, unit=1):
            s = Signal(ctx.enter_context(nc.semaphore(name)), unit)
            sem_list.append(s)
            return s

        def sb(scope, name, shape, dt=F32, side=None):
            names[name] = names.get(name, 0) + 1
            full = name if names[name] == 1 else f"{name}_{names[name]}"
            return scope.enter_context(nc.sbuf_tensor(full, shape, dt, side=side))

        raw = sb(ctx, "raw", [P, 2, KT, P])
        w_hi = sb(ctx, "w_hi", [P, 2, KT, P], F32R)
        w_lo = sb(ctx, "w_lo", [P, 2, KT, P], F32R)
        h_hi = sb(ctx, "h_hi", [P, KT, T], F32R)
        h_lo = sb(ctx, "h_lo", [P, KT, T], F32R)
        vec = sb(ctx, "vec", [P, 2 * P])
        ident = sb(ctx, "ident", [P, P])
        ones = sb(ctx, "ones", [P, P])
        gate_t = sb(ctx, "gate_t", [P, KT])
        q_bias = sb(ctx, "q_bias", [P, 4])
        carrier = sb(ctx, "carrier", [P, 4])
        lb = sb(ctx, "lb", [P, 8])
        ps = [ctx.enter_context(nc.psum_tensor(f"ps{n}", [P, 2 * HALF], F32)) for n in range(4)]

        loaded = [signal(f"weights_loaded{s}", 16) for s in range(2)]
        rounded = signal("weights_rounded")
        split = signal("weights_split")
        used = signal("weights_used")
        const_loaded = signal("const_loaded", 16)
        x_loaded = signal("x_loaded", 16)
        side_loaded = signal("side_loaded", 16)
        tabs = [signal(f"table_loaded{s}", 16) for s in range(2)]
        stored = signal("stored", 16)
        evicted = signal("evicted")
        evicted2 = signal("evicted2")
        h_ready = signal("h_ready")
        hi_ready = signal("hi_ready")
        lo_ready = signal("lo_ready")
        transposed = signal("transposed")
        tr_evicted = signal("tr_evicted")
        scores = signal("scores_ready")
        biased = signal("biased")
        exped = signal("exped")
        probs = signal("probs_ready")
        pt_ready = signal("pt_ready")
        pt_evicted = signal("pt_evicted")
        o_ready = signal("o_ready")
        o_evicted = signal("o_evicted")
        y_ready = signal("y_ready")
        y_hi = signal("y_hi")
        mod_ready = signal("mod_ready")
        norm_ready = signal("norm_ready")
        stat_ready = signal("stat_ready")
        sq_ready = signal("sq_ready")
        sum_ready = signal("sum_ready")
        aux = signal("aux")
        aux2 = signal("aux2")
        aux3 = signal("aux3")
        aux4 = signal("aux4")
        act_steps = Steps(signal("act_steps"))
        dve_steps = Steps(signal("dve_steps"))
        top_steps = Steps(signal("top_steps"))

        chunks = [0]

        def column(name, t=0, n=1):
            return vec[:, COL[name] + t:COL[name] + t + n]

        def carry_wait(k):
            return nc.vector.memset(carrier[:, k:k + 1], 0.0)

        def after(sig, m, i, per):
            return sig.at(chunks[0] + m + 1, i, per)

        def load_chunk(sp, m, i, per, pieces):
            sp.wait_ge(split.sem, after(split, m - 2, i, per))
            s = m % 2
            dst, src = pieces(raw[:, s])
            sp.dma_start(dst, src).then_inc(loaded[s].sem, 16)

        def stream(sp, iters, per, source, following, each=None):
            def body(i, last):
                if each:
                    each(sp, i)
                for m in range(2, per + 2):
                    if m < per:
                        load_chunk(sp, m, i, per, source(i, m))
                    elif not last:
                        load_chunk(sp, m, i, per, source(i + 1, m - per))
                    elif following:
                        load_chunk(sp, m, i, per, following(0, m - per))
            if iters > 1:
                with sp.Fori(0, iters - 1) as i:
                    body(i, False)
            body(iters - 1, True)

        def round_chunk(act, m, i, per, kt=KT):
            s = m % 2
            act.wait_ge(loaded[s].sem, loaded[s].at((chunks[0] + m - s) // 2 + 1, i, per // 2))
            act.wait_ge(used.sem, after(used, m - 2, i, per))
            act.activation(w_hi[:, s, 0:kt], raw[:, s, 0:kt], ACT.Copy).then_inc(rounded.sem, 1)

        def rest_chunk(pool, m, i, per, kt=KT):
            s = m % 2
            pool.wait_ge(rounded.sem, after(rounded, m, i, per))
            pool.tensor_tensor(w_lo[:, s, 0:kt], raw[:, s, 0:kt], w_hi[:, s, 0:kt].bitcast(F32),
                               ALU.subtract).then_inc(split.sem, 1)

        def split_ready(pe, m, i, per):
            pe.wait_ge(split.sem, after(split, m, i, per))

        def product(pe, s, outs, kt=KT, arrived=None, part=(0, 1)):
            order = [(k, o) for o in outs for k in range(kt)] if arrived is None else \
                    [(k, o) for k in range(kt) for o in outs]
            for k, (dst, hi, lo) in order[len(order) * part[0] // part[1]:len(order) * (part[0] + 1) // part[1]]:
                if arrived and dst is outs[0][0]:
                    arrived(k)
                for n, (w, x) in enumerate(((w_hi, hi), (w_hi, lo), (w_lo, hi))):
                    last = pe.matmul(dst, w[:, s, k], x(k), start=(k == 0 and n == 0), stop=(k == kt - 1 and n == 2))
            return last

        def halves(dst, hi, lo):
            def cut(x, c):
                return lambda k: x[:, k, c:c + HALF]
            return [(dst[:, c:c + HALF], cut(hi, c), cut(lo, c)) for c in (0, HALF)]

        def wide(dst):
            return halves(dst, h_hi, h_lo)

        def chunk_of(w, col):
            kt = w.shape[0] // P
            src = w.rearrange("(k p) n -> p k n", p=P)
            return lambda slot: (slot[:, 0:kt], src[:, :, bass.ds(col, P)])

        w_in, w_in2 = a["w_in"][0], a["w_in_2"][0]
        w_gate2, w_branch2 = a["w_gate_2"][0], a["w_branch_2"][0]
        def attention_source(i, m):
            return chunk_of(w_in, (Q1, K1, V1, C_Z)[m] + i * P)

        def setup(hc_hi, hc_lo, rpb_rows):
            with ExitStack() as sc, nc.Block() as block:
                rows = sb(sc, "rows", [P, 2, P])
                rpb_pad = sb(sc, "rpb_pad", [8 * N_DR, P])
                x_tok = sb(sc, "x_tok", [P, TT, D])
                c_tok = sb(sc, "c_tok", [P, CTX // P, D])
                w_ada = sb(sc, "w_ada", [P, 2, KT, 2 * P])
                sums = sb(sc, "sums", [P, 10])
                rstd = sb(sc, "rstd", [P, 10])
                power = sb(sc, "power", [P, 10])
                cond = sb(sc, "cond", [P, KT, 2])
                mods = sb(sc, "mods", [P, 3 * KT, 2])
                scale = sb(sc, "scale", [P, KT, 2])
                shift = sb(sc, "shift", [P, KT, 2])
                lb_tmp = sb(sc, "lb_tmp", [P, 8])
                h32 = sb(sc, "h32", [P, 2, T])
                ada = a["w_ada"][0].rearrange("(k p) n -> p k n", p=P)
                n_rows = len(ROWS_A) + len(ROWS_B)

                @block.sync
                def _(sp):
                    sp.wait_ge(aux.sem, aux.at(1))
                    for names, which in ((ROWS_A, 0), (ROWS_B, 1)):
                        for name, n in names:
                            at = COL[name] - which * P
                            flat = a[name]
                            while len(flat.shape) > 1:
                                flat = flat.rearrange("a b ... -> (a b) ...")
                            sp.dma_start(rows[at:at + n, which, :], flat.rearrange("(t p) -> t p", p=P))\
                              .then_inc(const_loaded.sem, 16)
                    sp.dma_start(ident[:], a["k_ident"]).then_inc(const_loaded.sem, 16)
                    sp.dma_start(x_tok[:], a["x"][0].rearrange("(t p) d -> p t d", p=P)).then_inc(x_loaded.sem, 16)
                    sp.dma_start(c_tok[:], a["ctx"][0].rearrange("(t p) d -> p t d", p=P)).then_inc(x_loaded.sem, 16)
                    for s in range(2):
                        sp.dma_start(w_ada[:, s], ada[:, :, s * 256:s * 256 + 256]).then_inc(tabs[s].sem, 16)
                    with sp.Fori(0, 5) as i:
                        for s in range(2):
                            sp.wait_ge(aux2.sem, aux2.at(s + 1, i, 2))
                            sp.dma_start(w_ada[:, s], ada[:, :, bass.ds(i * 512 + (512 + s * 256), 256)])\
                              .then_inc(tabs[s].sem, 16)
                    for m in range(2):
                        load_chunk(sp, m, 0, 4, attention_source(0, m))

                @block.gpsimd
                def _(pool):
                    for s in sem_list:
                        if s.unit == 1:
                            pool.sem_inc(s.sem, CREDIT)
                    pool.memset(rows[:], 0.0).then_inc(aux.sem, 1)
                    pool.memset(rpb_pad[:], 0.0).then_inc(aux3.sem, 1)
                    pool.memset(power[:], -0.5).then_inc(mod_ready.sem, 1)
                    pool.memset(ones[:], 1.0).then_inc(mod_ready.sem, 1)
                    pool.wait_ge(stat_ready.sem, stat_ready.at(1))
                    pool.wait_ge(mod_ready.sem, mod_ready.at(2))
                    pool.tensor_tensor(rstd[:], sums[:], power[:], ALU.pow).then_inc(norm_ready.sem, 1)
                    rest_chunk(pool, 0, 0, 4)

                @block.scalar
                def _(act):
                    act.wait_ge(aux3.sem, aux3.at(1))
                    act.dma_start(rpb_pad[:, 48:48 + N_DC], a["rpb"][0].rearrange("h r c -> (h r) c"))\
                       .then_inc(side_loaded.sem, 16)
                    act.wait_ge(side_loaded.sem, side_loaded.at(1))
                    act.dma_start(rpb_rows, rpb_pad[:]).then_inc(stored.sem, 16)
                    act.wait_ge(aux4.sem, aux4.at(1))
                    for v, name in enumerate(("c", "c_ctx")):
                        act.activation(cond[:, :, v], column(name, 0, KT), ACT.Silu).then_inc(y_ready.sem, 1)
                    act.wait_ge(x_loaded.sem, x_loaded.at(2))
                    for t in range(10):
                        src = x_tok[:, t] if t < TT else c_tok[:, t - TT]
                        act_steps.wait(act)
                        act_steps.done(act.activation(h32[:, 0], src, ACT.Square, accum_out=sums[:, t:t + 1]))
                    act.wait_ge(biased.sem, biased.at(1))
                    act.activation(lb_tmp[:, 4:8], lb_tmp[:, 0:4], ACT.Exp).then_inc(exped.sem, 1)
                    round_chunk(act, 0, 0, 4)
                    act.wait_ge(probs.sem, probs.at(1))
                    for d in range(KT):
                        act.wait_ge(transposed.sem, transposed.at(1 + d + 1))
                        act.wait_ge(lo_ready.sem, lo_ready.at(d - 1))
                        act.activation(h32[:, d % 2], ps[d % 2][:], ACT.Identity, bias=shift[:, d, 0:1],
                                       scale=scale[:, d, 0:1]).then_inc(h_ready.sem, 1)
                    for g in range(2):
                        act.wait_ge(transposed.sem, transposed.at(9 + g + 1))
                        act.wait_ge(lo_ready.sem, lo_ready.at(8 + g - 1))
                        for d in range(4):
                            act.activation(h32[:, g, d * CTX:(d + 1) * CTX],
                                           ps[2 + g][:, d * CTX:(d + 1) * CTX], ACT.Identity,
                                           bias=shift[:, 4 * g + d, 1:2],
                                           scale=scale[:, 4 * g + d, 1:2]).then_inc(h_ready.sem, 1)

                @block.vector
                def _(dve):
                    dve.wait_ge(transposed.sem, transposed.at(1))
                    dve.tensor_copy(vec[:], ps[0][:, 0:2 * P]).then_inc(aux4.sem, 1)
                    dve.wait_ge(act_steps.counted.sem, act_steps.counted.at(10))
                    dve.tensor_scalar(sums[:], sums[:], 1.0 / D, EPS, ALU.mult, ALU.add).then_inc(stat_ready.sem, 1)
                    dve.wait_ge(norm_ready.sem, norm_ready.at(1))
                    for t in range(10):
                        src = x_tok[:, t] if t < TT else c_tok[:, t - TT]
                        dve.tensor_scalar(src, src, rstd[:, t:t + 1], None, ALU.mult).then_inc(sq_ready.sem, 1)
                    dve.wait_ge(aux4.sem, aux4.at(1))
                    lbl = column("lb_logits_2", 0, 4)
                    dve.tensor_tensor(lb_tmp[:, 0:4], lbl, lbl, ALU.subtract).then_inc(biased.sem, 1)
                    dve.wait_ge(exped.sem, exped.at(1))
                    dve_steps.done(dve.reciprocal(lb_tmp[:, 0:4], lb_tmp[:, 4:8]))
                    dve_steps.wait(dve)
                    dve_steps.done(dve.tensor_tensor(lb_tmp[:, 4:8], lb_tmp[:, 4:8], lb_tmp[:, 0:4], ALU.mult))
                    dve_steps.wait(dve)
                    dve_steps.done(dve.tensor_tensor(lb[:, 0:4], lb_tmp[:, 4:8], lb_tmp[:, 4:8], ALU.subtract))
                    dve_steps.wait(dve)
                    dve_steps.done(dve.tensor_scalar(lb[:, 4:8], lb[:, 0:4], -1.0, 1.0, ALU.mult, ALU.add))
                    dve_steps.done(dve.tensor_scalar(q_bias[:], column("b_in", Q1 // P, 4), DH ** -0.5, None, ALU.mult))
                    with dve.Fori(0, 6) as i:
                        for s in range(2):
                            dve.wait_ge(aux2.sem, aux2.at(s + 1, i, 2))
                            dve.tensor_copy(mods[:, bass.ds(i * 4 + 2 * s, 2), :],
                                            ps[3][:, s * HALF:s * HALF + 4].rearrange("p (j v) -> p j v", v=2))\
                               .then_inc(evicted.sem, 1)
                    dve.wait_ge(evicted.sem, evicted.at(12))
                    for v in range(2):
                        dve_steps.done(dve.tensor_tensor(shift[:, :, v], mods[:, 0:KT, v], column("b_ada", 0, KT), ALU.add))
                        dve_steps.done(dve.tensor_tensor(scale[:, :, v], mods[:, KT:2 * KT, v], column("b_ada", KT, KT), ALU.add))
                        dve_steps.wait(dve)
                        dve_steps.done(dve.scalar_tensor_tensor(out=scale[:, :, v], in0=scale[:, :, v], scalar=1.0,
                                                                in1=column("norm_g", 0, KT), op0=ALU.add, op1=ALU.mult))
                    dve.tensor_tensor(gate_t[:], mods[:, 2 * KT:, 0], column("b_ada", 2 * KT, KT), ALU.add)\
                       .then_inc(probs.sem, 1)
                    for d in range(KT):
                        dve.wait_ge(h_ready.sem, h_ready.at(d + 1))
                        dve.tensor_copy(h_hi[:, d], h32[:, d % 2]).then_inc(hi_ready.sem, 1)
                        dve.wait_ge(hi_ready.sem, hi_ready.at(d + 1))
                        dve.tensor_tensor(h_lo[:, d], h32[:, d % 2], h_hi[:, d].bitcast(F32), ALU.subtract)\
                           .then_inc(lo_ready.sem, 1)
                    for g in range(2):
                        dve.wait_ge(h_ready.sem, h_ready.at(KT + 4 * g + 4))
                        src = h32[:, g].rearrange("p (d t) -> p d t", d=4)
                        dve.tensor_copy(hc_hi[:, 4 * g:4 * g + 4], src).then_inc(hi_ready.sem, 1)
                        dve.wait_ge(hi_ready.sem, hi_ready.at(KT + g + 1))
                        dve.tensor_tensor(hc_lo[:, 4 * g:4 * g + 4], src, hc_hi[:, 4 * g:4 * g + 4].bitcast(F32), ALU.subtract)\
                           .then_inc(lo_ready.sem, 1)

                @block.tensor
                def _(pe):
                    pe.wait_ge(const_loaded.sem, const_loaded.at(n_rows + 1))
                    for which in range(2):
                        last = pe.transpose(ps[0][:, which * P:which * P + P], rows[:, which], ident[:])
                    last.then_inc(transposed.sem, 1)
                    pe.wait_ge(y_ready.sem, y_ready.at(2))
                    with pe.Fori(0, 6) as i:
                        for s in range(2):
                            pe.wait_ge(tabs[s].sem, tabs[s].at(1, i, 1))
                            pe.wait_ge(evicted.sem, evicted.at(s - 1, i, 2))
                            for j in range(2):
                                for k in range(KT):
                                    last = pe.matmul(ps[3][:, s * HALF + 2 * j:s * HALF + 2 * j + 2],
                                                     w_ada[:, s, k, j * P:j * P + P], cond[:, k],
                                                     start=(k == 0), stop=(k == KT - 1))
                            last.then_inc(aux2.sem, 1)
                    pe.wait_ge(sq_ready.sem, sq_ready.at(10))
                    pe.wait_ge(aux4.sem, aux4.at(1))
                    for d in range(KT):
                        pe.wait_ge(h_ready.sem, h_ready.at(d - 1))
                        for t in range(TT):
                            last = pe.transpose(ps[d % 2][:, t * P:t * P + P], x_tok[:, t, d * P:d * P + P], ident[:])
                        last.then_inc(transposed.sem, 1)
                    pe.wait_ge(evicted.sem, evicted.at(12))
                    for g in range(2):
                        for d in range(4):
                            for t in range(2):
                                last = pe.transpose(ps[2 + g][:, d * CTX + t * P:d * CTX + t * P + P],
                                                    c_tok[:, t, (4 * g + d) * P:(4 * g + d + 1) * P], ident[:])
                        last.then_inc(transposed.sem, 1)

            const_loaded.passed(n_rows + 1)
            x_loaded.passed(2)
            side_loaded.passed(1)
            stored.passed(1)
            for t in tabs:
                t.passed(6)
            act_steps.close()
            dve_steps.close()
            for s, n in ((aux, 1), (aux2, 12), (aux3, 1), (aux4, 1), (mod_ready, 2), (stat_ready, 1), (norm_ready, 1),
                         (y_ready, 2), (sq_ready, 10), (biased, 1), (exped, 1), (probs, 1), (transposed, 11),
                         (h_ready, 16), (hi_ready, 10), (lo_ready, 10), (evicted, 12)):
                s.passed(n)

        def attention(hc_hi, hc_lo, rpb_rows, y_hi_t, y_lo_t, following):
            N = 4
            KEYS = WIN_H * GRID
            ALL = KEYS + CTX
            with ExitStack() as sc, nc.Block() as block:
                diag_all = sb(sc, "diag_all", [P, 4, N_DR, GRID])
                window = sb(sc, "window", [P, GRID])
                bias = sb(sc, "bias", [P, N_DR, GRID])
                q_blk = sb(sc, "q_blk", [P, ROWS, P])
                k_t = sb(sc, "k_t", [P, T])
                kc_t = sb(sc, "kc_t", [P, CTX])
                v_t = sb(sc, "v_t", [P, T])
                y32 = v_t
                vc_t = sb(sc, "vc_t", [P, CTX])
                v_even = sb(sc, "v_even", [P, TT, P])
                v_odd = sb(sc, "v_odd", [P, TT - 1, P])
                v_ctx = sb(sc, "v_ctx", [P, CTX // P, P])
                z_silu = sb(sc, "z_silu", [P, T])
                prob = sb(sc, "prob", [P, 2, ALL])
                prob_t = sb(sc, "prob_t", [P, 2, ALL // P, P])
                stat = sb(sc, "stat", [P, 2, 8])
                minus = sb(sc, "minus", [P, 1])

                def row_start(r):
                    return min(max(r - WIN_H // 2, 0), ROWS - WIN_H)

                def value_tiles(r):
                    rs = row_start(r)
                    src = v_even if rs % 2 == 0 else v_odd
                    return [src[:, rs // 2 + j] for j in range(4)] + [v_ctx[:, j] for j in range(2)]

                @block.sync
                def _(sp):
                    sp.wait_ge(stored.sem, stored.at(0))
                    sp.dma_start(window[:], a["k_window"]).then_inc(side_loaded.sem, 16)
                    for pair in range(4):
                        for half in range(2):
                            src = bass.AP(rpb_rows.tensor, (2 * pair + half) * N_DR * P, [[1, GRID], [P, N_DR], [1, GRID]])
                            sp.dma_start(diag_all[half * 64:half * 64 + 64, pair], src).then_inc(side_loaded.sem, 16)
                    stream(sp, N, 4, attention_source, following)

                @block.gpsimd
                def _(pool):
                    pool.memset(q_blk[:], 0.0).then_inc(aux.sem, 1)
                    pool.memset(minus[:], -1.0).then_inc(aux.sem, 1)
                    with pool.Fori(0, N) as i:
                        for m in range(4):
                            rest_chunk(pool, m + 1, i, 4)
                        pool.wait_ge(y_hi.sem, y_hi.at(1, i, 1))
                        pool.tensor_tensor(y_lo_t[:, bass.ds(i, 1)], y32[:].rearrange("p (a t) -> p a t", a=1),
                                           y_hi_t[:, bass.ds(i, 1)].bitcast(F32), ALU.subtract)\
                            .then_inc(y_ready.sem, 1)

                @block.scalar
                def _(act):
                    act.wait_ge(aux.sem, aux.at(2))
                    with act.Fori(0, N) as i:
                        round_chunk(act, 1, i, 4)
                        act.wait_ge(used.sem, after(used, 0, i, 4))
                        for half in range(2):
                            p0 = half * 64
                            last = act.activation(q_blk[p0:p0 + 64, :, p0:p0 + 64][:, :, ::-1],
                                                  ps[0][p0:p0 + 64].rearrange("p (r c) -> p r c", c=GRID), ACT.Identity,
                                                  bias=q_bias[p0:p0 + 64, bass.ds(i, 1)], scale=DH ** -0.5)
                        last.then_inc(evicted.sem, 1)
                        round_chunk(act, 2, i, 4)
                        round_chunk(act, 3, i, 4)
                        act.wait_ge(used.sem, after(used, 2, i, 4))
                        act.wait_ge(y_ready.sem, y_ready.at(0, i, 1))
                        act.activation(v_t[:], ps[0][:], ACT.Identity, bias=vec[:, bass.ds(i + (COL["b_in"] + V1 // P), 1)])
                        act.activation(vc_t[:], ps[2][:, HALF:HALF + CTX], ACT.Identity,
                                       bias=vec[:, bass.ds(i + (COL["b_in"] + V1 // P), 1)]).then_inc(h_ready.sem, 1)
                        round_chunk(act, 4, i, 4)
                        act.wait_ge(used.sem, after(used, 3, i, 4))
                        act.activation(z_silu[:], ps[1][:], ACT.Silu,
                                       bias=vec[:, bass.ds(i + (COL["b_in"] + C_Z // P), 1)]).then_inc(mod_ready.sem, 1)
                        act.wait_ge(transposed.sem, transposed.at(1, i, 3))
                        act.activation(v_even[:], ps[3][:].rearrange("p (t c) -> p t c", c=P), ACT.Copy)\
                           .then_inc(tr_evicted.sem, 1)

                        def exps(r):
                            b = r % 2
                            act.wait_ge(biased.sem, biased.at(r + 1, i, ROWS))
                            act.activation(prob[:, b, 0:KEYS], prob[:, b, 0:KEYS], ACT.Exp, bias=stat[:, b, 2:3],
                                           accum_out=stat[:, b, 3:4])
                            act.activation(prob[:, b, KEYS:ALL], ps[b][:, HALF:HALF + CTX], ACT.Exp, bias=stat[:, b, 2:3],
                                           accum_out=stat[:, b, 4:5]).then_inc(exped.sem, 1)

                        def evict_probs(r):
                            act.wait_ge(pt_ready.sem, pt_ready.at(r + 1, i, ROWS))
                            act.wait_ge(o_ready.sem, o_ready.at(r - 1, i, ROWS))
                            act.activation(prob_t[:, r % 2], ps[2][:, 0:ALL].rearrange("p (j c) -> p j c", c=P), ACT.Copy)\
                               .then_inc(pt_evicted.sem, 1)

                        exps(0)
                        for r in range(ROWS):
                            if r + 1 < ROWS:
                                exps(r + 1)
                            evict_probs(r)
                        act.wait_ge(o_evicted.sem, o_evicted.at(4, i, 4))
                        act.activation(y_hi_t[:, bass.ds(i, 1)], y32[:].rearrange("p (a t) -> p a t", a=1), ACT.Copy)\
                           .then_inc(y_hi.sem, 1)

                @block.vector
                def _(dve):
                    dve.wait_ge(side_loaded.sem, side_loaded.at(9))
                    dve.wait_ge(aux.sem, aux.at(2))
                    with dve.Fori(0, N) as i:
                        dve.tensor_tensor(bias[:], diag_all[:, bass.ds(i, 1)].rearrange("p a r c -> p (a r) c"),
                                          window[:].rearrange("p (a c) -> p a c", a=1).broadcast_to([P, N_DR, GRID]),
                                          ALU.add).then_inc(aux2.sem, 1)
                        dve.wait_ge(used.sem, after(used, 1, i, 4))
                        kb = vec[:, bass.ds(i + (COL["b_in"] + K1 // P), 1)]
                        dve.tensor_scalar(k_t[:], ps[1][:], kb, None, ALU.add)
                        dve.tensor_scalar(kc_t[:], ps[2][:, 0:CTX], kb, None, ALU.add).then_inc(evicted2.sem, 1)
                        dve.wait_ge(transposed.sem, transposed.at(2, i, 3))
                        dve.tensor_copy(v_odd[:], ps[2][:, 0:(TT - 1) * P].rearrange("p (t c) -> p t c", c=P))
                        dve.wait_ge(transposed.sem, transposed.at(3, i, 3))
                        dve.tensor_copy(v_ctx[:], ps[0][:, 0:CTX].rearrange("p (t c) -> p t c", c=P))\
                           .then_inc(aux3.sem, 1)
                        dve.wait_ge(aux2.sem, aux2.at(1, i, 1))

                        def bias_scores(r):
                            b = r % 2
                            dr = row_start(r) - r + WIN_H - 1
                            dve.wait_ge(scores.sem, scores.at(r + 1, i, ROWS))
                            dve.wait_ge(pt_ready.sem, pt_ready.at(r - 1, i, ROWS))
                            dve_steps.done(dve.reduce_max(stat[:, b, 1:2], ps[b][:, HALF:HALF + CTX], AX))
                            dve_steps.done(dve.tensor_tensor_reduce(
                                prob[:, b, 0:KEYS], ps[b][:, 0:KEYS], bias[:, dr:dr + WIN_H].rearrange("p r c -> p (r c)"),
                                1.0, -3e38, ALU.add, ALU.max, stat[:, b, 0:1]))
                            dve_steps.wait(dve)
                            dve.scalar_tensor_tensor(out=stat[:, b, 2:3], in0=stat[:, b, 0:1], scalar=stat[:, b, 1:2],
                                                     in1=minus[:], op0=ALU.max, op1=ALU.mult).then_inc(biased.sem, 1)

                        def normalise(r):
                            b = r % 2
                            dve.wait_ge(exped.sem, exped.at(r + 1, i, ROWS))
                            dve_steps.done(dve.tensor_tensor(stat[:, b, 5:6], stat[:, b, 3:4], stat[:, b, 4:5], ALU.add))
                            dve_steps.wait(dve)
                            dve_steps.done(dve.reciprocal(stat[:, b, 6:7], stat[:, b, 5:6]))
                            dve_steps.wait(dve)
                            dve.tensor_scalar(prob[:, b], prob[:, b], stat[:, b, 6:7], None, ALU.mult).then_inc(probs.sem, 1)

                        def evict_o(g):
                            dve.wait_ge(o_ready.sem, o_ready.at(4 * g + 4, i, ROWS))
                            if g == 0:
                                dve.wait_ge(mod_ready.sem, mod_ready.at(1, i, 1))
                            o = ps[3][:, (g % 2) * HALF:(g % 2) * HALF + HALF].rearrange("p (r c) -> p r c", c=P)
                            for half in range(2):
                                p0 = half * 64
                                cols = slice(g * 256, g * 256 + 256)
                                last = dve.tensor_tensor(
                                    y32[p0:p0 + 64, cols].rearrange("p (r c) -> p r c", c=64), o[p0:p0 + 64, :, p0:p0 + 64][:, :, ::-1],
                                    z_silu[p0:p0 + 64, cols].rearrange("p (r c) -> p r c", c=64), ALU.mult)
                            last.then_inc(o_evicted.sem, 1)

                        dve_steps.open(i, 4 * ROWS)
                        bias_scores(0)
                        for r in range(ROWS):
                            if r + 1 < ROWS:
                                bias_scores(r + 1)
                            normalise(r)
                            if r >= 5 and (r - 5) % 4 == 0:
                                evict_o((r - 5) // 4)
                        evict_o(3)

                @block.tensor
                def _(pe):
                    with pe.Fori(0, N) as i:
                        def ctx_part(dst, s):
                            return [(dst, lambda k: hc_hi[:, k], lambda k: hc_lo[:, k])]

                        split_ready(pe, 0, i, 4)
                        product(pe, 0, wide(ps[0])).then_inc(used.sem, 1)
                        split_ready(pe, 1, i, 4)
                        product(pe, 1, wide(ps[1]) + ctx_part(ps[2][:, 0:CTX], 1)).then_inc(used.sem, 1)
                        split_ready(pe, 2, i, 4)
                        pe.wait_ge(evicted.sem, evicted.at(1, i, 1))
                        product(pe, 0, wide(ps[0]) + ctx_part(ps[2][:, HALF:HALF + CTX], 0)).then_inc(used.sem, 1)
                        split_ready(pe, 3, i, 4)
                        pe.wait_ge(evicted2.sem, evicted2.at(1, i, 1))
                        product(pe, 1, wide(ps[1])).then_inc(used.sem, 1)
                        pe.wait_ge(h_ready.sem, h_ready.at(1, i, 1))
                        pe.wait_ge(o_evicted.sem, o_evicted.at(0, i, 4))
                        for t in range(TT):
                            last = pe.transpose(ps[3][:, t * P:t * P + P], v_t[:, t * P:t * P + P], ident[:])
                        last.then_inc(transposed.sem, 1)
                        for t in range(TT - 1):
                            last = pe.transpose(ps[2][:, t * P:t * P + P], v_t[:, t * P + 64:t * P + 64 + P], ident[:])
                        last.then_inc(transposed.sem, 1)
                        for t in range(CTX // P):
                            last = pe.transpose(ps[0][:, t * P:t * P + P], vc_t[:, t * P:t * P + P], ident[:])
                        last.then_inc(transposed.sem, 1)

                        def score(r):
                            first = row_start(r) * GRID
                            pe.matmul(ps[r % 2][:, 0:KEYS], q_blk[:, r], k_t[:, first:first + KEYS], start=True, stop=True)
                            pe.matmul(ps[r % 2][:, HALF:HALF + CTX], q_blk[:, r], kc_t[:], start=True, stop=True)\
                              .then_inc(scores.sem, 1)

                        def turn(r):
                            pe.wait_ge(probs.sem, probs.at(r + 1, i, ROWS))
                            pe.wait_ge(pt_evicted.sem, pt_evicted.at(r, i, ROWS))
                            for j in range(ALL // P):
                                last = pe.transpose(ps[2][:, j * P:j * P + P], prob[:, r % 2, j * P:j * P + P], ident[:])
                            last.then_inc(pt_ready.sem, 1)

                        def weigh(r):
                            pe.wait_ge(pt_evicted.sem, pt_evicted.at(r + 1, i, ROWS))
                            if r % 4 == 0 and r >= 8:
                                pe.wait_ge(o_evicted.sem, o_evicted.at(r // 4 - 1, i, 4))
                            at = (r // 4 % 2) * HALF + r % 4 * P
                            for j, v in enumerate(value_tiles(r)):
                                last = pe.matmul(ps[3][:, at:at + P], v, prob_t[:, r % 2, j], start=(j == 0), stop=(j == 5))
                            last.then_inc(o_ready.sem, 1)

                        pe.wait_ge(aux3.sem, aux3.at(1, i, 1))
                        pe.wait_ge(mod_ready.sem, mod_ready.at(1, i, 1))
                        pe.wait_ge(tr_evicted.sem, tr_evicted.at(1, i, 1))
                        score(0)
                        for r in range(ROWS):
                            if r + 1 < ROWS:
                                score(r + 1)
                            if r >= 1:
                                weigh(r - 1)
                            turn(r)
                        weigh(ROWS - 1)

            dve_steps.close(N)
            side_loaded.passed(9)
            for s, n in ((aux, 2), (evicted, N), (evicted2, N), (h_ready, N), (mod_ready, N), (transposed, 3 * N),
                         (tr_evicted, N), (aux2, N), (aux3, N), (scores, ROWS * N), (biased, ROWS * N), (exped, ROWS * N),
                         (probs, ROWS * N), (pt_ready, ROWS * N), (pt_evicted, ROWS * N), (o_ready, ROWS * N),
                         (o_evicted, 4 * N), (y_hi, N), (y_ready, N)):
                s.passed(n)
            chunk_passed(N * 4)

        def chunk_passed(n):
            chunks[0] += n

        def merged_tile(i, j):
            return i * -2 + (KT - 2 + j)

        def merge_source(branches):
            def source(i, m):
                gate_w, gate_col, _, branch_w, _, _, _ = branches[m // 2 % len(branches)]
                first = (KT - 2 + m // 2 // len(branches)) * P
                return (chunk_of(gate_w, i * (-2 * P) + (first + gate_col)) if m % 2 == 0 else
                        chunk_of(branch_w, i * (-2 * P) + first))
            return source

        def merge(acc, branches, accumulate, following, beside=None, early=None):
            units = [(tile, b) for tile in range(2) for b in range(len(branches))]
            N, U = KT // 2, len(units)
            per = 2 * U
            with ExitStack() as sc, nc.Block() as block:
                sig = sb(sc, "sig", [P, 2, T])
                part = sb(sc, "part", [P, T])

                def tiles(m):
                    return KT if m % 2 == 0 else units_k(m // 2 % U)

                def units_k(u):
                    return branches[units[u][1]][4]

                @block.sync
                def _(sp):
                    if early:
                        early(sp)
                    stream(sp, N, per, merge_source(branches), following)

                @block.gpsimd
                def _(pool):
                    with pool.Fori(0, N) as i:
                        for m in range(per):
                            rest_chunk(pool, m + 1, i, per, tiles(m + 1))

                @block.scalar
                def _(act):
                    with act.Fori(0, N) as i:
                        for u, (tile, b) in enumerate(units):
                            round_chunk(act, 2 * u + 1, i, per, tiles(2 * u + 1))
                            act.wait_ge(used.sem, after(used, 2 * u, i, per))
                            act.wait_ge(evicted2.sem, evicted2.at(u - 1, i, U))
                            col = branches[b][2]
                            bias = 0.0 if col is None else vec[:, bass.ds(merged_tile(i, col + tile), 1)]
                            act.activation(sig[:, u % 2], ps[2 * (u % 2)][:], ACT.Sigmoid, bias=bias).then_inc(evicted.sem, 1)
                            round_chunk(act, 2 * u + 2, i, per, tiles(2 * u + 2))

                @block.vector
                def _(dve):
                    with dve.Fori(0, N) as i:
                        dve_steps.open(i, U - 2 if not accumulate else U)
                        for u, (tile, b) in enumerate(units):
                            if beside:
                                beside(dve, i, u)
                            dve.wait_ge(evicted.sem, evicted.at(u + 1, i, U))
                            dve.wait_ge(used.sem, after(used, 2 * u + 1, i, per))
                            to = acc[:, bass.ds(merged_tile(i, tile), 1)].rearrange("p a t -> p (a t)")
                            if b == 0 and not accumulate:
                                dve.tensor_tensor(to, sig[:, u % 2], ps[2 * (u % 2) + 1][:], ALU.mult).then_inc(evicted2.sem, 1)
                            else:
                                dve_steps.wait(dve)
                                dve.tensor_tensor(part[:], sig[:, u % 2], ps[2 * (u % 2) + 1][:], ALU.mult)\
                                   .then_inc(evicted2.sem, 1)
                                dve.wait_ge(evicted2.sem, evicted2.at(u + 1, i, U))
                                dve_steps.done(dve.tensor_tensor(to, to, part[:], ALU.add))

                @block.tensor
                def _(pe):
                    with pe.Fori(0, N) as i:
                        for u, (tile, b) in enumerate(units):
                            split_ready(pe, 2 * u, i, per)
                            pe.wait_ge(evicted.sem, evicted.at(u - 1, i, U))
                            product(pe, 0, wide(ps[2 * (u % 2)])).then_inc(used.sem, 1)
                            split_ready(pe, 2 * u + 1, i, per)
                            pe.wait_ge(evicted2.sem, evicted2.at(u - 1, i, U))
                            product(pe, 1, halves(ps[2 * (u % 2) + 1], branches[b][5], branches[b][6]),
                                    branches[b][4]).then_inc(used.sem, 1)

            dve_steps.close(N)
            for s in (evicted, evicted2):
                s.passed(U * N)
            chunk_passed(per * N)

        def conv_source(i, m):
            return chunk_of(w_in, (A_X, A_C, A_B, A_Z)[m] + i * P)

        def convolution(y_hi_t, y_lo_t, following):
            N = WB // P
            b_in = COL["b_in"]
            with ExitStack() as sc, nc.Block() as block:
                ax = sb(sc, "ax", [P, T])
                u = sb(sc, "u", [P, T + 2])
                z = sb(sc, "z", [P, T])
                y = sb(sc, "y", [P, T])

                @block.sync
                def _(sp):
                    stream(sp, N, 4, conv_source, following)

                @block.gpsimd
                def _(pool):
                    pool.memset(u[:], 0.0).then_inc(aux.sem, 1)
                    with pool.Fori(0, N) as i:
                        for m in range(4):
                            rest_chunk(pool, m + 1, i, 4)
                        pool.wait_ge(y_hi.sem, y_hi.at(1, i, 1))
                        pool.tensor_tensor(y_lo_t[:, bass.ds(i, 1)], y[:].rearrange("p (a t) -> p a t", a=1),
                                           y_hi_t[:, bass.ds(i, 1)].bitcast(F32), ALU.subtract).then_inc(y_ready.sem, 1)

                @block.scalar
                def _(act):
                    with act.Fori(0, N) as i:
                        round_chunk(act, 1, i, 4)
                        act.wait_ge(used.sem, after(used, 0, i, 4))
                        act.wait_ge(evicted2.sem, evicted2.at(0, i, 2))
                        act.activation(ax[:], ps[0][:], ACT.Identity, bias=vec[:, bass.ds(i + (b_in + A_X // P), 1)])\
                           .then_inc(evicted.sem, 1)
                        round_chunk(act, 2, i, 4)
                        round_chunk(act, 3, i, 4)
                        round_chunk(act, 4, i, 4)
                        act.wait_ge(used.sem, after(used, 3, i, 4))
                        act.wait_ge(h_ready.sem, h_ready.at(0, i, 1))
                        act.activation(z[:], ps[3][:], ACT.Silu, bias=vec[:, bass.ds(i + (b_in + A_Z // P), 1)])\
                           .then_inc(evicted.sem, 1)
                        act.wait_ge(h_ready.sem, h_ready.at(1, i, 1))
                        act.activation(y_hi_t[:, bass.ds(i, 1)], y[:].rearrange("p (a t) -> p a t", a=1), ACT.Copy)\
                           .then_inc(y_hi.sem, 1)

                @block.vector
                def _(dve):
                    dve.wait_ge(aux.sem, aux.at(1))
                    with dve.Fori(0, N) as i:
                        dve_steps.open(i, 4)
                        dve.wait_ge(evicted.sem, evicted.at(1, i, 2))
                        dve.wait_ge(used.sem, after(used, 1, i, 4))
                        dve.scalar_tensor_tensor(out=u[:, 1:T + 1], in0=ps[1][:], scalar=vec[:, bass.ds(i + (b_in + A_C // P), 1)],
                                                 in1=ax[:], op0=ALU.add, op1=ALU.mult).then_inc(evicted2.sem, 1)
                        dve.wait_ge(evicted2.sem, evicted2.at(1, i, 2))
                        dve.wait_ge(y_ready.sem, y_ready.at(0, i, 1))
                        dve_steps.done(dve.tensor_scalar(y[:], u[:, 0:T], vec[:, bass.ds(i + COL["w_conv"], 1)],
                                                         vec[:, bass.ds(i + COL["b_conv"], 1)], ALU.mult, ALU.add))
                        for tap in (1, 2):
                            dve_steps.wait(dve)
                            dve_steps.done(dve.scalar_tensor_tensor(
                                out=y[:], in0=u[:, tap:tap + T], scalar=vec[:, bass.ds(i + (COL["w_conv"] + 4 * tap), 1)],
                                in1=y[:], op0=ALU.mult, op1=ALU.add))
                        dve_steps.wait(dve)
                        dve.wait_ge(used.sem, after(used, 2, i, 4))
                        dve_steps.done(dve.scalar_tensor_tensor(
                            out=y[:], in0=ps[2][:], scalar=vec[:, bass.ds(i + (b_in + A_B // P), 1)], in1=y[:],
                            op0=ALU.add, op1=ALU.mult))
                        dve_steps.wait(dve)
                        dve.wait_ge(evicted.sem, evicted.at(2, i, 2))
                        dve.tensor_tensor(y[:], y[:], z[:], ALU.mult).then_inc(h_ready.sem, 1)
                        dve.wait_ge(h_ready.sem, h_ready.at(1, i, 1))
                        carry_wait(0).then_inc(evicted2.sem, 1)

                @block.tensor
                def _(pe):
                    with pe.Fori(0, N) as i:
                        for m in range(4):
                            split_ready(pe, m, i, 4)
                            if m == 0:
                                pe.wait_ge(evicted.sem, evicted.at(0, i, 2))
                            else:
                                pe.wait_ge(h_ready.sem, h_ready.at(0, i, 1))
                            product(pe, m % 2, wide(ps[m])).then_inc(used.sem, 1)

            dve_steps.close(N)
            for s, n in ((aux, 1), (evicted, 2 * N), (evicted2, 2 * N), (h_ready, N), (y_hi, N), (y_ready, N)):
                s.passed(n)
            chunk_passed(4 * N)

        def fourier_source(i, m):
            return chunk_of(w_in, (F_U, F_Z)[m] + i * P)

        def fourier(y_hi_t, y_lo_t, following):
            N = WB // P
            HT = HALF // P
            b_in = COL["b_in"]
            with ExitStack() as sc, nc.Block() as block:
                cos_t = sb(sc, "cos_t", [P, HT, HALF + 1])
                sin_t = sb(sc, "sin_t", [P, HT, HALF + 1])
                alt = sb(sc, "alt", [1, HALF + 1])
                chan = sb(sc, "chan", [P, 2, P])
                f = sb(sc, "f", [P, T])
                y = f
                even = sb(sc, "even", [P, HALF])
                odd = sb(sc, "odd", [P, HALF])
                parts = sb(sc, "parts", [P, 2 * HT, P])
                mid = sb(sc, "mid", [1, P])
                zc = sb(sc, "zc", [P, HALF + 1])
                zs = sb(sc, "zs", [P, HALF])
                big_a = sb(sc, "big_a", [P, HALF + 1])
                z = sb(sc, "z", [P, T])

                @block.sync
                def _(sp):
                    sp.dma_start(cos_t[:], a["k_cos"].rearrange("(t p) k -> p t k", p=P)).then_inc(side_loaded.sem, 16)
                    sp.dma_start(sin_t[:], a["k_sin"].rearrange("(t p) k -> p t k", p=P)).then_inc(side_loaded.sem, 16)
                    sp.dma_start(alt[:], a["k_alt"]).then_inc(side_loaded.sem, 16)
                    sp.dma_start(chan[:], a["k_chan"]).then_inc(side_loaded.sem, 16)
                    stream(sp, N, 2, fourier_source, following)

                @block.gpsimd
                def _(pool):
                    pool.memset(odd[:], 0.0).then_inc(aux.sem, 1)
                    with pool.Fori(0, N) as i:
                        for m in range(2):
                            rest_chunk(pool, m + 1, i, 2)
                        pool.wait_ge(y_hi.sem, y_hi.at(1, i, 1))
                        pool.tensor_tensor(y_lo_t[:, bass.ds(i, 1)], y[:].rearrange("p (a t) -> p a t", a=1),
                                           y_hi_t[:, bass.ds(i, 1)].bitcast(F32), ALU.subtract).then_inc(y_ready.sem, 1)

                @block.scalar
                def _(act):
                    with act.Fori(0, N) as i:
                        round_chunk(act, 1, i, 2)
                        act.wait_ge(used.sem, after(used, 0, i, 2))
                        act.wait_ge(y_ready.sem, y_ready.at(0, i, 1))
                        act.activation(f[:], ps[0][:], ACT.Identity, bias=vec[:, bass.ds(i + (b_in + F_U // P), 1)])\
                           .then_inc(evicted.sem, 1)
                        round_chunk(act, 2, i, 2)
                        act.wait_ge(transposed.sem, transposed.at(1, i, 1))
                        act.activation(parts[:], ps[2][:].rearrange("p (t c) -> p t c", c=P), ACT.Copy).then_inc(tr_evicted.sem, 1)
                        act.wait_ge(scores.sem, scores.at(1, i, 2))
                        act.activation(zc[:, 0:HALF], ps[2][:, 0:HALF], ACT.Copy)
                        act.activation(zc[:, HALF:HALF + 1], ps[3][:, HALF:HALF + 1], ACT.Copy).then_inc(exped.sem, 1)
                        act.wait_ge(scores.sem, scores.at(2, i, 2))
                        act.wait_ge(h_ready.sem, h_ready.at(0, i, 1))
                        act.activation(big_a[:, 0:HALF], ps[2][:, 0:HALF], ACT.Copy)
                        act.activation(big_a[:, HALF:HALF + 1], ps[3][:, HALF:HALF + 1], ACT.Copy).then_inc(exped.sem, 1)
                        act.wait_ge(used.sem, after(used, 1, i, 2))
                        act.activation(z[:], ps[1][:], ACT.Silu, bias=vec[:, bass.ds(i + (b_in + F_Z // P), 1)])\
                           .then_inc(evicted2.sem, 1)
                        act.wait_ge(h_ready.sem, h_ready.at(1, i, 1))
                        act.activation(y_hi_t[:, bass.ds(i, 1)], y[:].rearrange("p (a t) -> p a t", a=1), ACT.Copy)\
                           .then_inc(y_hi.sem, 1)

                @block.vector
                def _(dve):
                    dve.wait_ge(aux.sem, aux.at(1))
                    with dve.Fori(0, N) as i:
                        dve_steps.open(i, 3)
                        dve.wait_ge(evicted.sem, evicted.at(1, i, 1))
                        mirror = f[:, T - 1:HALF:-1]
                        dve.tensor_tensor(even[:, 1:HALF], f[:, 1:HALF], mirror, ALU.add)
                        dve.tensor_tensor(odd[:, 1:HALF], f[:, 1:HALF], mirror, ALU.subtract)
                        dve.tensor_copy(even[:, 0:1], f[:, 0:1]).then_inc(aux2.sem, 1)
                        dve.wait_ge(transposed.sem, transposed.at(1, i, 1))
                        dve.tensor_copy(mid[:], ps[3][0:1, 0:P]).then_inc(aux3.sem, 1)
                        dve.wait_ge(scores.sem, scores.at(1, i, 2))
                        dve.tensor_copy(zs[:], ps[2][:, HALF:2 * HALF]).then_inc(biased.sem, 1)
                        dve.wait_ge(exped.sem, exped.at(2, i, 2))
                        back = y[:, T - 1:HALF:-1]
                        dve.tensor_tensor(y[:, 0:HALF], big_a[:, 0:HALF], ps[2][:, HALF:2 * HALF], ALU.subtract)
                        dve_steps.done(dve.tensor_tensor(back, big_a[:, 1:HALF], ps[2][:, HALF + 1:2 * HALF], ALU.add))
                        dve_steps.done(dve.tensor_copy(y[:, HALF:HALF + 1], big_a[:, HALF:HALF + 1]))
                        dve_steps.wait(dve)
                        dve.wait_ge(evicted2.sem, evicted2.at(1, i, 1))
                        dve.tensor_tensor(y[:], y[:], z[:], ALU.mult).then_inc(h_ready.sem, 1)
                        dve.wait_ge(h_ready.sem, h_ready.at(1, i, 1))
                        dve_steps.done(carry_wait(0))

                @block.tensor
                def _(pe):
                    pe.wait_ge(side_loaded.sem, side_loaded.at(4))
                    with pe.Fori(0, N) as i:
                        split_ready(pe, 0, i, 2)
                        pe.wait_ge(evicted.sem, evicted.at(0, i, 1))
                        product(pe, 0, wide(ps[0])).then_inc(used.sem, 1)
                        split_ready(pe, 1, i, 2)
                        pe.wait_ge(evicted2.sem, evicted2.at(0, i, 1))
                        product(pe, 1, wide(ps[1])).then_inc(used.sem, 1)
                        pe.wait_ge(aux2.sem, aux2.at(1, i, 1))
                        pe.wait_ge(h_ready.sem, h_ready.at(0, i, 1))
                        for n, src in enumerate((even, odd)):
                            for t in range(HT):
                                pe.transpose(ps[2][:, (n * HT + t) * P:(n * HT + t + 1) * P], src[:, t * P:t * P + P], ident[:])
                        pe.transpose(ps[3][0:1, 0:P], f[:, HALF:HALF + 1], ident[:]).then_inc(transposed.sem, 1)
                        pe.wait_ge(tr_evicted.sem, tr_evicted.at(1, i, 1))
                        pe.wait_ge(aux3.sem, aux3.at(1, i, 1))
                        for dst, c0, c1 in ((ps[2][:, 0:HALF], 0, HALF), (ps[3][:, HALF:HALF + 1], HALF, HALF + 1)):
                            for t in range(HT):
                                pe.matmul(dst, parts[:, t], cos_t[:, t, c0:c1], start=(t == 0), stop=False)
                            pe.matmul(dst, mid[:], alt[:, c0:c1], start=False, stop=True)
                        for t in range(HT):
                            last = pe.matmul(ps[2][:, HALF:2 * HALF], parts[:, HT + t], sin_t[:, t, 0:HALF],
                                             start=(t == 0), stop=(t == HT - 1))
                        last.then_inc(scores.sem, 1)
                        pe.wait_ge(exped.sem, exped.at(1, i, 2))
                        pe.wait_ge(biased.sem, biased.at(1, i, 1))
                        pe.matmul(ps[2][:, 0:HALF], chan[:, 0], zc[:, 0:HALF], start=True, stop=True)
                        pe.matmul(ps[3][:, HALF:HALF + 1], chan[:, 0], zc[:, HALF:HALF + 1], start=True, stop=True)
                        pe.matmul(ps[2][:, HALF:2 * HALF], chan[:, 1], zs[:], start=True, stop=True).then_inc(scores.sem, 1)

            dve_steps.close(N)
            side_loaded.passed(4)
            for s, n in ((aux, 1), (aux2, N), (aux3, N), (evicted, N), (evicted2, N), (transposed, N), (tr_evicted, N),
                         (scores, 2 * N), (exped, 2 * N), (biased, N), (h_ready, N), (y_hi, N), (y_ready, N)):
                s.passed(n)
            chunk_passed(2 * N)

        def project_source(w):
            return lambda i, m: chunk_of(w, m * P)

        def project(w, acc, res, first, gains, following, kept=None):
            with ExitStack() as sc, nc.Block() as block:
                xs = sb(sc, "xs", [P, 2, T])
                sq = sb(sc, "sq", [P, 2, T])
                ssq = sb(sc, "ssq", [P, T])
                inv = sb(sc, "inv", [P, T])

                @block.sync
                def _(sp):
                    stream(sp, 1, KT, project_source(w), following)
                    if kept is not None:
                        for m in range(KT):
                            sp.wait_ge(y_ready.sem, y_ready.at(m + 1))
                            sp.dma_start(kept[:, m], res[:, m]).then_inc(stored.sem, 16)
                        sp.wait_ge(stored.sem, stored.at(KT))

                @block.gpsimd
                def _(pool):
                    for m in range(KT):
                        rest_chunk(pool, m + 1, 0, KT)

                @block.scalar
                def _(act):
                    for k in range(KT):
                        act.activation(h_hi[:, k], acc[:, k], ACT.Copy).then_inc(hi_ready.sem, 1)
                        if k == 0:
                            round_chunk(act, 1, 0, KT)
                    def square(m):
                        act.wait_ge(evicted.sem, evicted.at(m + 1))
                        act.wait_ge(sum_ready.sem, sum_ready.at(m - 1))
                        act.activation(sq[:, m % 2], acc[:, m], ACT.Square).then_inc(sq_ready.sem, 1)

                    for m in range(KT):
                        if first:
                            act.wait_ge(transposed.sem, transposed.at(m + 1))
                            act.wait_ge(evicted.sem, evicted.at(m - 1))
                            act.activation(xs[:, m % 2], ps[2 + m % 2][:], ACT.Copy).then_inc(tr_evicted.sem, 1)
                        if m >= 1:
                            round_chunk(act, m + 1, 0, KT)
                            square(m - 1)
                    square(KT - 1)
                    act.wait_ge(stat_ready.sem, stat_ready.at(1))
                    act.activation(inv[:], inv[:], ACT.Sqrt).then_inc(norm_ready.sem, 1)
                    for m in range(KT):
                        act.wait_ge(y_ready.sem, y_ready.at(m + 1))
                        act.wait_ge(scores.sem, scores.at(1 + m - 1))
                        act.activation(sq[:, m % 2], res[:, m], ACT.Square).then_inc(sq_ready.sem, 1)
                    act.wait_ge(stat_ready.sem, stat_ready.at(2))
                    act.activation(inv[:], inv[:], ACT.Sqrt).then_inc(norm_ready.sem, 1)
                    for m in range(KT):
                        act.wait_ge(h_ready.sem, h_ready.at(m + 1))
                        act.activation(h_hi[:, m], xs[:, m % 2], ACT.Copy).then_inc(hi_ready.sem, 1)

                @block.vector
                def _(dve):
                    for k in range(KT):
                        dve.wait_ge(hi_ready.sem, hi_ready.at(k + 1))
                        dve.tensor_tensor(h_lo[:, k], acc[:, k], h_hi[:, k].bitcast(F32), ALU.subtract).then_inc(lo_ready.sem, 1)

                    def add_square(m):
                        dve.wait_ge(sq_ready.sem, sq_ready.at(m + 1))
                        if m == 0:
                            dve.tensor_copy(ssq[:], sq[:, 0]).then_inc(sum_ready.sem, 1)
                        else:
                            dve.wait_ge(sum_ready.sem, sum_ready.at(m))
                            dve.tensor_tensor(ssq[:], ssq[:], sq[:, m % 2], ALU.add).then_inc(sum_ready.sem, 1)

                    for m in range(KT):
                        dve.wait_ge(used.sem, after(used, m, 0, KT))
                        if first:
                            dve.wait_ge(tr_evicted.sem, tr_evicted.at(m + 1))
                            dve.scalar_tensor_tensor(out=acc[:, m], in0=ps[m % 2][:], scalar=gate_t[:, m:m + 1],
                                                     in1=xs[:, m % 2], op0=ALU.mult, op1=ALU.add).then_inc(evicted.sem, 1)
                        else:
                            dve.tensor_copy(acc[:, m], ps[m % 2][:]).then_inc(evicted.sem, 1)
                        if m >= 1:
                            add_square(m - 1)
                    add_square(KT - 1)

                    def inverse_rms(n, bank):
                        dve.wait_ge(scores.sem, scores.at((1, 1 + KT)[n]))
                        dve.tensor_scalar(inv[:], bank[:], 1.0 / D, EPS, ALU.mult, ALU.add).then_inc(stat_ready.sem, 1)
                        dve.wait_ge(norm_ready.sem, norm_ready.at(n + 1))
                        dve_steps.done(dve.reciprocal(inv[:], inv[:]))
                        dve_steps.wait(dve)

                    inverse_rms(0, ps[2])
                    if not first:
                        dve.wait_ge(x_loaded.sem, x_loaded.at(1))
                    for m in range(KT):
                        if first:
                            dve.scalar_tensor_tensor(out=res[:, m], in0=acc[:, m], scalar=column(gains[0], m), in1=inv[:],
                                                     op0=ALU.mult, op1=ALU.mult).then_inc(y_ready.sem, 1)
                        else:
                            dve_steps.done(dve.scalar_tensor_tensor(
                                out=acc[:, m], in0=acc[:, m], scalar=column(gains[0], m), in1=inv[:],
                                op0=ALU.mult, op1=ALU.mult))
                            dve_steps.wait(dve)
                            dve.tensor_tensor(res[:, m], res[:, m], acc[:, m], ALU.add).then_inc(y_ready.sem, 1)
                    inverse_rms(1, ps[3])
                    def subtract(m):
                        dve.wait_ge(hi_ready.sem, hi_ready.at(KT + m + 1))
                        dve.tensor_tensor(h_lo[:, m], xs[:, m % 2], h_hi[:, m].bitcast(F32), ALU.subtract).then_inc(lo_ready.sem, 1)

                    for m in range(KT):
                        if m >= 2:
                            dve.wait_ge(lo_ready.sem, lo_ready.at(KT + m - 1))
                        dve.scalar_tensor_tensor(out=xs[:, m % 2], in0=res[:, m], scalar=column(gains[1], m), in1=inv[:],
                                                 op0=ALU.mult, op1=ALU.mult).then_inc(h_ready.sem, 1)
                        if m >= 1:
                            subtract(m - 1)
                    subtract(KT - 1)

                @block.tensor
                def _(pe):
                    if first:
                        pe.wait_ge(x_loaded.sem, x_loaded.at(1))
                    for m in range(KT):
                        if first:
                            pe.wait_ge(tr_evicted.sem, tr_evicted.at(m - 1))
                            for t in range(TT):
                                last = pe.transpose(ps[2 + m % 2][:, t * P:t * P + P], res[:, t, m * P:m * P + P], ident[:])
                            last.then_inc(transposed.sem, 1)
                        split_ready(pe, m, 0, KT)
                        pe.wait_ge(evicted.sem, evicted.at(m - 1))
                        arrived = (lambda k: pe.wait_ge(lo_ready.sem, lo_ready.at(k + 1))) if m == 0 else None
                        product(pe, m % 2, wide(ps[m % 2]), KT, arrived).then_inc(used.sem, 1)
                    pe.wait_ge(sum_ready.sem, sum_ready.at(KT))
                    if first:
                        pe.wait_ge(tr_evicted.sem, tr_evicted.at(KT))
                    for c in (0, HALF):
                        last = pe.matmul(ps[2][:, c:c + HALF], ones[:], ssq[:, c:c + HALF], start=True, stop=True)
                    last.then_inc(scores.sem, 1)
                    for m in range(KT):
                        pe.wait_ge(sq_ready.sem, sq_ready.at(KT + m + 1))
                        for c in (0, HALF):
                            last = pe.matmul(ps[3][:, c:c + HALF], ones[:], sq[:, m % 2, c:c + HALF],
                                             start=(m == 0), stop=(m == KT - 1))
                        last.then_inc(scores.sem, 1)

            dve_steps.close()
            x_loaded.passed(1)
            if first:
                transposed.passed(KT)
                tr_evicted.passed(KT)
            if kept is not None:
                stored.passed(KT)
            for s, n in ((hi_ready, 2 * KT), (lo_ready, 2 * KT), (evicted, KT), (sq_ready, 2 * KT), (sum_ready, KT),
                         (stat_ready, 2), (norm_ready, 2), (y_ready, KT), (scores, 1 + KT), (h_ready, KT)):
                s.passed(n)
            chunk_passed(KT)

        def hgrn_source(i, m):
            head = (m % 4) // 2
            return (chunk_of(w_in2, (H_Q, H_F)[m % 2] + i * 2 * P + head * P) if m < 4
                    else chunk_of(w_in2, (H_I, H_G)[m - 4] + i * P))

        def hgrn(y_hi_t, y_lo_t, following):
            N, NC, LEVELS = 2, T // CHUNK, 8
            SMALL = 2.0 ** -60
            with ExitStack() as sc, nc.Block() as block:
                masks = sb(sc, "masks", [P, LEVELS, CHUNK])
                blocks = sb(sc, "blocks", [P, P])
                reset = sb(sc, "reset", [P, T])
                q = sb(sc, "q", [P, T])
                k = sb(sc, "k", [P, T])
                f = sb(sc, "f", [P, T])
                tiny = sb(sc, "tiny", [P, T])
                b = sb(sc, "b", [P, T])
                e = sb(sc, "e", [P, 2, T])
                qe = sb(sc, "qe", [P, 2, T])
                ke = sb(sc, "ke", [P, 2, T])
                att = sb(sc, "att", [P, 2, NC, CHUNK])
                qx = sb(sc, "qx", [P, 2, T])
                kd = sb(sc, "kd", [P, 2, T])
                e_last = sb(sc, "e_last", [P, 2, NC])
                kd_tok = sb(sc, "kd_tok", [P, NC, P])
                v_t = sb(sc, "v_t", [P, T])
                v_tok = sb(sc, "v_tok", [P, NC, P])
                state = sb(sc, "state", [P, 2, NC, 64])
                g_silu = sb(sc, "g_silu", [P, T])
                o_t = sb(sc, "o_t", [P, T])

                def chunked(x):
                    return x.rearrange("p (c t) -> p c t", t=CHUNK)

                @block.sync
                def _(sp):
                    sp.dma_start(masks[:], a["k_levels"]).then_inc(side_loaded.sem, 16)
                    sp.dma_start(blocks[:], a["k_blocks"]).then_inc(side_loaded.sem, 16)
                    stream(sp, N, 6, hgrn_source, following)

                @block.gpsimd
                def _(pool):
                    pool.memset(reset[:], 1.0).then_inc(aux.sem, 1)
                    pool.wait_ge(aux.sem, aux.at(1))
                    pool.memset(chunked(reset[:])[:, :, 0:1], 0.0).then_inc(aux.sem, 1)
                    with pool.Fori(0, N) as i:
                        rest_chunk(pool, 1, i, 6)
                        rest_chunk(pool, 2, i, 6)
                        for h in range(2):
                            pool.wait_ge(exped.sem, exped.at(9 * h + 2, i, 18))
                            pool.tensor_tensor(kd[:, h], k[:], e[:, 1], ALU.mult).then_inc(aux3.sem, 1)
                            for n in range(7):
                                pool.wait_ge(exped.sem, exped.at(9 * h + 3 + n, i, 18))
                                pool.wait_ge(scores.sem, scores.at(8 * h + n, i, 16))
                                pool.tensor_tensor(ke[:, n % 2], k[:], e[:, n % 2], ALU.mult).then_inc(y_ready.sem, 1)
                                if n in (2, 5):
                                    rest_chunk(pool, 3 + 2 * h + (n == 5), i, 6)
                        pool.wait_ge(y_hi.sem, y_hi.at(1, i, 1))
                        pool.tensor_tensor(y_lo_t[:, bass.ds(i, 1)], o_t[:].rearrange("p (a t) -> p a t", a=1),
                                           y_hi_t[:, bass.ds(i, 1)].bitcast(F32), ALU.subtract).then_inc(lo_ready.sem, 1)

                @block.scalar
                def _(act):
                    with act.Fori(0, N) as i:
                        for h in range(2):
                            if h == 0:
                                round_chunk(act, 1, i, 6)
                            act.wait_ge(used.sem, after(used, 2 * h, i, 6))
                            act.wait_ge(scores.sem, scores.at(8 * h, i, 16))
                            act.wait_ge(aux3.sem, aux3.at(h, i, 2))
                            act.wait_ge(evicted2.sem, evicted2.at(8 * h, i, 16))
                            act.activation(q[:], ps[0][:], ACT.Silu).then_inc(evicted.sem, 1)
                            if h == 0:
                                round_chunk(act, 2, i, 6)
                            act.wait_ge(used.sem, after(used, 2 * h + 1, i, 6))
                            act.wait_ge(lo_ready.sem, lo_ready.at(0, i, 1))
                            act.activation(k[:], ps[1][:], ACT.Sigmoid, scale=-1.0)
                            act.activation(f[:], ps[1][:], ACT.Sigmoid).then_inc(evicted.sem, 1)
                            act.wait_ge(h_ready.sem, h_ready.at(2 * h + 1, i, 4))
                            act.activation(f[:], f[:], ACT.Ln)
                            act.activation(tiny[:], tiny[:], ACT.Ln, scale=1.0 / SMALL).then_inc(mod_ready.sem, 1)
                            act.wait_ge(h_ready.sem, h_ready.at(2 * h + 2, i, 4))
                            act.activation(e[:, 0], b[:], ACT.Exp).then_inc(exped.sem, 1)
                            act.activation(e_last[:, h], chunked(b[:])[:, :, CHUNK - 1], ACT.Exp)
                            act.wait_ge(biased.sem, biased.at(8 * h + 1, i, 16))
                            act.activation(e[:, 1], e[:, 1], ACT.Exp).then_inc(exped.sem, 1)
                            for n in range(7):
                                act.wait_ge(biased.sem, biased.at(8 * h + 2 + n, i, 16))
                                act_steps.open(i, 14)
                                act_steps.k = 7 * h + n
                                act_steps.done(act.activation(e[:, n % 2], e[:, n % 2], ACT.Abs))
                                act_steps.wait(act)
                                act.activation(e[:, n % 2], e[:, n % 2], ACT.Exp, scale=-1.0).then_inc(exped.sem, 1)
                                if n in (2, 5):
                                    round_chunk(act, 3 + 2 * h + (n == 5), i, 6)
                        act.wait_ge(used.sem, after(used, 4, i, 6))
                        act.activation(v_t[:], ps[0][:], ACT.Copy).then_inc(evicted.sem, 1)
                        act.wait_ge(transposed.sem, transposed.at(1, i, 3))
                        act.activation(v_tok[:], chunked(ps[0][:]), ACT.Copy).then_inc(tr_evicted.sem, 1)
                        act.wait_ge(used.sem, after(used, 5, i, 6))
                        act.activation(g_silu[:], ps[1][:], ACT.Silu).then_inc(evicted.sem, 1)
                        for h in range(2):
                            act.wait_ge(transposed.sem, transposed.at(2 + h, i, 3))
                            if h == 1:
                                act.wait_ge(pt_ready.sem, pt_ready.at(1, i, 2))
                            act.activation(kd_tok[:], chunked(ps[2][:]), ACT.Copy).then_inc(tr_evicted.sem, 1)
                        act.wait_ge(o_ready.sem, o_ready.at(1, i, 1))
                        act.activation(o_t[:], ps[3][:], ACT.Copy)
                        act.activation(e[:, 0], ps[3][:], ACT.Square).then_inc(sq_ready.sem, 1)
                        act.wait_ge(stat_ready.sem, stat_ready.at(1, i, 2))
                        act.activation(e[:, 1], e[:, 1], ACT.Sqrt).then_inc(norm_ready.sem, 1)
                        act.wait_ge(stat_ready.sem, stat_ready.at(2, i, 2))
                        act.activation(y_hi_t[:, bass.ds(i, 1)], o_t[:].rearrange("p (a t) -> p a t", a=1), ACT.Copy)\
                           .then_inc(y_hi.sem, 1)

                @block.vector
                def _(dve):
                    dve.wait_ge(aux.sem, aux.at(2))
                    dve.wait_ge(side_loaded.sem, side_loaded.at(2))
                    with dve.Fori(0, N) as i:
                        dve_steps.open(i, 2 * (2 + 3) + 14 + 3)
                        for h in range(2):
                            one_minus, low = lb[:, bass.ds(i * 2 + (4 + h), 1)], lb[:, bass.ds(i * 2 + h, 1)]
                            dve.wait_ge(evicted.sem, evicted.at(2 * h + 2, i, 6))
                            dve_steps.done(dve.tensor_scalar(k[:], k[:], one_minus, None, ALU.mult))
                            dve_steps.done(dve.tensor_scalar(f[:], f[:], one_minus, low, ALU.mult, ALU.add))
                            dve_steps.wait(dve)
                            dve_steps.done(dve.tensor_scalar(tiny[:], f[:], 1e-30, SMALL, ALU.max, ALU.min))
                            dve_steps.wait(dve)
                            dve.tensor_scalar(f[:], f[:], SMALL, None, ALU.max).then_inc(h_ready.sem, 1)
                            dve.wait_ge(mod_ready.sem, mod_ready.at(h + 1, i, 2))
                            dve_steps.done(dve.tensor_tensor(f[:], f[:], tiny[:], ALU.add))
                            dve_steps.wait(dve)
                            dve.tensor_tensor_scan(b[:], reset[:], f[:], 0.0, ALU.mult, ALU.add).then_inc(h_ready.sem, 1)
                            dve.wait_ge(h_ready.sem, h_ready.at(2 * h + 2, i, 4))

                            def minus_reference(dst, size, at, flip):
                                x = b[:].rearrange("p (c t) -> p c t", t=size)
                                r = x[:, :, at:at + 1].broadcast_to([P, T // size, size])
                                y = dst.rearrange("p (c t) -> p c t", t=size)
                                return dve.tensor_tensor(y, r if flip else x, x if flip else r, ALU.subtract)

                            minus_reference(e[:, 1], CHUNK, CHUNK - 1, True).then_inc(biased.sem, 1)
                            dve.wait_ge(exped.sem, exped.at(9 * h + 1, i, 18))
                            dve_steps.done(dve.tensor_tensor(qx[:, h], q[:], e[:, 0], ALU.mult))
                            dve_steps.wait(dve)

                            def difference(n):
                                half = CHUNK >> (n + 1)
                                if n == 1:
                                    dve.wait_ge(aux3.sem, aux3.at(h + 1, i, 2))
                                if n >= 2:
                                    dve_steps.wait(dve)
                                    dve.wait_ge(y_ready.sem, y_ready.at(7 * h + n - 1, i, 14))
                                minus_reference(e[:, n % 2], 2 * half, half - 1, False).then_inc(biased.sem, 1)

                            def take(n):
                                mask = masks[:, (n - 1) % LEVELS:(n - 1) % LEVELS + 1].broadcast_to([P, NC, CHUNK])
                                if n == 0:
                                    dve.wait_ge(o_ready.sem, o_ready.at(0, i, 1))
                                    dve.tensor_tensor(att[:, h], mask, chunked(ps[2][:]), ALU.mult).then_inc(evicted2.sem, 1)
                                else:
                                    dve.copy_predicated(att[:, h], mask.bitcast(U32), chunked(ps[2][:])).then_inc(evicted2.sem, 1)

                            difference(0)
                            for n in range(7):
                                if n < 6:
                                    difference(n + 1)
                                dve.wait_ge(exped.sem, exped.at(9 * h + 3 + n, i, 18))
                                dve.wait_ge(evicted2.sem, evicted2.at(8 * h + n, i, 16))
                                dve.wait_ge(scores.sem, scores.at(8 * h + n + 1, i, 16))
                                dve_steps.done(dve.tensor_tensor(qe[:, n % 2], q[:], e[:, n % 2], ALU.mult))
                                take(n)
                            dve.wait_ge(evicted2.sem, evicted2.at(8 * h + 7, i, 16))
                            dve.wait_ge(scores.sem, scores.at(8 * h + 8, i, 16))
                            carry_wait(h)
                            take(7)
                        for h in range(2):
                            dve.wait_ge(pt_ready.sem, pt_ready.at(h + 1, i, 2))
                            for c in range(NC - 1):
                                add = ps[1][:, h * HALF + c * 64:h * HALF + c * 64 + 64]
                                if c == 0:
                                    dve.tensor_copy(state[:, h, 1], add).then_inc(pt_evicted.sem, 1)
                                else:
                                    dve.wait_ge(pt_evicted.sem, pt_evicted.at(7 * h + c, i, 14))
                                    dve.scalar_tensor_tensor(out=state[:, h, c + 1], in0=state[:, h, c],
                                                             scalar=e_last[:, h, c:c + 1], in1=add, op0=ALU.mult,
                                                             op1=ALU.add).then_inc(pt_evicted.sem, 1)
                        dve.wait_ge(sum_ready.sem, sum_ready.at(1, i, 1))
                        dve.tensor_scalar(e[:, 1], ps[2][:], 1.0 / 64, EPS, ALU.mult, ALU.add).then_inc(stat_ready.sem, 1)
                        dve.wait_ge(norm_ready.sem, norm_ready.at(1, i, 1))
                        dve_steps.done(dve.reciprocal(e[:, 1], e[:, 1]))
                        dve_steps.wait(dve)
                        dve_steps.done(dve.scalar_tensor_tensor(
                            out=o_t[:], in0=o_t[:], scalar=vec[:, bass.ds(i + COL["hgrn_norm_2"], 1)], in1=e[:, 1],
                            op0=ALU.mult, op1=ALU.mult))
                        dve_steps.wait(dve)
                        dve.tensor_tensor(o_t[:], o_t[:], g_silu[:], ALU.mult).then_inc(stat_ready.sem, 1)
                        dve.wait_ge(stat_ready.sem, stat_ready.at(2, i, 2))
                        dve_steps.done(carry_wait(2))

                @block.tensor
                def _(pe):
                    pe.wait_ge(side_loaded.sem, side_loaded.at(2))
                    with pe.Fori(0, N) as i:
                        split_ready(pe, 0, i, 6)
                        product(pe, 0, wide(ps[0])).then_inc(used.sem, 1)
                        split_ready(pe, 1, i, 6)
                        product(pe, 1, wide(ps[1])).then_inc(used.sem, 1)
                        for h in range(2):
                            pe.wait_ge(h_ready.sem, h_ready.at(2 * h + 1, i, 4))
                            for n in range(8):
                                if n >= 1:
                                    pe.wait_ge(y_ready.sem, y_ready.at(7 * h + n, i, 14))
                                    pe.wait_ge(dve_steps.counted.sem, dve_steps.counted.at(12 * h + 5 + n, i, 27))
                                    pe.wait_ge(evicted2.sem, evicted2.at(8 * h + n, i, 16))
                                for c in range(NC):
                                    cut = slice(c * CHUNK, c * CHUNK + CHUNK)
                                    ks, qs = (k[:, cut], q[:, cut]) if n == 0 else (ke[:, (n - 1) % 2, cut], qe[:, (n - 1) % 2, cut])
                                    last = pe.matmul(ps[2][:, cut], ks, qs, start=True, stop=True)
                                last.then_inc(scores.sem, 1)
                                m = 2 + 2 * h + n // 4
                                if n % 4 == 0:
                                    split_ready(pe, m, i, 6)
                                    pe.wait_ge(evicted.sem, evicted.at(2 * h + 1 + n // 4, i, 6))
                                last = product(pe, m % 2, wide(ps[m % 2]), part=(n % 4, 4))
                                if n % 4 == 3:
                                    last.then_inc(used.sem, 1)
                        pe.wait_ge(evicted.sem, evicted.at(5, i, 6))
                        for c in range(NC):
                            last = pe.transpose(ps[0][:, c * P:c * P + P], v_t[:, c * P:c * P + P], ident[:])
                        last.then_inc(transposed.sem, 1)
                        pe.wait_ge(evicted.sem, evicted.at(6, i, 6))
                        pe.wait_ge(evicted2.sem, evicted2.at(16, i, 16))
                        for h in range(2):
                            if h == 1:
                                pe.wait_ge(tr_evicted.sem, tr_evicted.at(2, i, 3))
                            for c in range(NC):
                                last = pe.transpose(ps[2][:, c * P:c * P + P], kd[:, h, c * P:c * P + P], ident[:])
                            last.then_inc(transposed.sem, 1)
                            pe.wait_ge(tr_evicted.sem, tr_evicted.at(2 + h, i, 3))
                            for c in range(NC - 1):
                                last = pe.matmul(ps[1][:, h * HALF + c * 64:h * HALF + c * 64 + 64], kd_tok[:, c],
                                                 v_tok[:, c, h * 64:h * 64 + 64], start=True, stop=True)
                            last.then_inc(pt_ready.sem, 1)
                        for h in range(2):
                            rows = slice(h * 64, h * 64 + 64)
                            for c in range(NC):
                                cut = slice(c * CHUNK, c * CHUNK + CHUNK)
                                if c >= 1:
                                    pe.wait_ge(pt_evicted.sem, pt_evicted.at(7 * h + c, i, 14))
                                last = pe.matmul(ps[3][rows, cut], v_tok[:, c, rows], att[:, h, c], start=True, stop=(c == 0))
                                if c >= 1:
                                    last = pe.matmul(ps[3][rows, cut], state[:, h, c], qx[:, h, cut], start=False, stop=True)
                        last.then_inc(o_ready.sem, 1)
                        pe.wait_ge(sq_ready.sem, sq_ready.at(1, i, 1))
                        for c in (0, HALF):
                            last = pe.matmul(ps[2][:, c:c + HALF], blocks[:], e[:, 0, c:c + HALF], start=True, stop=True)
                        last.then_inc(sum_ready.sem, 1)

            act_steps.close(0)
            act_steps.counted.passed(14 * N)
            dve_steps.close(N)
            side_loaded.passed(2)
            for s, n in ((aux, 2), (aux3, 2 * N), (evicted, 6 * N), (evicted2, 16 * N), (h_ready, 4 * N),
                         (mod_ready, 2 * N), (exped, 18 * N), (biased, 16 * N), (scores, 16 * N), (y_ready, 14 * N),
                         (transposed, 3 * N), (tr_evicted, 3 * N), (pt_ready, 2 * N), (pt_evicted, 14 * N), (o_ready, N),
                         (sq_ready, N), (sum_ready, N), (stat_ready, 2 * N), (norm_ready, N), (y_hi, N), (lo_ready, N)):
                s.passed(n)
            chunk_passed(6 * N)

        def memory_source(i, m):
            return chunk_of(w_in2, m * P + M_Q) if m < 2 else chunk_of(a["w_mem_kv_2"][0], (m - 2) * P)

        def memory_attention(y_hi_t, y_lo_t, following):
            H = BW // DH
            with ExitStack() as sc, nc.Block() as block:
                mem_tok = sb(sc, "mem_tok", [P, 2, D])
                mem32 = sb(sc, "mem32", [P, KT, NMEM])
                mem_hi = sb(sc, "mem_hi", [P, KT, NMEM], F32R)
                mem_lo = sb(sc, "mem_lo", [P, KT, NMEM], F32R)
                power = sb(sc, "power", [P, 2])
                sums = sb(sc, "sums", [P, 2])
                rstd = sb(sc, "rstd", [P, 2])
                q_t = sb(sc, "q_t", [P, 2, T])
                k_t = sb(sc, "k_t", [P, 2, NMEM])
                v_t = sb(sc, "v_t", [P, 2, NMEM])
                v_tok = sb(sc, "v_tok", [P, 2, BW])
                prob = sb(sc, "prob", [P, 2, H, NMEM])
                prob_t = sb(sc, "prob_t", [P, 2, 2 * H, P])
                stat = sb(sc, "stat", [P, 2, 4, H])

                def place(h):
                    return h % 2 * 2 + h // 2

                @block.sync
                def _(sp):
                    sp.dma_start(mem_tok[:], a["mem_2"][0].rearrange("(t p) d -> p t d", p=P)).then_inc(side_loaded.sem, 16)
                    stream(sp, 1, 6, memory_source, following)

                @block.gpsimd
                def _(pool):
                    pool.memset(power[:], -0.5).then_inc(aux.sem, 1)
                    rest_chunk(pool, 1, 0, 6)
                    pool.wait_ge(aux.sem, aux.at(1))
                    pool.wait_ge(stat_ready.sem, stat_ready.at(1))
                    pool.tensor_tensor(rstd[:], sums[:], power[:], ALU.pow).then_inc(norm_ready.sem, 1)
                    for m in range(2, 7):
                        rest_chunk(pool, m, 0, 6)

                @block.scalar
                def _(act):
                    round_chunk(act, 1, 0, 6)
                    act.wait_ge(side_loaded.sem, side_loaded.at(1))
                    for t in range(2):
                        act.activation(prob[:, t].rearrange("p h k -> p (h k)"), mem_tok[:, t], ACT.Square,
                                       accum_out=sums[:, t:t + 1]).then_inc(sq_ready.sem, 1)
                    act.wait_ge(used.sem, after(used, 0, 0, 6))
                    act.activation(q_t[:, 0], ps[0][:], ACT.Copy).then_inc(evicted.sem, 1)
                    round_chunk(act, 2, 0, 6)
                    act.wait_ge(h_ready.sem, h_ready.at(KT))
                    act.activation(mem_hi[:], mem32[:], ACT.Copy).then_inc(hi_ready.sem, 1)
                    act.wait_ge(used.sem, after(used, 1, 0, 6))
                    act.activation(q_t[:, 1], ps[1][:], ACT.Copy).then_inc(evicted.sem, 1)
                    for m in range(3, 7):
                        round_chunk(act, m, 0, 6)
                    act.wait_ge(transposed.sem, transposed.at(3))
                    act.activation(v_tok[:], ps[2][:, 0:2 * BW].rearrange("p (t c) -> p t c", c=BW), ACT.Copy)\
                       .then_inc(tr_evicted.sem, 1)

                    def exps(b):
                        act.wait_ge(biased.sem, biased.at(b + 1))
                        act.wait_ge(pt_ready.sem, pt_ready.at(b - 1))
                        for h in range(H):
                            last = act.activation(prob[:, b % 2, h], ps[b % 2][:, h * NMEM:h * NMEM + NMEM], ACT.Exp,
                                                  bias=stat[:, b % 2, 1, h:h + 1], scale=DH ** -0.5,
                                                  accum_out=stat[:, b % 2, 2, h:h + 1])
                        last.then_inc(exped.sem, 1)

                    def evict_probs(b):
                        act.wait_ge(pt_ready.sem, pt_ready.at(b + 1))
                        act.wait_ge(o_ready.sem, o_ready.at(b - 1))
                        act.activation(prob_t[:, b % 2], ps[2][:].rearrange("p (j c) -> p j c", c=P), ACT.Copy)\
                           .then_inc(pt_evicted.sem, 1)

                    def evict_o(b):
                        act.wait_ge(o_ready.sem, o_ready.at(b + 1))
                        at = b % 2 * HALF
                        act.activation(y_hi_t[:, :, b * P:b * P + P], ps[3][:, at:at + 2 * P].rearrange("p (t c) -> p t c", c=P),
                                       ACT.Copy).then_inc(y_hi.sem, 1)

                    exps(0)
                    for b in range(TT):
                        if b + 1 < TT:
                            exps(b + 1)
                        evict_probs(b)
                        if b >= 1:
                            evict_o(b - 1)
                    evict_o(TT - 1)

                @block.vector
                def _(dve):
                    dve.wait_ge(sq_ready.sem, sq_ready.at(2))
                    dve.tensor_scalar(sums[:], sums[:], 1.0 / D, EPS, ALU.mult, ALU.add).then_inc(stat_ready.sem, 1)
                    dve.wait_ge(norm_ready.sem, norm_ready.at(1))
                    for t in range(2):
                        dve.tensor_scalar(mem_tok[:, t], mem_tok[:, t], rstd[:, t:t + 1], None, ALU.mult).then_inc(sum_ready.sem, 1)
                    for d in range(KT):
                        dve.wait_ge(transposed.sem, transposed.at(1 + d // 4))
                        dve.tensor_scalar(mem32[:, d], ps[2 + d // 4][:, d % 4 * NMEM:(d % 4 + 1) * NMEM],
                                          column("norm_mem_2", d), None, ALU.mult).then_inc(h_ready.sem, 1)
                    dve.wait_ge(hi_ready.sem, hi_ready.at(1))
                    dve.tensor_tensor(mem_lo[:], mem32[:], mem_hi[:].bitcast(F32), ALU.subtract).then_inc(lo_ready.sem, 1)
                    for m in range(4):
                        dve.wait_ge(used.sem, after(used, 2 + m, 0, 6))
                        dve.tensor_copy((k_t, v_t)[m // 2][:, m % 2], ps[2 + m // 2][:, m % 2 * HALF:m % 2 * HALF + NMEM])\
                           .then_inc(evicted2.sem, 1)

                    def maxima(b):
                        dve.wait_ge(scores.sem, scores.at(b + 1))
                        st = stat[:, b % 2]
                        dve_steps.done(dve.reduce_max(st[:, 0], ps[b % 2][:].rearrange("p (h k) -> p h k", k=NMEM), AX))
                        dve_steps.wait(dve)
                        dve.tensor_scalar(st[:, 1], st[:, 0], -DH ** -0.5, None, ALU.mult).then_inc(biased.sem, 1)

                    def normalise(b):
                        st = stat[:, b % 2]
                        dve.wait_ge(exped.sem, exped.at(b + 1))
                        dve_steps.done(dve.reciprocal(st[:, 3], st[:, 2]))
                        dve_steps.wait(dve)
                        dve.tensor_tensor(prob[:, b % 2], prob[:, b % 2],
                                          st[:, 3].rearrange("p (h k) -> p h k", k=1).broadcast_to([P, H, NMEM]),
                                          ALU.mult).then_inc(probs.sem, 1)

                    def rest_o(b):
                        dve.wait_ge(y_hi.sem, y_hi.at(b + 1))
                        at = b % 2 * HALF
                        cols = slice(b * P, b * P + P)
                        dve.tensor_tensor(y_lo_t[:, :, cols], ps[3][:, at:at + 2 * P].rearrange("p (t c) -> p t c", c=P),
                                          y_hi_t[:, :, cols].bitcast(F32), ALU.subtract).then_inc(o_evicted.sem, 1)

                    maxima(0)
                    for b in range(TT):
                        if b + 1 < TT:
                            maxima(b + 1)
                        normalise(b)
                        if b >= 2:
                            rest_o(b - 2)
                    rest_o(TT - 2)
                    rest_o(TT - 1)

                @block.tensor
                def _(pe):
                    split_ready(pe, 0, 0, 6)
                    product(pe, 0, wide(ps[0])).then_inc(used.sem, 1)
                    split_ready(pe, 1, 0, 6)
                    product(pe, 1, wide(ps[1])).then_inc(used.sem, 1)
                    pe.wait_ge(sum_ready.sem, sum_ready.at(2))
                    for d in range(KT):
                        for t in range(2):
                            c = d % 4 * NMEM + t * P
                            last = pe.transpose(ps[2 + d // 4][:, c:c + P], mem_tok[:, t, d * P:d * P + P], ident[:])
                        if d % 4 == 3:
                            last.then_inc(transposed.sem, 1)
                    pe.wait_ge(lo_ready.sem, lo_ready.at(1))
                    for m in range(2, 6):
                        split_ready(pe, m, 0, 6)
                        c = m % 2 * HALF
                        product(pe, m % 2, [(ps[1 + m // 2][:, c:c + NMEM], lambda k: mem_hi[:, k], lambda k: mem_lo[:, k])])\
                            .then_inc(used.sem, 1)
                    pe.wait_ge(evicted2.sem, evicted2.at(4))
                    for t in range(2):
                        for ft in range(2):
                            c = t * BW + ft * P
                            last = pe.transpose(ps[2][:, c:c + P], v_t[:, ft, t * P:t * P + P], ident[:])
                    last.then_inc(transposed.sem, 1)
                    pe.wait_ge(evicted.sem, evicted.at(2))

                    def score(b):
                        pe.wait_ge(exped.sem, exped.at(b - 1))
                        for h in range(H):
                            rows, c = slice(h % 2 * 64, h % 2 * 64 + 64), place(h) * NMEM
                            last = pe.matmul(ps[b % 2][:, c:c + NMEM], q_t[rows, h // 2, b * P:b * P + P],
                                             k_t[rows, h // 2], start=True, stop=True)
                        last.then_inc(scores.sem, 1)

                    def turn(b):
                        pe.wait_ge(probs.sem, probs.at(b + 1))
                        pe.wait_ge(pt_evicted.sem, pt_evicted.at(b))
                        for j in range(2 * H):
                            last = pe.transpose(ps[2][:, j * P:j * P + P], prob[:, b % 2, j // 2, j % 2 * P:j % 2 * P + P], ident[:])
                        last.then_inc(pt_ready.sem, 1)

                    def weigh(b):
                        pe.wait_ge(pt_evicted.sem, pt_evicted.at(b + 1))
                        pe.wait_ge(o_evicted.sem, o_evicted.at(b - 1))
                        for h in range(H):
                            rows = slice(h % 2 * 64, h % 2 * 64 + 64)
                            c = b % 2 * HALF + h // 2 * P
                            for t in range(2):
                                last = pe.matmul(ps[3][rows, c:c + P], v_tok[:, t, h * DH:h * DH + DH], prob_t[:, b % 2, 2 * place(h) + t],
                                                 start=(t == 0), stop=(t == 1))
                        last.then_inc(o_ready.sem, 1)

                    score(0)
                    pe.wait_ge(tr_evicted.sem, tr_evicted.at(1))
                    for b in range(TT):
                        if b + 1 < TT:
                            score(b + 1)
                        if b >= 1:
                            weigh(b - 1)
                        turn(b)
                    weigh(TT - 1)

            dve_steps.close()
            side_loaded.passed(1)
            for s, n in ((aux, 1), (sq_ready, 2), (stat_ready, 1), (norm_ready, 1), (sum_ready, 2), (h_ready, KT), (hi_ready, 1),
                         (lo_ready, 1), (evicted, 2), (evicted2, 4), (transposed, 3), (tr_evicted, 1), (scores, TT), (biased, TT),
                         (exped, TT), (probs, TT), (pt_ready, TT), (pt_evicted, TT), (o_ready, TT), (o_evicted, TT), (y_hi, TT)):
                s.passed(n)
            chunk_passed(6)

        SCORED = range(TOPK // P, TT)

        def keys_of(b):
            return (b + 1) * P

        def score_at(b):
            return sum(keys_of(c) for c in SCORED if c < b)

        def indexer_source(i, m):
            return chunk_of(w_in2, (P_Z, P_Z + P, I_Q, I_Q + P, I_Q + 2 * P, I_Q + 3 * P, I_K, S_K)[m])

        def indexer(y_hi_t, y_lo_t, score, kv_t, following):
            H = 8
            PAD = 16
            Z, SUM_A, SUM_B = (0, 3), 1, 2
            units = [(b, h) for b in SCORED for h in range(H)]
            n_y = len(units)
            with ExitStack() as sc, nc.Block() as block:
                pad = sb(sc, "pad", [P, 4, PAD + T])
                map_w = sb(sc, "map_w", [P, 2, P])
                inv_n = sb(sc, "inv_n", [P, 2, PAD])
                iq_t = sb(sc, "iq_t", [P, 4, T])
                kw_t = sb(sc, "kw_t", [P, T])
                ik_two = sb(sc, "ik_two", [P, T])
                head_w = sb(sc, "head_w", [P, TT, H])

                @block.sync
                def _(sp):
                    sp.wait_ge(aux.sem, aux.at(1))
                    for g in range(4):
                        half = g % 2 * 64
                        sp.dma_start(map_w[half:half + 64, g // 2, half:half + 64], a["pool_w_2"][0, g]).then_inc(side_loaded.sem, 16)
                    sp.dma_start(inv_n[:], a["k_pool"]).then_inc(side_loaded.sem, 16)
                    stream(sp, 1, 8, indexer_source, following)

                @block.gpsimd
                def _(pool):
                    pool.memset(map_w[:], 0.0).then_inc(aux.sem, 1)
                    pool.memset(pad[:, :, 0:PAD], 0.0).then_inc(aux.sem, 1)
                    for m in range(8):
                        rest_chunk(pool, m + 1, 0, 8)
                    for t in range(2):
                        pool.wait_ge(y_hi.sem, y_hi.at(t + 1))
                        pool.tensor_tensor(y_lo_t[:, t], pad[:, (SUM_A, SUM_B)[t], PAD:], y_hi_t[:, t].bitcast(F32), ALU.subtract)\
                            .then_inc(lo_ready.sem, 1)

                @block.scalar
                def _(act):
                    targets = [pad[:, Z[0], PAD:], pad[:, Z[1], PAD:]] + [iq_t[:, j] for j in range(4)] + [kw_t[:], kv_t[:]]
                    for m in range(8):
                        round_chunk(act, m + 1, 0, 8)
                        act.wait_ge(used.sem, after(used, m, 0, 8))
                        act.activation(targets[m], ps[m % 4][:], ACT.Copy).then_inc(evicted.sem, 1)
                    act.wait_ge(pt_ready.sem, pt_ready.at(1))
                    act.activation(ik_two[:], ps[2][:], ACT.Copy).then_inc(pt_evicted.sem, 1)
                    for t in range(2):
                        act.wait_ge(y_ready.sem, y_ready.at(t + 1))
                        act.activation(y_hi_t[:, t], pad[:, (SUM_A, SUM_B)[t], PAD:], ACT.Copy).then_inc(y_hi.sem, 1)
                    act.wait_ge(lo_ready.sem, lo_ready.at(2))
                    for n, (b, h) in enumerate(units):
                        act.wait_ge(scores.sem, scores.at(n + 1))
                        act.wait_ge(biased.sem, biased.at(n - 3))
                        act.activation(pad[:, n % 4, 0:keys_of(b)], ps[n % 4][:, 0:keys_of(b)], ACT.Relu).then_inc(exped.sem, 1)

                @block.vector
                def _(dve):
                    dve.wait_ge(side_loaded.sem, side_loaded.at(5))
                    dve.wait_ge(aux.sem, aux.at(2))

                    def doubled(dst, src, shift, rows):
                        dve_steps.wait(dve)
                        dve_steps.done(dve.tensor_tensor(pad[rows, dst, PAD:], pad[rows, src, PAD:],
                                                         pad[rows, src, PAD - shift:PAD + T - shift], ALU.add))

                    every, lower, upper = slice(0, P), slice(0, 64), slice(64, P)
                    for t in range(2):
                        dve.wait_ge(evicted.sem, evicted.at(t + 1))
                        doubled(SUM_A, Z[t], 1, every)
                        if t == 0:
                            doubled(SUM_B, SUM_A, 2, upper)
                        else:
                            doubled(SUM_B, SUM_A, 2, every)
                            doubled(SUM_A, SUM_B, 4, every)
                            doubled(SUM_B, SUM_A, 8, upper)
                        dve_steps.wait(dve)
                        for rows, s in ((lower, SUM_A), (upper, SUM_B)):
                            first, rest = slice(PAD, 2 * PAD), slice(2 * PAD, PAD + T)
                            dve_steps.done(dve.scalar_tensor_tensor(out=pad[rows, Z[t], rest], in0=pad[rows, s, rest],
                                                                    scalar=inv_n[rows, t, PAD - 1:PAD], in1=pad[rows, Z[t], rest],
                                                                    op0=ALU.mult, op1=ALU.subtract))
                            dve_steps.done(dve.tensor_tensor(pad[rows, s, first], pad[rows, s, first], inv_n[rows, t], ALU.mult))
                            dve_steps.wait(dve)
                            last = dve.tensor_tensor(pad[rows, Z[t], first], pad[rows, s, first], pad[rows, Z[t], first], ALU.subtract)
                            if s == SUM_A:
                                dve_steps.done(last)
                            else:
                                last.then_inc(h_ready.sem, 1)
                    for t in range(2):
                        dve.wait_ge(o_ready.sem, o_ready.at(t + 1))
                        dve.tensor_scalar(pad[:, (SUM_A, SUM_B)[t], PAD:], ps[t][:], column("pool_scale_2", t), None, ALU.mult)\
                           .then_inc(y_ready.sem, 1)
                    dve.wait_ge(transposed.sem, transposed.at(1))
                    dve.tensor_scalar(head_w[:], ps[3][:].rearrange("p (t c) -> p t c", c=P)[:, :, 64:64 + H],
                                      DH ** -0.5 * H ** -0.5, None, ALU.mult).then_inc(tr_evicted.sem, 1)
                    dve.wait_ge(tr_evicted.sem, tr_evicted.at(1))
                    for n, (b, h) in enumerate(units):
                        dve.wait_ge(exped.sem, exped.at(n + 1))
                        to, r = score[:, score_at(b):score_at(b) + keys_of(b)], pad[:, n % 4, 0:keys_of(b)]
                        if h == 0:
                            dve.tensor_scalar(to, r, head_w[:, b, 0:1], None, ALU.mult).then_inc(biased.sem, 1)
                        else:
                            dve.wait_ge(biased.sem, biased.at(n))
                            dve.scalar_tensor_tensor(out=to, in0=r, scalar=head_w[:, b, h:h + 1], in1=to,
                                                     op0=ALU.mult, op1=ALU.add).then_inc(biased.sem, 1)
                    dve.wait_ge(biased.sem, biased.at(n_y))
                    for b in SCORED:
                        end = score_at(b) + keys_of(b)
                        dve_steps.done(dve.memset(score[0:64, end - 64:end], NEG))

                @block.tensor
                def _(pe):
                    for m in range(8):
                        split_ready(pe, m, 0, 8)
                        pe.wait_ge(evicted.sem, evicted.at(m - 3))
                        product(pe, m % 2, wide(ps[m % 4])).then_inc(used.sem, 1)
                    pe.wait_ge(evicted.sem, evicted.at(7))
                    for c in (0, HALF):
                        for half in (0, 64):
                            last = pe.matmul(ps[2][half:half + 64, c:c + HALF], ident[0:64, 0:64], kw_t[0:64, c:c + HALF],
                                             start=True, stop=True)
                    last.then_inc(pt_ready.sem, 1)
                    pe.wait_ge(evicted.sem, evicted.at(8))
                    for t in range(TT):
                        last = pe.transpose(ps[3][:, t * P:t * P + P], kw_t[:, t * P:t * P + P], ident[:])
                    last.then_inc(transposed.sem, 1)
                    for t in range(2):
                        pe.wait_ge(h_ready.sem, h_ready.at(t + 1))
                        for c in (0, HALF):
                            last = pe.matmul(ps[t][:, c:c + HALF], map_w[:, t], pad[:, Z[t], PAD + c:PAD + c + HALF],
                                             start=True, stop=True)
                        last.then_inc(o_ready.sem, 1)
                    pe.wait_ge(y_ready.sem, y_ready.at(2))
                    pe.wait_ge(pt_evicted.sem, pt_evicted.at(1))
                    pe.wait_ge(tr_evicted.sem, tr_evicted.at(1))
                    for n in range(0, n_y, 2):
                        b, h = units[n]
                        pe.wait_ge(exped.sem, exped.at(n - 2))
                        n_keys = keys_of(b)
                        for c in range(0, n_keys, HALF):
                            to = min(c + HALF, n_keys)
                            for odd in range(2):
                                rows = slice(odd * 64, odd * 64 + 64)
                                last = pe.matmul(ps[(n + odd) % 4][:, c:to], iq_t[rows, h // 2, b * P:b * P + P], ik_two[rows, c:to],
                                                 start=True, stop=True)
                                if to == n_keys:
                                    last.then_inc(scores.sem, 1)

            dve_steps.close()
            side_loaded.passed(5)
            for s, n in ((aux, 2), (evicted, 8), (pt_ready, 1), (pt_evicted, 1), (transposed, 1), (tr_evicted, 1), (h_ready, 2),
                         (o_ready, 2), (y_ready, 2), (y_hi, 2), (lo_ready, 2), (scores, n_y), (exped, n_y), (biased, n_y)):
                s.passed(n)
            chunk_passed(8)

        def top_rounds(score, best, rounds):
            per = (2 * len(SCORED) + 2) * sum(rounds)

            def part(b):
                return score[:, score_at(b):score_at(b) + keys_of(b)]

            def beside(dve, i, u):
                if u == 0:
                    top_steps.open(i, per)
                for _ in range(rounds[u]):
                    top_steps.wait(dve)
                    top_steps.done(carry_wait(0))
                    for j, b in enumerate(SCORED):
                        top_steps.done(dve.max(best[:, j], part(b)))
                    top_steps.wait(dve)
                    top_steps.done(carry_wait(1))
                    for j, b in enumerate(SCORED):
                        top_steps.done(dve.match_replace(part(b), best[:, j], part(b), TAKEN))
            return beside

        def sparse_source(i, m):
            return chunk_of(w_in2, m * P + S_Q)

        def sparse_attention(y_hi_t, y_lo_t, score, kv_t, following):
            H = BW // DH
            order = (0, 7, 1, 6, 2, 5, 3, 4)
            turns = [(n, j) for n, b in enumerate(order) for j in range(b + 1)]
            with ExitStack() as sc, nc.Block() as block:
                q_t = sb(sc, "q_t", [P, 2, T])
                k_two = sb(sc, "k_two", [P, T])
                v_two = sb(sc, "v_two", [P, TT, 2, DH])
                edge = sb(sc, "edge", [P, keys_of(1)])
                prob_short = sb(sc, "prob_short", [P, H, keys_of(3)])
                prob_long = sb(sc, "prob_long", [P, H, keys_of(7)])
                prob_t = sb(sc, "prob_t", [P, 2, H * P])
                stat = sb(sc, "stat", [P, 2, 4, H])

                def place(h):
                    return h % 2 * 2 + h // 2

                def out_of(n, half):
                    c = n % 2 * HALF + half * 2 * P
                    return ps[3][half * 64:half * 64 + 64, c:c + 2 * P].rearrange("p (t c) -> p t c", c=P)

                def prob_of(n):
                    return (prob_short, prob_long)[n % 2][:, :, 0:keys_of(order[n])]

                @block.sync
                def _(sp):
                    stream(sp, 1, 2, sparse_source, following)

                @block.gpsimd
                def _(pool):
                    pool.memset(edge[:], 0.0).then_inc(aux.sem, 1)
                    pool.wait_ge(aux.sem, aux.at(1))
                    pool.memset(edge[0:64, keys_of(1) - 64:], NEG).then_inc(aux.sem, 1)
                    for m in range(2):
                        rest_chunk(pool, m + 1, 0, 2)

                @block.scalar
                def _(act):
                    act.wait_ge(transposed.sem, transposed.at(1))
                    act.activation(k_two[:], ps[2][:], ACT.Copy).then_inc(tr_evicted.sem, 1)
                    v = ps[3][:].rearrange("p (t c) -> p t c", c=P)[:, :, DH:]
                    for n in range(2):
                        last = act.activation(v_two[:, :, n], v, ACT.Copy)
                    last.then_inc(tr_evicted.sem, 1)
                    for m in range(2):
                        round_chunk(act, m + 1, 0, 2)
                        act.wait_ge(used.sem, after(used, m, 0, 2))
                        act.activation(q_t[:, m], ps[m][:], ACT.Copy).then_inc(evicted.sem, 1)

                    def exps(n):
                        act.wait_ge(mod_ready.sem, mod_ready.at(n + 1))
                        for h in range(H):
                            x = prob_of(n)[:, h]
                            last = act.activation(x, x, ACT.Exp, bias=stat[:, n % 2, 1, h:h + 1],
                                                  accum_out=stat[:, n % 2, 2, h:h + 1])
                        last.then_inc(exped.sem, 1)

                    exps(0)
                    for n, b in enumerate(order):
                        if n + 1 < TT:
                            exps(n + 1)
                        for j in range(b + 1):
                            x = turns.index((n, j))
                            act.wait_ge(pt_ready.sem, pt_ready.at(x + 1))
                            act.wait_ge(o_ready.sem, o_ready.at(x - 1))
                            act.activation(prob_t[:, x % 2], ps[2][:, x % 2 * HALF:x % 2 * HALF + HALF], ACT.Copy)\
                               .then_inc(pt_evicted.sem, 1)
                        act.wait_ge(o_ready.sem, o_ready.at(turns.index((n, b)) + 1))
                        for half in range(2):
                            rows = slice(half * 64, half * 64 + 64)
                            last = act.activation(y_hi_t[rows, :, b * P:b * P + P], out_of(n, half), ACT.Copy)
                        last.then_inc(y_hi.sem, 1)

                @block.vector
                def _(dve):
                    dve.wait_ge(aux.sem, aux.at(2))
                    for b in SCORED:
                        x = score[:, score_at(b):score_at(b) + keys_of(b)]
                        dve_steps.done(dve.tensor_scalar(x, x, TAKEN, NEG, ALU.not_equal, ALU.mult))
                    dve_steps.wait(dve)

                    def mask(b):
                        if b in SCORED:
                            return score[:, score_at(b):score_at(b) + keys_of(b)]
                        return edge[:, keys_of(1) - keys_of(b):]

                    def bias_scores(n):
                        b = order[n]
                        if n >= 2:
                            dve.wait_ge(pt_ready.sem, pt_ready.at(turns.index((n - 1, 0))))
                        for h in range(H):
                            x = n * H + h
                            dve.wait_ge(scores.sem, scores.at(x + 1))
                            dve.tensor_tensor_reduce(prob_of(n)[:, h], ps[x % 2][:, 0:keys_of(b)], mask(b), DH ** -0.5, -3e38,
                                                     ALU.add, ALU.max, stat[:, n % 2, 0, h:h + 1]).then_inc(biased.sem, 1)
                        dve.wait_ge(biased.sem, biased.at(n * H + H))
                        dve.tensor_scalar(stat[:, n % 2, 1], stat[:, n % 2, 0], -1.0, None, ALU.mult).then_inc(mod_ready.sem, 1)

                    def normalise(n):
                        dve.wait_ge(exped.sem, exped.at(n + 1))
                        dve_steps.done(dve.reciprocal(stat[:, n % 2, 3], stat[:, n % 2, 2]))
                        dve_steps.wait(dve)
                        x = prob_of(n)
                        dve.tensor_tensor(x, x, stat[:, n % 2, 3].rearrange("p (h k) -> p h k", k=1).broadcast_to(list(x.shape)),
                                          ALU.mult).then_inc(probs.sem, 1)

                    def rest_o(n):
                        dve.wait_ge(y_hi.sem, y_hi.at(n + 1))
                        b = order[n]
                        for half in range(2):
                            rows = slice(half * 64, half * 64 + 64)
                            last = dve.tensor_tensor(y_lo_t[rows, :, b * P:b * P + P], out_of(n, half),
                                                     y_hi_t[rows, :, b * P:b * P + P].bitcast(F32), ALU.subtract)
                        last.then_inc(o_evicted.sem, 1)

                    bias_scores(0)
                    for n in range(TT):
                        normalise(n)
                        if n + 1 < TT:
                            bias_scores(n + 1)
                        if n >= 1:
                            rest_o(n - 1)
                    rest_o(TT - 1)

                @block.tensor
                def _(pe):
                    for c in (0, HALF):
                        for half in (0, 64):
                            pe.matmul(ps[2][half:half + 64, c:c + HALF], ident[0:64, 0:64], kv_t[0:64, c:c + HALF],
                                      start=True, stop=True)
                    for t in range(TT):
                        last = pe.transpose(ps[3][:, t * P:t * P + P], kv_t[:, t * P:t * P + P], ident[:])
                    last.then_inc(transposed.sem, 1)
                    for m in range(2):
                        split_ready(pe, m, 0, 2)
                        product(pe, m, wide(ps[m])).then_inc(used.sem, 1)
                    pe.wait_ge(evicted.sem, evicted.at(2))
                    pe.wait_ge(tr_evicted.sem, tr_evicted.at(2))

                    def score_heads(n):
                        n_keys = keys_of(order[n])
                        for h0 in range(0, H, 2):
                            pe.wait_ge(biased.sem, biased.at(n * H + h0))
                            for c in range(0, n_keys, HALF):
                                to = min(c + HALF, n_keys)
                                for odd in range(2):
                                    rows = slice(odd * 64, odd * 64 + 64)
                                    last = pe.matmul(ps[odd][:, c:to], q_t[rows, h0 // 2, order[n] * P:order[n] * P + P],
                                                     k_two[rows, c:to], start=True, stop=True)
                                    if to == n_keys:
                                        last.then_inc(scores.sem, 1)

                    def turn(n, j):
                        x = turns.index((n, j))
                        pe.wait_ge(pt_evicted.sem, pt_evicted.at(x - 1))
                        for h in range(H):
                            c = x % 2 * HALF + place(h) * P
                            last = pe.transpose(ps[2][:, c:c + P], prob_of(n)[:, h, j * P:j * P + P], ident[:])
                        last.then_inc(pt_ready.sem, 1)

                    def weigh(n, j):
                        x = turns.index((n, j))
                        pe.wait_ge(pt_evicted.sem, pt_evicted.at(x + 1))
                        if j == 0:
                            pe.wait_ge(o_evicted.sem, o_evicted.at(n - 1))
                        pe.matmul(ps[3][:, n % 2 * HALF:n % 2 * HALF + HALF], v_two[:, j].rearrange("p a c -> p (a c)"), prob_t[:, x % 2],
                                  start=(j == 0), stop=(j == order[n])).then_inc(o_ready.sem, 1)

                    score_heads(0)
                    for n in range(TT):
                        if n + 1 < TT:
                            score_heads(n + 1)
                        pe.wait_ge(probs.sem, probs.at(n + 1))
                        for j in range(order[n] + 1):
                            turn(n, j)
                            if j >= 1:
                                weigh(n, j - 1)
                        weigh(n, order[n])

            dve_steps.close()
            X = len(turns)
            for s, n in ((aux, 2), (transposed, 1), (tr_evicted, 2), (evicted, 2), (scores, TT * H), (biased, TT * H), (mod_ready, TT),
                         (exped, TT), (probs, TT), (pt_ready, X), (pt_evicted, X), (o_ready, X), (o_evicted, TT), (y_hi, TT)):
                s.passed(n)
            chunk_passed(2)

        w_gate_up, w_down = a["w_ffn_gate_up_2"][0], a["w_ffn_down_2"][0]

        def down_rows(f):
            src = w_down.rearrange("(f p) n -> p f n", p=P)[:, bass.ds(f, 1)]
            return lambda slot: (slot.rearrange("p k n -> p (k n)").rearrange("p (a n) -> p a n", a=1), src)

        def ffn_source(i, m):
            return chunk_of(w_gate_up, m * DFF)

        def ffn(acc, following):
            N = (FT - 2) // 2

            def loop_source(i, m):
                tile = i * (2 * P) + (1 + m // 3) * P
                return down_rows(i * 2 + m // 3) if m % 3 == 2 else chunk_of(w_gate_up, tile + m % 3 * DFF)

            def end_source(i, m):
                return chunk_of(w_gate_up, (FT - 1) * P + m * DFF) if m < 2 else down_rows(FT - 2 + m - 2)

            begin = chunks[0]

            def sections(engine, body):
                chunks[0] = begin
                body(0, 2, 0, (("gate", 0), ("up", 0)))
                chunks[0] = begin + 2
                with engine.Fori(0, N) as i:
                    body(i, 6, 2, (("gate", 1), ("up", 1), ("down", 0), ("gate", 2), ("up", 2), ("down", 1)))
                chunks[0] = begin + 2 + 6 * N
                body(0, 4, 0, (("gate", FT - 1), ("up", FT - 1), ("down", FT - 2), ("down", FT - 1)))
                chunks[0] = begin

            with ExitStack() as sc, nc.Block() as block:
                gate = sb(sc, "gate", [P, T])
                act32 = sb(sc, "act32", [P, T])
                act_hi = sb(sc, "act_hi", [P, 2, T], F32R)
                act_lo = sb(sc, "act_lo", [P, 2, T], F32R)

                @block.sync
                def _(sp):
                    stream(sp, 1, 2, ffn_source, loop_source)
                    chunks[0] = begin + 2
                    stream(sp, N, 6, loop_source, end_source)
                    chunks[0] = begin + 2 + 6 * N
                    stream(sp, 1, 4, end_source, following)
                    chunks[0] = begin

                @block.gpsimd
                def _(pool):
                    pool.memset(acc[:], 0.0).then_inc(aux.sem, 1)

                    def body(i, per, n, parts):
                        for m, (part, f) in enumerate(parts):
                            if following or parts[-1] != ("down", FT - 1) or m + 1 < per:
                                rest_chunk(pool, m + 1, i, per)
                            if part == "up":
                                pool.wait_ge(y_hi.sem, y_hi.at(f + 1, i, n))
                                pool.tensor_tensor(act_lo[:, f % 2], act32[:], act_hi[:, f % 2].bitcast(F32), ALU.subtract)\
                                    .then_inc(lo_ready.sem, 1)
                    sections(pool, body)

                @block.scalar
                def _(act):
                    def body(i, per, n, parts):
                        for m, (part, f) in enumerate(parts):
                            if following or parts[-1] != ("down", FT - 1) or m + 1 < per:
                                round_chunk(act, m + 1, i, per)
                            if part == "gate":
                                act.wait_ge(used.sem, after(used, m, i, per))
                                act.wait_ge(h_ready.sem, h_ready.at(f, i, n))
                                act.activation(gate[:], ps[0][:], ACT.Silu).then_inc(evicted.sem, 1)
                            if part == "up":
                                act.wait_ge(h_ready.sem, h_ready.at(f + 1, i, n))
                                act.wait_ge(used.sem, after(used, m - 2, i, per))
                                act.activation(act_hi[:, f % 2], act32[:], ACT.Copy).then_inc(y_hi.sem, 1)
                    sections(act, body)

                @block.vector
                def _(dve):
                    dve.wait_ge(aux.sem, aux.at(1))

                    def body(i, per, n, parts):
                        for m, (part, f) in enumerate(parts):
                            if part == "up":
                                dve.wait_ge(evicted.sem, evicted.at(f + 1, i, n))
                                dve.wait_ge(used.sem, after(used, m, i, per))
                                dve.wait_ge(lo_ready.sem, lo_ready.at(f, i, n))
                                dve.tensor_tensor(act32[:], gate[:], ps[1][:], ALU.mult).then_inc(h_ready.sem, 1)
                            if part == "down":
                                for o in range(KT):
                                    if o < KT - 1:
                                        dve.wait_ge(o_ready.sem, o_ready.at((KT - 1) * f + o + 1, i, (KT - 1) * n))
                                    else:
                                        dve.wait_ge(used.sem, after(used, m, i, per))
                                    dve.wait_ge(o_evicted.sem, o_evicted.at(8 * f + o - 7 if f or n else 0, i, 8 * n))
                                    dve.tensor_tensor(acc[:, o], acc[:, o], ps[2 + o % 2][:], ALU.add).then_inc(o_evicted.sem, 1)
                    sections(dve, body)

                @block.tensor
                def _(pe):
                    def body(i, per, n, parts):
                        for m, (part, f) in enumerate(parts):
                            split_ready(pe, m, i, per)
                            if part == "gate":
                                pe.wait_ge(evicted.sem, evicted.at(f, i, n))
                                product(pe, m % 2, wide(ps[0])).then_inc(used.sem, 1)
                            if part == "up":
                                pe.wait_ge(h_ready.sem, h_ready.at(f, i, n))
                                product(pe, m % 2, wide(ps[1])).then_inc(used.sem, 1)
                            if part == "down":
                                pe.wait_ge(lo_ready.sem, lo_ready.at(f + 1, i, n))
                                for o in range(KT):
                                    pe.wait_ge(o_evicted.sem, o_evicted.at(8 * f + o - 1, i, 8 * n))
                                    for w, x in ((w_hi, act_hi), (w_hi, act_lo), (w_lo, act_hi)):
                                        for c in (0, HALF):
                                            last = pe.matmul(ps[2 + o % 2][:, c:c + HALF], w[:, m % 2, o], x[:, f % 2, c:c + HALF],
                                                             start=(w is w_hi and x is act_hi), stop=(w is w_lo))
                                    last.then_inc(o_ready.sem if o < KT - 1 else used.sem, 1)
                    sections(pe, body)

            aux.passed(1)
            for s, n in ((evicted, FT), (h_ready, FT), (y_hi, FT), (lo_ready, FT), (o_ready, (KT - 1) * FT), (o_evicted, KT * FT)):
                s.passed(n)
            chunk_passed(3 * FT)

        def finish(acc, res):
            with ExitStack() as sc, nc.Block() as block:
                sq = sb(sc, "sq", [P, 2, T])
                inv = sb(sc, "inv", [P, T])

                @block.sync
                def _(sp):
                    for d in range(KT):
                        sp.wait_ge(tr_evicted.sem, tr_evicted.at(d + 1))
                        sp.dma_start(out.rearrange("(t p) d -> p t d", p=P)[:, :, d * P:d * P + P],
                                     res[:, d].rearrange("p (t c) -> p t c", c=P)).then_inc(stored.sem, 16)
                    sp.wait_ge(stored.sem, stored.at(KT))

                @block.scalar
                def _(act):
                    for d in range(KT):
                        act.wait_ge(sum_ready.sem, sum_ready.at(d - 1))
                        act.activation(sq[:, d % 2], acc[:, d], ACT.Square).then_inc(sq_ready.sem, 1)
                    act.wait_ge(stat_ready.sem, stat_ready.at(1))
                    act.activation(inv[:], inv[:], ACT.Sqrt).then_inc(norm_ready.sem, 1)
                    for d in range(KT):
                        act.wait_ge(transposed.sem, transposed.at(d + 1))
                        act.activation(res[:, d], ps[d % 2][:], ACT.Copy).then_inc(tr_evicted.sem, 1)

                @block.vector
                def _(dve):
                    dve.wait_ge(sum_ready.sem, sum_ready.at(KT))
                    dve.tensor_scalar(inv[:], ps[3][:], 1.0 / D, EPS, ALU.mult, ALU.add).then_inc(stat_ready.sem, 1)
                    dve.wait_ge(norm_ready.sem, norm_ready.at(1))
                    dve_steps.done(dve.reciprocal(inv[:], inv[:]))
                    dve_steps.wait(dve)
                    for d in range(KT):
                        dve_steps.done(dve.scalar_tensor_tensor(out=acc[:, d], in0=acc[:, d], scalar=column("norm_ffn_post_2", d),
                                                                in1=inv[:], op0=ALU.mult, op1=ALU.mult))
                        dve_steps.wait(dve)
                        dve.tensor_tensor(acc[:, d], acc[:, d], res[:, d], ALU.add).then_inc(h_ready.sem, 1)

                @block.tensor
                def _(pe):
                    for d in range(KT):
                        pe.wait_ge(sq_ready.sem, sq_ready.at(d + 1))
                        for c in (0, HALF):
                            last = pe.matmul(ps[3][:, c:c + HALF], ones[:], sq[:, d % 2, c:c + HALF], start=(d == 0), stop=(d == KT - 1))
                        last.then_inc(sum_ready.sem, 1)
                    for d in range(KT):
                        pe.wait_ge(h_ready.sem, h_ready.at(d + 1))
                        pe.wait_ge(tr_evicted.sem, tr_evicted.at(d - 1))
                        for t in range(TT):
                            last = pe.transpose(ps[d % 2][:, t * P:t * P + P], acc[:, d, t * P:t * P + P], ident[:])
                        last.then_inc(transposed.sem, 1)

        rpb_rows = nc.dram_tensor("rpb_rows", [8 * N_DR, P], F32, kind="Internal").ap()
        x2_kept = nc.dram_tensor("x2_kept", [P, KT, T], F32, kind="Internal").ap()
        w_out1, w_out2 = a["w_out"][0], a["w_out_2"][0]
        with ExitStack() as first:
            with ExitStack() as branch:
                y_hi_t = sb(branch, "y_hi_t", [P, WB // P, T], F32R)
                y_lo_t = sb(branch, "y_lo_t", [P, WB // P, T], F32R)
                b_in = COL["b_in"]
                from_c, from_a, from_f = (
                    [(w_in, col, b_in + col // P, a[name][0], WB // P, y_hi_t, y_lo_t)]
                    for name, col in (("w_br_c", G_C), ("w_br_a", G_A), ("w_br_f", G_F)))
                with ExitStack() as attended:
                    hc_hi = sb(attended, "hc_hi", [P, KT, CTX], F32R)
                    hc_lo = sb(attended, "hc_lo", [P, KT, CTX], F32R)
                    setup(hc_hi, hc_lo, rpb_rows)
                    attention(hc_hi, hc_lo, rpb_rows, y_hi_t, y_lo_t, merge_source(from_c))
                acc = sb(first, "acc", [P, KT, T], side="right")
                merge(acc, from_c, False, conv_source)
                convolution(y_hi_t, y_lo_t, merge_source(from_a))
                merge(acc, from_a, True, fourier_source)
                fourier(y_hi_t, y_lo_t, merge_source(from_f))
                res = sb(first, "res", [P, KT, T], side="right")

                def load_x(sp):
                    sp.dma_start(res[:], a["x"][0].rearrange("(t p) d -> p t d", p=P)).then_inc(x_loaded.sem, 16)

                merge(acc, from_f, True, project_source(w_out1), early=load_x)
            project(w_out1, acc, res, True, ("final_g", "norm_mix_pre_2"), hgrn_source, x2_kept)
        with ExitStack() as second:
            with ExitStack() as early3:
                def pair(n):
                    return [sb(early3, f"y{n}_{part}", [P, BW // P, T], F32R, side="right") for part in ("hi", "lo")]

                ya_hi, ya_lo = pair("a")
                hgrn(ya_hi, ya_lo, memory_source)
                ym_hi, ym_lo = pair("m")
                memory_attention(ym_hi, ym_lo, indexer_source)
                yb_hi, yb_lo = pair("b")

                def branch2(n, y_hi, y_lo):
                    return (w_gate2[n], 0, None, w_branch2[n], BW // P, y_hi, y_lo)

                from_abm = [branch2(0, ya_hi, ya_lo), branch2(1, yb_hi, yb_lo), branch2(3, ym_hi, ym_lo)]
                score = sb(second, "score", [P, score_at(TT)])
                kv_t = sb(second, "kv_t", [P, T])
                indexer(yb_hi, yb_lo, score, kv_t, merge_source(from_abm))
                acc = sb(second, "acc", [P, KT, T])
                best = sb(second, "best", [P, len(SCORED), 8])
                merge(acc, from_abm, False, sparse_source, beside=top_rounds(score, best, (2, 1, 1) * 2))
                top_steps.close(KT // 2)
            with ExitStack() as late:
                yc_hi, yc_lo = (sb(late, f"yc_{part}", [P, BW // P, T], F32R, side="right") for part in ("hi", "lo"))
                from_y = [branch2(2, yc_hi, yc_lo)]
                sparse_attention(yc_hi, yc_lo, score, kv_t, merge_source(from_y))
                res = sb(second, "res", [P, KT, T])

                def load_x2(sp):
                    sp.dma_start(res[:], x2_kept).then_inc(x_loaded.sem, 16)

                merge(acc, from_y, True, project_source(w_out2), early=load_x2)
            project(w_out2, acc, res, False, ("norm_mix_post_2", "norm_ffn_pre_2"), ffn_source)
            ffn(acc, None)
            finish(acc, res)


_INS = ["x", "c", "ctx", "c_ctx", "norm_g", "w_ada", "b_ada", "w_in", "b_in", "w_conv", "b_conv", "rpb", "w_br_a",
        "w_br_f", "w_br_c", "w_out", "final_g", "mem_2", "lb_logits_2", "w_in_2", "w_gate_2", "w_branch_2", "w_out_2",
        "hgrn_norm_2", "pool_w_2", "pool_scale_2", "w_mem_kv_2", "norm_mem_2", "norm_mix_pre_2", "norm_mix_post_2",
        "norm_ffn_pre_2", "norm_ffn_post_2", "w_ffn_gate_up_2", "w_ffn_down_2"]


def kernel(**inputs):
    import concourse.bacc as _bacc
    from concourse.bass_utils import run_bass_kernel_spmd as _run

    nc = _bacc.Bacc("TRN2", target_bir_lowering=False, num_devices=1)
    arrays, args = {}, {}
    for name in _INS:
        arrays[f"in_{name}"] = np.ascontiguousarray(inputs[name])
    arrays.update(constants())
    for name, x in arrays.items():
        ap = nc.dram_tensor(name, x.shape, mybir.dt.from_np(x.dtype), kind="ExternalInput").ap()
        args[name.removeprefix("in_")] = ap
    out = nc.dram_tensor("out", [T, D], F32, kind="ExternalOutput").ap()
    first_then_second_block(nc, args, out)
    r = _run(nc, [arrays], core_ids=[0])
    return r.results[0]["out"].reshape(1, T, D)
```

```python
from contextlib import ExitStack

import numpy as np

import concourse.bass as bass
from concourse import mybir

P = 128
T = 1024
D = 1024
KT = D // P
TT = T // P
HALF = 512
CTX = 256
NMEM = 256
WB = 512
BW = 256
DFF = 2816
FT = DFF // P
GRID = 64
ROWS = T // GRID
WIN_H, WIN_W = 8, 16
N_DR, N_DC = 2 * WIN_H - 1, 2 * WIN_W - 1
DH = 64
CHUNK = 128
TOPK = 256
EPS = 1e-6
NEG = -1e30
TAKEN = -3e38
CREDIT = 4

F32 = mybir.dt.float32
F32R = mybir.dt.float32r
U32 = mybir.dt.uint32
ACT = mybir.ActivationFunctionType
ALU = mybir.AluOpType
AX = mybir.AxisListType.X

A_X, A_B, A_C, A_Z, F_U, F_Z, Q1, K1, V1, C_Z, G_A, G_F, G_C = (
    0, 512, 1024, 1536, 2048, 2560, 3072, 3584, 4096, 4608, 5120, 6144, 7168)
H_Q, H_F, H_I, H_G, P_Z, S_Q, S_K, S_V, I_Q, I_K, I_W, M_Q = (
    0, 512, 1024, 1280, 1536, 1792, 2048, 2112, 2176, 2688, 2752, 2760)

ROWS_A = [("norm_g", 8), ("b_ada", 24), ("b_in", 64), ("w_conv", 12), ("b_conv", 4), ("final_g", 8)]
ROWS_B = [("lb_logits_2", 4), ("hgrn_norm_2", 2), ("pool_scale_2", 2),
          ("norm_mem_2", 8), ("norm_mix_pre_2", 8), ("norm_mix_post_2", 8), ("norm_ffn_pre_2", 8),
          ("norm_ffn_post_2", 8)]
COL = {}
for _rows, _at in ((ROWS_A, 0), (ROWS_B, P)):
    for _name, _n in _rows:
        COL[_name] = _at
        _at += _n


def constants():
    t = np.arange(HALF)[:, None].astype(np.float64)
    k = np.arange(HALF + 1)[None, :]
    norm = 1.0 / np.sqrt(T * P)
    angle = 2 * np.pi * ((t * k) % T) / T
    c = np.arange(P)[:, None] * np.arange(P)[None, :] % P
    col = np.arange(GRID)
    start = np.clip(col - WIN_W // 2, 0, GRID - WIN_W)
    inside = (col[None, :] >= start[:, None]) & (col[None, :] < start[:, None] + WIN_W)
    s, q = np.arange(CHUNK)[:, None], np.arange(CHUNK)[None, :]
    levels = []
    for b in (64, 32, 16, 8, 4, 2, 1):
        levels.append((s // (2 * b) == q // (2 * b)) & (s % (2 * b) < b) & (q % (2 * b) >= b))
    levels.append(s == q)
    pool = np.zeros((P, 2, 16))
    for tile, ws in enumerate(((2, 4), (8, 16))):
        for half, w in enumerate(ws):
            pool[half * 64:half * 64 + 64, tile] = 1.0 / np.minimum(np.arange(16) + 1, w)
    f = np.float32
    return {
        "k_ident": np.eye(P, dtype=f),
        "k_cos": (np.cos(angle) * norm).astype(f),
        "k_sin": (np.sin(angle) * norm).astype(f),
        "k_alt": (((-1.0) ** k) * norm).astype(f),
        "k_chan": np.stack([np.cos(2 * np.pi * c / P), np.sin(2 * np.pi * c / P)], 1).astype(f),
        "k_window": np.where(np.concatenate([inside[::-1]] * 2, 0), 0.0, NEG).astype(f),
        "k_levels": np.stack(levels, 1).astype(f),
        "k_pool": pool.astype(f),
        "k_blocks": np.kron(np.eye(2), np.ones((64, 64))).astype(f),
    }


class Signal:

    def __init__(self, sem, unit=1):
        self.sem, self.unit, self.base = sem, unit, CREDIT if unit == 1 else 0

    def at(self, k, i=0, per=0):
        return i * (per * self.unit) + (self.base + k * self.unit)

    def passed(self, units):
        self.base += units * self.unit


class Steps:

    def __init__(self, counted):
        self.counted, self.k, self.i, self.per = counted, 0, 0, 0

    def open(self, i, per):
        self.i, self.per, self.k = i, per, 0

    def done(self, instruction):
        instruction.then_inc(self.counted.sem, 1)
        self.k += 1

    def wait(self, engine, k=None):
        engine.wait_ge(self.counted.sem, self.counted.at(self.k if k is None else k, self.i, self.per))

    def close(self, loops=1):
        assert self.per in (0, self.k), ("steps of one iteration", self.per, self.k)
        self.counted.passed(self.k * loops)
        self.k = self.per = self.i = 0


def first_then_second_block(nc, a, out):
    ctx = ExitStack()
    with ctx:
        sem_list = []
        names = {}

        def signal(name, unit=1):
            s = Signal(ctx.enter_context(nc.semaphore(name)), unit)
            sem_list.append(s)
            return s

        def sb(scope, name, shape, dt=F32, side=None):
            names[name] = names.get(name, 0) + 1
            full = name if names[name] == 1 else f"{name}_{names[name]}"
            return scope.enter_context(nc.sbuf_tensor(full, shape, dt, side=side))

        raw = sb(ctx, "raw", [P, 2, KT, P])
        w_hi = sb(ctx, "w_hi", [P, 2, KT, P], F32R)
        w_lo = sb(ctx, "w_lo", [P, 2, KT, P], F32R)
        h_hi = sb(ctx, "h_hi", [P, KT, T], F32R)
        h_lo = sb(ctx, "h_lo", [P, KT, T], F32R)
        vec = sb(ctx, "vec", [P, 2 * P])
        ident = sb(ctx, "ident", [P, P])
        ones = sb(ctx, "ones", [P, P])
        cond = sb(ctx, "cond", [P, KT, 2])
        gate_t = sb(ctx, "gate_t", [P, KT])
        q_bias = sb(ctx, "q_bias", [P, 4])
        carrier = sb(ctx, "carrier", [P, 4])
        lb = sb(ctx, "lb", [P, 8])
        ps = [ctx.enter_context(nc.psum_tensor(f"ps{n}", [P, 2 * HALF], F32)) for n in range(4)]

        loaded = [signal(f"weights_loaded{s}", 16) for s in range(2)]
        rounded = signal("weights_rounded")
        split = signal("weights_split")
        used = signal("weights_used")
        const_loaded = signal("const_loaded", 16)
        x_loaded = signal("x_loaded", 16)
        side_loaded = signal("side_loaded", 16)
        tabs = [signal(f"table_loaded{s}", 16) for s in range(2)]
        stored = signal("stored", 16)
        ada_loaded = [signal(f"ada_loaded{s}", 16) for s in range(3)]
        evicted = signal("evicted")
        evicted2 = signal("evicted2")
        h_ready = signal("h_ready")
        hi_ready = signal("hi_ready")
        lo_ready = signal("lo_ready")
        lo_ready2 = signal("lo_ready2")
        transposed = signal("transposed")
        tr_evicted = signal("tr_evicted")
        scores = signal("scores_ready")
        biased = signal("biased")
        exped = signal("exped")
        probs = signal("probs_ready")
        pt_ready = signal("pt_ready")
        pt_evicted = signal("pt_evicted")
        o_ready = signal("o_ready")
        o_evicted = signal("o_evicted")
        y_ready = signal("y_ready")
        y_ready2 = signal("y_ready2")
        y_hi = signal("y_hi")
        mod_ready = signal("mod_ready")
        norm_ready = signal("norm_ready")
        stat_ready = signal("stat_ready")
        sq_ready = signal("sq_ready")
        sum_ready = signal("sum_ready")
        aux = signal("aux")
        aux2 = signal("aux2")
        aux3 = signal("aux3")
        aux4 = signal("aux4")
        act_steps = Steps(signal("act_steps"))
        dve_steps = Steps(signal("dve_steps"))
        top_steps = Steps(signal("top_steps"))

        chunks = [0]

        def column(name, t=0, n=1):
            return vec[:, COL[name] + t:COL[name] + t + n]

        def carry_wait(k):
            return nc.vector.memset(carrier[:, k:k + 1], 0.0)

        def pool_carry_wait():
            return nc.gpsimd.tensor_tensor(carrier[:, 3:4], ones[:, 0:1], ones[:, 0:1], ALU.add)

        def after(sig, m, i, per):
            return sig.at(chunks[0] + m + 1, i, per)

        def half_after(sig, m, half, i, per):
            return sig.at(2 * (chunks[0] + m) + half + 1, i, 2 * per)

        def load_chunk(sp, m, i, per, pieces):
            sp.wait_ge(split.sem, half_after(split, m - 2, 1, i, per))
            s = m % 2
            dst, src = pieces(raw[:, s])
            sp.dma_start(dst, src).then_inc(loaded[s].sem, 16)

        def stream(sp, iters, per, source, following, each=None):
            def body(i, last):
                if each:
                    each(sp, i)
                for m in range(2, per + 2):
                    if m < per:
                        load_chunk(sp, m, i, per, source(i, m))
                    elif not last:
                        load_chunk(sp, m, i, per, source(i + 1, m - per))
                    elif following:
                        load_chunk(sp, m, i, per, following(0, m - per))
            if iters > 1:
                with sp.Fori(0, iters - 1) as i:
                    body(i, False)
            body(iters - 1, True)

        def round_chunk(act, m, i, per, kt=KT):
            s = m % 2
            act.wait_ge(loaded[s].sem, loaded[s].at((chunks[0] + m - s) // 2 + 1, i, per // 2))
            act.wait_ge(used.sem, after(used, m - 2, i, per))
            for cut in (slice(0, kt // 2), slice(kt // 2, kt)):
                act.activation(w_hi[:, s, cut], raw[:, s, cut], ACT.Copy).then_inc(rounded.sem, 1)

        def rest_chunk(pool, m, i, per, kt=KT):
            s = m % 2
            for half, cut in enumerate((slice(0, kt // 2), slice(kt // 2, kt))):
                pool.wait_ge(rounded.sem, half_after(rounded, m, half, i, per))
                pool.tensor_tensor(w_lo[:, s, cut], raw[:, s, cut], w_hi[:, s, cut].bitcast(F32),
                                   ALU.subtract).then_inc(split.sem, 1)

        def split_ready(pe, m, i, per, half=0):
            pe.wait_ge(split.sem, half_after(split, m, half, i, per))

        def product(pe, chunk, outs, kt=KT, arrived=None, part=(0, 1)):
            order = [(k, o) for o in outs for k in range(kt)] if arrived is None else \
                    [(k, o) for k in range(kt) for o in outs]
            for k, (dst, hi, lo) in order[len(order) * part[0] // part[1]:len(order) * (part[0] + 1) // part[1]]:
                if arrived and dst is outs[0][0]:
                    arrived(k)
                if k == kt // 2 and dst is outs[0][0]:
                    split_ready(pe, *chunk, half=1)
                for n, (w, x) in enumerate(((w_hi, hi), (w_hi, lo), (w_lo, hi))):
                    last = pe.matmul(dst, w[:, chunk[0] % 2, k], x(k), start=(k == 0 and n == 0), stop=(k == kt - 1 and n == 2))
            return last

        def halves(dst, hi, lo):
            def cut(x, c):
                return lambda k: x[:, k, c:c + HALF]
            return [(dst[:, c:c + HALF], cut(hi, c), cut(lo, c)) for c in (0, HALF)]

        def wide(dst):
            return halves(dst, h_hi, h_lo)

        def chunk_of(w, col):
            kt = w.shape[0] // P
            src = w.rearrange("(k p) n -> p k n", p=P)
            return lambda slot: (slot[:, 0:kt], src[:, :, bass.ds(col, P)])

        w_in, w_in2 = a["w_in"][0], a["w_in_2"][0]
        w_gate2, w_branch2 = a["w_gate_2"][0], a["w_branch_2"][0]
        def attention_source(i, m):
            return chunk_of(w_in, (Q1, K1, V1, C_Z)[m] + i * P)

        ada = a["w_ada"][0].rearrange("(k p) n -> p k n", p=P)

        def setup(hc_hi, hc_lo, rpb_rows):
            SLOTS = 3
            with ExitStack() as sc, nc.Block() as block:
                rows = sb(sc, "rows", [P, 2, P])
                cond_rows = sb(sc, "cond_rows", [2 * KT, P])
                rpb_pad = sb(sc, "rpb_pad", [8 * N_DR, P])
                x_tok = sb(sc, "x_tok", [P, TT, D])
                c_tok = sb(sc, "c_tok", [P, CTX // P, D])
                w_ada = sb(sc, "w_ada", [P, SLOTS, 2 * D])
                sums = sb(sc, "sums", [P, 10])
                rstd = sb(sc, "rstd", [P, 10])
                power = sb(sc, "power", [P, 10])
                scale = sb(sc, "scale", [P, KT, 2])
                shift = sb(sc, "shift", [P, KT, 2])
                lb_tmp = sb(sc, "lb_tmp", [P, 8])
                h32 = w_ada[:, 0].rearrange("p (n t) -> p n t", n=2)
                mod_rows = w_ada[0:2, 1]
                n_rows = len(ROWS_A) + len(ROWS_B)

                def tokens(t):
                    return x_tok[:, t] if t < TT else c_tok[:, t - TT]

                def split_of(n):
                    if n < KT:
                        return h32[:, n % 2], h_hi[:, n], h_lo[:, n]
                    cut = slice(4 * (n - KT), 4 * (n - KT) + 4)
                    return h32[:, n % 2].rearrange("p (d t) -> p d t", d=4), hc_hi[:, cut], hc_lo[:, cut]

                def rest_of(engine, n):
                    src, hi, lo = split_of(n)
                    engine.wait_ge(hi_ready.sem, hi_ready.at(n + 1))
                    engine.tensor_tensor(lo, src, hi.bitcast(F32), ALU.subtract).then_inc((lo_ready, lo_ready2)[n % 2].sem, 1)

                @block.sync
                def _(sp):
                    sp.dma_start(ident[:], a["k_ident"]).then_inc(const_loaded.sem, 16)
                    sp.dma_start(cond_rows[0:KT], a["c"][0].rearrange("(t p) -> t p", p=P)).then_inc(const_loaded.sem, 16)
                    sp.dma_start(cond_rows[KT:], a["c_ctx"].rearrange("(t p) -> t p", p=P)).then_inc(const_loaded.sem, 16)
                    for k in range(KT):
                        if k >= SLOTS:
                            sp.wait_ge(aux2.sem, aux2.at(k - SLOTS + 1))
                        sp.dma_start(w_ada[:, k % SLOTS], ada[:, k, 0:2 * D]).then_inc(ada_loaded[k % SLOTS].sem, 16)
                    for m in range(2):
                        load_chunk(sp, m, 0, 4, attention_source(0, m))

                @block.gpsimd
                def _(pool):
                    for s in sem_list:
                        if s.unit == 1:
                            pool.sem_inc(s.sem, CREDIT)
                    pool.memset(rows[:], 0.0).then_inc(aux.sem, 1)
                    pool.memset(rpb_pad[:], 0.0).then_inc(aux3.sem, 1)
                    pool.memset(power[:], -0.5).then_inc(mod_ready.sem, 1)
                    pool.memset(ones[:], 1.0).then_inc(mod_ready.sem, 1)
                    pool.wait_ge(stat_ready.sem, stat_ready.at(1))
                    pool.wait_ge(mod_ready.sem, mod_ready.at(2))
                    pool.tensor_tensor(rstd[:], sums[:], power[:], ALU.pow).then_inc(norm_ready.sem, 1)
                    rest_chunk(pool, 0, 0, 4)
                    for n in range(0, 10, 2):
                        rest_of(pool, n)

                @block.scalar
                def _(act):
                    act.dma_start(x_tok[:], a["x"][0].rearrange("(t p) d -> p t d", p=P)).then_inc(x_loaded.sem, 16)
                    act.dma_start(c_tok[:], a["ctx"][0].rearrange("(t p) d -> p t d", p=P)).then_inc(x_loaded.sem, 16)
                    act.wait_ge(aux.sem, aux.at(1))
                    for group, which in ((ROWS_A, 0), (ROWS_B, 1)):
                        for name, n in group:
                            at = COL[name] - which * P
                            flat = a[name]
                            while len(flat.shape) > 1:
                                flat = flat.rearrange("a b ... -> (a b) ...")
                            act.dma_start(rows[at:at + n, which, :], flat.rearrange("(t p) -> t p", p=P))\
                               .then_inc(side_loaded.sem, 16)
                    act.wait_ge(aux3.sem, aux3.at(1))
                    act.dma_start(rpb_pad[:, 48:48 + N_DC], a["rpb"][0].rearrange("h r c -> (h r) c"))\
                       .then_inc(tabs[0].sem, 16)
                    act.wait_ge(transposed.sem, transposed.at(1))
                    act.activation(cond[:], ps[0][:, 0:2 * KT].rearrange("p (v t) -> p t v", v=2), ACT.Silu).then_inc(y_ready.sem, 1)
                    act.wait_ge(tabs[0].sem, tabs[0].at(1))
                    act.dma_start(rpb_rows, rpb_pad[:]).then_inc(stored.sem, 16)
                    act.wait_ge(x_loaded.sem, x_loaded.at(2))
                    for t in range(10):
                        act_steps.wait(act)
                        act_steps.done(act.activation(h_lo[:, 0], tokens(t), ACT.Square, accum_out=sums[:, t:t + 1]))
                    act.wait_ge(biased.sem, biased.at(1))
                    act.activation(lb_tmp[:, 4:8], lb_tmp[:, 0:4], ACT.Exp).then_inc(exped.sem, 1)
                    round_chunk(act, 0, 0, 4)
                    act.wait_ge(aux2.sem, aux2.at(KT))
                    act.activation(mod_rows[:, 0:D], ps[2][0:2, :], ACT.Copy).then_inc(evicted.sem, 1)
                    act.wait_ge(probs.sem, probs.at(1))
                    for d in range(KT):
                        act.wait_ge(transposed.sem, transposed.at(3 + d + (d >= 2)))
                        if d >= 2:
                            half = (lo_ready, lo_ready2)[d % 2]
                            act.wait_ge(half.sem, half.at(d // 2))
                        act.activation(h32[:, d % 2], ps[d % 2][:], ACT.Identity, bias=shift[:, d, 0:1],
                                       scale=scale[:, d, 0:1]).then_inc(h_ready.sem, 1)
                    for g in range(2):
                        act.wait_ge(transposed.sem, transposed.at(3 + KT + 1 + g))
                        half = (lo_ready, lo_ready2)[g]
                        act.wait_ge(half.sem, half.at(4))
                        for d in range(4):
                            act.activation(h32[:, g, d * CTX:(d + 1) * CTX],
                                           ps[2 + g][:, d * CTX:(d + 1) * CTX], ACT.Identity,
                                           bias=shift[:, 4 * g + d, 1:2],
                                           scale=scale[:, 4 * g + d, 1:2]).then_inc(h_ready.sem, 1)

                @block.vector
                def _(dve):
                    dve.wait_ge(transposed.sem, transposed.at(2))
                    dve.tensor_copy(vec[:], ps[1][:, 0:2 * P]).then_inc(aux4.sem, 1)
                    dve.wait_ge(aux4.sem, aux4.at(1))
                    lbl = column("lb_logits_2", 0, 4)
                    dve.tensor_tensor(lb_tmp[:, 0:4], lbl, lbl, ALU.subtract).then_inc(biased.sem, 1)
                    dve.wait_ge(act_steps.counted.sem, act_steps.counted.at(10))
                    dve.tensor_scalar(sums[:], sums[:], 1.0 / D, EPS, ALU.mult, ALU.add).then_inc(stat_ready.sem, 1)
                    dve.wait_ge(norm_ready.sem, norm_ready.at(1))
                    for t in range(10):
                        dve.tensor_scalar(tokens(t), tokens(t), rstd[:, t:t + 1], None, ALU.mult).then_inc(sq_ready.sem, 1)
                    dve.wait_ge(exped.sem, exped.at(1))
                    dve_steps.done(dve.reciprocal(lb_tmp[:, 0:4], lb_tmp[:, 4:8]))
                    dve_steps.wait(dve)
                    dve_steps.done(dve.tensor_tensor(lb_tmp[:, 4:8], lb_tmp[:, 4:8], lb_tmp[:, 0:4], ALU.mult))
                    dve_steps.wait(dve)
                    dve_steps.done(dve.tensor_tensor(lb[:, 0:4], lb_tmp[:, 4:8], lb_tmp[:, 4:8], ALU.subtract))
                    dve_steps.wait(dve)
                    dve_steps.done(dve.tensor_scalar(lb[:, 4:8], lb[:, 0:4], -1.0, 1.0, ALU.mult, ALU.add))
                    dve_steps.done(dve.tensor_scalar(q_bias[:], column("b_in", Q1 // P, 4), DH ** -0.5, None, ALU.mult))
                    dve.wait_ge(aux2.sem, aux2.at(KT))
                    dve.tensor_copy(mod_rows[:, D:2 * D], ps[3][0:2, :]).then_inc(evicted2.sem, 1)
                    dve.wait_ge(transposed.sem, transposed.at(5))
                    mods = ps[2][:, 0:4 * KT].rearrange("p (j v) -> p j v", v=2)
                    for v in range(2):
                        dve_steps.done(dve.tensor_tensor(shift[:, :, v], mods[:, 0:KT, v], column("b_ada", 0, KT), ALU.add))
                        dve_steps.done(dve.tensor_tensor(scale[:, :, v], mods[:, KT:, v], column("b_ada", KT, KT), ALU.add))
                        dve_steps.wait(dve)
                        last = dve.scalar_tensor_tensor(out=scale[:, :, v], in0=scale[:, :, v], scalar=1.0,
                                                        in1=column("norm_g", 0, KT), op0=ALU.add, op1=ALU.mult)
                        if v == 0:
                            dve_steps.done(last)
                        else:
                            last.then_inc(probs.sem, 1)
                    for n in range(10):
                        dve.wait_ge(h_ready.sem, h_ready.at(n + 1 if n < KT else KT + 4 * (n - KT) + 4))
                        src, hi, _ = split_of(n)
                        dve.tensor_copy(hi, src).then_inc(hi_ready.sem, 1)
                        if n % 2:
                            rest_of(dve, n)

                @block.tensor
                def _(pe):
                    pe.wait_ge(const_loaded.sem, const_loaded.at(3))
                    pe.transpose(ps[0][:, 0:2 * KT], cond_rows[:], ident[0:2 * KT, 0:2 * KT]).then_inc(transposed.sem, 1)
                    pe.wait_ge(side_loaded.sem, side_loaded.at(n_rows))
                    for which in range(2):
                        last = pe.transpose(ps[1][:, which * P:which * P + P], rows[:, which], ident[:])
                    last.then_inc(transposed.sem, 1)
                    pe.wait_ge(y_ready.sem, y_ready.at(1))
                    for k in range(KT):
                        pe.wait_ge(ada_loaded[k % SLOTS].sem, ada_loaded[k % SLOTS].at(k // SLOTS + 1))
                        for n in range(4):
                            last = pe.matmul(ps[2 + n // 2][0:2, n % 2 * HALF:n % 2 * HALF + HALF], cond[:, k],
                                             w_ada[:, k % SLOTS, n * HALF:n * HALF + HALF], start=(k == 0), stop=(k == KT - 1))
                        last.then_inc(aux2.sem, 1)

                    def turn(d):
                        for t in range(TT):
                            last = pe.transpose(ps[d % 2][:, t * P:t * P + P], x_tok[:, t, d * P:d * P + P], ident[:])
                        last.then_inc(transposed.sem, 1)

                    pe.wait_ge(sq_ready.sem, sq_ready.at(10))
                    pe.wait_ge(aux4.sem, aux4.at(1))
                    turn(0)
                    turn(1)
                    pe.wait_ge(evicted.sem, evicted.at(1))
                    pe.wait_ge(evicted2.sem, evicted2.at(1))
                    for j in range(2 * KT):
                        last = pe.transpose(ps[2][:, 2 * j:2 * j + 2], mod_rows[:, j * P:j * P + P], ident[0:2, 0:2])
                    last.then_inc(transposed.sem, 1)
                    for d in range(2, KT):
                        pe.wait_ge(h_ready.sem, h_ready.at(d - 1))
                        turn(d)
                    pe.wait_ge(probs.sem, probs.at(1))
                    for g in range(2):
                        for d in range(4):
                            for t in range(CTX // P):
                                last = pe.transpose(ps[2 + g][:, d * CTX + t * P:d * CTX + t * P + P],
                                                    c_tok[:, t, (4 * g + d) * P:(4 * g + d + 1) * P], ident[:])
                        last.then_inc(transposed.sem, 1)

            const_loaded.passed(3)
            x_loaded.passed(2)
            side_loaded.passed(n_rows)
            stored.passed(1)
            tabs[0].passed(1)
            for n, s in enumerate(ada_loaded):
                s.passed(len(range(n, KT, SLOTS)))
            act_steps.close()
            dve_steps.close()
            for s, n in ((aux, 1), (aux2, KT), (aux3, 1), (aux4, 1), (mod_ready, 2), (stat_ready, 1), (norm_ready, 1),
                         (y_ready, 1), (sq_ready, 10), (biased, 1), (exped, 1), (probs, 1), (transposed, 13),
                         (h_ready, 16), (hi_ready, 10), (lo_ready, 5), (lo_ready2, 5), (evicted, 1), (evicted2, 1)):
                s.passed(n)

        def attention(hc_hi, hc_lo, rpb_rows, y_hi_t, y_lo_t, following):
            N = 4
            KEYS = WIN_H * GRID
            ALL = KEYS + CTX
            with ExitStack() as sc, nc.Block() as block:
                diag_all = sb(sc, "diag_all", [P, 4, N_DR, GRID])
                window = sb(sc, "window", [P, GRID])
                bias = sb(sc, "bias", [P, N_DR, GRID])
                q_blk = sb(sc, "q_blk", [P, ROWS, P])
                k_t = sb(sc, "k_t", [P, T])
                kc_t = sb(sc, "kc_t", [P, CTX])
                v_t = sb(sc, "v_t", [P, T])
                y32 = v_t
                vc_t = sb(sc, "vc_t", [P, CTX])
                v_even = sb(sc, "v_even", [P, TT, P])
                v_odd = sb(sc, "v_odd", [P, TT - 1, P])
                v_ctx = sb(sc, "v_ctx", [P, CTX // P, P])
                z_silu = sb(sc, "z_silu", [P, T])
                prob = sb(sc, "prob", [P, 2, ALL])
                prob_t = sb(sc, "prob_t", [P, 2, ALL // P, P])
                stat = sb(sc, "stat", [P, 2, 8])
                minus = sb(sc, "minus", [P, 1])

                def row_start(r):
                    return min(max(r - WIN_H // 2, 0), ROWS - WIN_H)

                def value_tiles(r):
                    rs = row_start(r)
                    src = v_even if rs % 2 == 0 else v_odd
                    return [src[:, rs // 2 + j] for j in range(4)] + [v_ctx[:, j] for j in range(2)]

                @block.sync
                def _(sp):
                    sp.wait_ge(stored.sem, stored.at(0))
                    sp.dma_start(window[:], a["k_window"]).then_inc(side_loaded.sem, 16)
                    for pair in range(4):
                        for half in range(2):
                            src = bass.AP(rpb_rows.tensor, (2 * pair + half) * N_DR * P, [[1, GRID], [P, N_DR], [1, GRID]])
                            sp.dma_start(diag_all[half * 64:half * 64 + 64, pair], src).then_inc(side_loaded.sem, 16)
                    stream(sp, N, 4, attention_source, following)

                @block.gpsimd
                def _(pool):
                    pool.memset(q_blk[:], 0.0).then_inc(aux.sem, 1)
                    pool.memset(minus[:], -1.0).then_inc(aux.sem, 1)
                    with pool.Fori(0, N) as i:
                        for m in range(4):
                            rest_chunk(pool, m + 1, i, 4)
                        pool.wait_ge(y_hi.sem, y_hi.at(1, i, 1))
                        pool.tensor_tensor(y_lo_t[:, bass.ds(i, 1)], y32[:].rearrange("p (a t) -> p a t", a=1),
                                           y_hi_t[:, bass.ds(i, 1)].bitcast(F32), ALU.subtract)\
                            .then_inc(y_ready.sem, 1)

                @block.scalar
                def _(act):
                    act.wait_ge(aux.sem, aux.at(2))
                    with act.Fori(0, N) as i:
                        round_chunk(act, 1, i, 4)
                        act.wait_ge(used.sem, after(used, 0, i, 4))
                        for half in range(2):
                            p0 = half * 64
                            last = act.activation(q_blk[p0:p0 + 64, :, p0:p0 + 64][:, :, ::-1],
                                                  ps[0][p0:p0 + 64].rearrange("p (r c) -> p r c", c=GRID), ACT.Identity,
                                                  bias=q_bias[p0:p0 + 64, bass.ds(i, 1)], scale=DH ** -0.5)
                        last.then_inc(evicted.sem, 1)
                        round_chunk(act, 2, i, 4)
                        round_chunk(act, 3, i, 4)
                        act.wait_ge(used.sem, after(used, 2, i, 4))
                        act.wait_ge(y_ready.sem, y_ready.at(0, i, 1))
                        act.activation(v_t[:], ps[0][:], ACT.Identity, bias=vec[:, bass.ds(i + (COL["b_in"] + V1 // P), 1)])
                        act.activation(vc_t[:], ps[2][:, HALF:HALF + CTX], ACT.Identity,
                                       bias=vec[:, bass.ds(i + (COL["b_in"] + V1 // P), 1)]).then_inc(h_ready.sem, 1)
                        round_chunk(act, 4, i, 4)
                        act.wait_ge(used.sem, after(used, 3, i, 4))
                        act.activation(z_silu[:], ps[1][:], ACT.Silu,
                                       bias=vec[:, bass.ds(i + (COL["b_in"] + C_Z // P), 1)]).then_inc(mod_ready.sem, 1)
                        act.wait_ge(transposed.sem, transposed.at(1, i, 3))
                        act.activation(v_even[:], ps[3][:].rearrange("p (t c) -> p t c", c=P), ACT.Copy)\
                           .then_inc(tr_evicted.sem, 1)

                        def exps(r):
                            b = r % 2
                            act.wait_ge(biased.sem, biased.at(r + 1, i, ROWS))
                            act.activation(prob[:, b, 0:KEYS], prob[:, b, 0:KEYS], ACT.Exp, bias=stat[:, b, 2:3],
                                           accum_out=stat[:, b, 3:4])
                            act.activation(prob[:, b, KEYS:ALL], ps[b][:, HALF:HALF + CTX], ACT.Exp, bias=stat[:, b, 2:3],
                                           accum_out=stat[:, b, 4:5]).then_inc(exped.sem, 1)

                        def evict_probs(r):
                            act.wait_ge(pt_ready.sem, pt_ready.at(r + 1, i, ROWS))
                            act.wait_ge(o_ready.sem, o_ready.at(r - 1, i, ROWS))
                            act.activation(prob_t[:, r % 2], ps[2][:, 0:ALL].rearrange("p (j c) -> p j c", c=P), ACT.Copy)\
                               .then_inc(pt_evicted.sem, 1)

                        exps(0)
                        for r in range(ROWS):
                            if r + 1 < ROWS:
                                exps(r + 1)
                            evict_probs(r)
                        act.wait_ge(o_evicted.sem, o_evicted.at(4, i, 4))
                        act.activation(y_hi_t[:, bass.ds(i, 1)], y32[:].rearrange("p (a t) -> p a t", a=1), ACT.Copy)\
                           .then_inc(y_hi.sem, 1)

                @block.vector
                def _(dve):
                    dve.wait_ge(side_loaded.sem, side_loaded.at(9))
                    dve.wait_ge(aux.sem, aux.at(2))
                    with dve.Fori(0, N) as i:
                        dve.tensor_tensor(bias[:], diag_all[:, bass.ds(i, 1)].rearrange("p a r c -> p (a r) c"),
                                          window[:].rearrange("p (a c) -> p a c", a=1).broadcast_to([P, N_DR, GRID]),
                                          ALU.add).then_inc(aux2.sem, 1)
                        dve.wait_ge(used.sem, after(used, 1, i, 4))
                        kb = vec[:, bass.ds(i + (COL["b_in"] + K1 // P), 1)]
                        dve.tensor_scalar(k_t[:], ps[1][:], kb, None, ALU.add)
                        dve.tensor_scalar(kc_t[:], ps[2][:, 0:CTX], kb, None, ALU.add).then_inc(evicted2.sem, 1)
                        dve.wait_ge(transposed.sem, transposed.at(2, i, 3))
                        dve.tensor_copy(v_odd[:], ps[2][:, 0:(TT - 1) * P].rearrange("p (t c) -> p t c", c=P))
                        dve.wait_ge(transposed.sem, transposed.at(3, i, 3))
                        dve.tensor_copy(v_ctx[:], ps[0][:, 0:CTX].rearrange("p (t c) -> p t c", c=P))\
                           .then_inc(aux3.sem, 1)
                        dve.wait_ge(aux2.sem, aux2.at(1, i, 1))

                        def bias_scores(r):
                            b = r % 2
                            dr = row_start(r) - r + WIN_H - 1
                            dve.wait_ge(scores.sem, scores.at(r + 1, i, ROWS))
                            dve.wait_ge(pt_ready.sem, pt_ready.at(r - 1, i, ROWS))
                            dve_steps.done(dve.reduce_max(stat[:, b, 1:2], ps[b][:, HALF:HALF + CTX], AX))
                            dve_steps.done(dve.tensor_tensor_reduce(
                                prob[:, b, 0:KEYS], ps[b][:, 0:KEYS], bias[:, dr:dr + WIN_H].rearrange("p r c -> p (r c)"),
                                1.0, -3e38, ALU.add, ALU.max, stat[:, b, 0:1]))
                            dve_steps.wait(dve)
                            dve.scalar_tensor_tensor(out=stat[:, b, 2:3], in0=stat[:, b, 0:1], scalar=stat[:, b, 1:2],
                                                     in1=minus[:], op0=ALU.max, op1=ALU.mult).then_inc(biased.sem, 1)

                        def normalise(r):
                            b = r % 2
                            dve.wait_ge(exped.sem, exped.at(r + 1, i, ROWS))
                            dve_steps.done(dve.tensor_tensor(stat[:, b, 5:6], stat[:, b, 3:4], stat[:, b, 4:5], ALU.add))
                            dve_steps.wait(dve)
                            dve_steps.done(dve.reciprocal(stat[:, b, 6:7], stat[:, b, 5:6]))
                            dve_steps.wait(dve)
                            dve.tensor_scalar(prob[:, b], prob[:, b], stat[:, b, 6:7], None, ALU.mult).then_inc(probs.sem, 1)

                        def evict_o(g):
                            dve.wait_ge(o_ready.sem, o_ready.at(4 * g + 4, i, ROWS))
                            if g == 0:
                                dve.wait_ge(mod_ready.sem, mod_ready.at(1, i, 1))
                            o = ps[3][:, (g % 2) * HALF:(g % 2) * HALF + HALF].rearrange("p (r c) -> p r c", c=P)
                            for half in range(2):
                                p0 = half * 64
                                cols = slice(g * 256, g * 256 + 256)
                                last = dve.tensor_tensor(
                                    y32[p0:p0 + 64, cols].rearrange("p (r c) -> p r c", c=64), o[p0:p0 + 64, :, p0:p0 + 64][:, :, ::-1],
                                    z_silu[p0:p0 + 64, cols].rearrange("p (r c) -> p r c", c=64), ALU.mult)
                            last.then_inc(o_evicted.sem, 1)

                        dve_steps.open(i, 4 * ROWS)
                        bias_scores(0)
                        for r in range(ROWS):
                            if r + 1 < ROWS:
                                bias_scores(r + 1)
                            normalise(r)
                            if r >= 5 and (r - 5) % 4 == 0:
                                evict_o((r - 5) // 4)
                        evict_o(3)

                @block.tensor
                def _(pe):
                    with pe.Fori(0, N) as i:
                        def ctx_part(dst, s):
                            return [(dst, lambda k: hc_hi[:, k], lambda k: hc_lo[:, k])]

                        split_ready(pe, 0, i, 4)
                        product(pe, (0, i, 4), wide(ps[0])).then_inc(used.sem, 1)
                        split_ready(pe, 1, i, 4)
                        product(pe, (1, i, 4), wide(ps[1]) + ctx_part(ps[2][:, 0:CTX], 1)).then_inc(used.sem, 1)
                        split_ready(pe, 2, i, 4)
                        pe.wait_ge(evicted.sem, evicted.at(1, i, 1))
                        product(pe, (2, i, 4), wide(ps[0]) + ctx_part(ps[2][:, HALF:HALF + CTX], 0)).then_inc(used.sem, 1)
                        split_ready(pe, 3, i, 4)
                        pe.wait_ge(evicted2.sem, evicted2.at(1, i, 1))
                        product(pe, (3, i, 4), wide(ps[1])).then_inc(used.sem, 1)
                        pe.wait_ge(h_ready.sem, h_ready.at(1, i, 1))
                        pe.wait_ge(o_evicted.sem, o_evicted.at(0, i, 4))
                        for t in range(TT):
                            last = pe.transpose(ps[3][:, t * P:t * P + P], v_t[:, t * P:t * P + P], ident[:])
                        last.then_inc(transposed.sem, 1)
                        for t in range(TT - 1):
                            last = pe.transpose(ps[2][:, t * P:t * P + P], v_t[:, t * P + 64:t * P + 64 + P], ident[:])
                        last.then_inc(transposed.sem, 1)
                        for t in range(CTX // P):
                            last = pe.transpose(ps[0][:, t * P:t * P + P], vc_t[:, t * P:t * P + P], ident[:])
                        last.then_inc(transposed.sem, 1)

                        def score(r):
                            if r >= 2:
                                pe.wait_ge(exped.sem, exped.at(r - 1, i, ROWS))
                            first = row_start(r) * GRID
                            pe.matmul(ps[r % 2][:, 0:KEYS], q_blk[:, r], k_t[:, first:first + KEYS], start=True, stop=True)
                            pe.matmul(ps[r % 2][:, HALF:HALF + CTX], q_blk[:, r], kc_t[:], start=True, stop=True)\
                              .then_inc(scores.sem, 1)

                        def turn(r):
                            pe.wait_ge(probs.sem, probs.at(r + 1, i, ROWS))
                            pe.wait_ge(pt_evicted.sem, pt_evicted.at(r, i, ROWS))
                            for j in range(ALL // P):
                                last = pe.transpose(ps[2][:, j * P:j * P + P], prob[:, r % 2, j * P:j * P + P], ident[:])
                            last.then_inc(pt_ready.sem, 1)

                        def weigh(r):
                            pe.wait_ge(pt_evicted.sem, pt_evicted.at(r + 1, i, ROWS))
                            if r % 4 == 0 and r >= 8:
                                pe.wait_ge(o_evicted.sem, o_evicted.at(r // 4 - 1, i, 4))
                            at = (r // 4 % 2) * HALF + r % 4 * P
                            for j, v in enumerate(value_tiles(r)):
                                last = pe.matmul(ps[3][:, at:at + P], v, prob_t[:, r % 2, j], start=(j == 0), stop=(j == 5))
                            last.then_inc(o_ready.sem, 1)

                        pe.wait_ge(aux3.sem, aux3.at(1, i, 1))
                        pe.wait_ge(mod_ready.sem, mod_ready.at(1, i, 1))
                        pe.wait_ge(tr_evicted.sem, tr_evicted.at(1, i, 1))
                        score(0)
                        score(1)
                        for r in range(ROWS):
                            if r + 2 < ROWS:
                                score(r + 2)
                            if r >= 1:
                                weigh(r - 1)
                            turn(r)
                        weigh(ROWS - 1)

            dve_steps.close(N)
            side_loaded.passed(9)
            for s, n in ((aux, 2), (evicted, N), (evicted2, N), (h_ready, N), (mod_ready, N), (transposed, 3 * N),
                         (tr_evicted, N), (aux2, N), (aux3, N), (scores, ROWS * N), (biased, ROWS * N), (exped, ROWS * N),
                         (probs, ROWS * N), (pt_ready, ROWS * N), (pt_evicted, ROWS * N), (o_ready, ROWS * N),
                         (o_evicted, 4 * N), (y_hi, N), (y_ready, N)):
                s.passed(n)
            chunk_passed(N * 4)

        def chunk_passed(n):
            chunks[0] += n

        def merged_tile(i, j):
            return i * -2 + (KT - 2 + j)

        def merge_source(branches):
            def source(i, m):
                gate_w, gate_col, _, branch_w, _, _, _ = branches[m // 2 % len(branches)]
                first = (KT - 2 + m // 2 // len(branches)) * P
                return (chunk_of(gate_w, i * (-2 * P) + (first + gate_col)) if m % 2 == 0 else
                        chunk_of(branch_w, i * (-2 * P) + first))
            return source

        def merge(acc, branches, accumulate, following, beside=None, early=None, residual_gate=None):
            units = [(tile, b) for tile in range(2) for b in range(len(branches))]
            N, U = KT // 2, len(units)
            per = 2 * U
            with ExitStack() as sc, nc.Block() as block:
                sig = sb(sc, "sig", [P, 2, T])
                part = sb(sc, "part", [P, T])

                def tiles(m):
                    return KT if m % 2 == 0 else units_k(m // 2 % U)

                def units_k(u):
                    return branches[units[u][1]][4]

                adds = [(u, b) for u, (_, b) in enumerate(units) if b > 0 or accumulate]

                @block.sync
                def _(sp):
                    if early:
                        early(sp)
                    if residual_gate is not None:
                        for k in range(KT):
                            sp.dma_start(residual_gate[:, k], ada[:, k, 2 * D:]).then_inc(side_loaded.sem, 16)
                    stream(sp, N, per, merge_source(branches), following)

                @block.gpsimd
                def _(pool):
                    with pool.Fori(0, N) as i:
                        for u, (tile, b) in enumerate(units):
                            for m in (2 * u, 2 * u + 1):
                                rest_chunk(pool, m + 1, i, per, tiles(m + 1))
                            if (u, b) in adds:
                                pool.wait_ge(evicted2.sem, evicted2.at(u + 1, i, U))
                                pool_carry_wait()
                                to = acc[:, bass.ds(merged_tile(i, tile), 1)].rearrange("p a t -> p (a t)")
                                pool.tensor_tensor(to, to, part[:], ALU.add).then_inc(o_evicted.sem, 1)

                @block.scalar
                def _(act):
                    with act.Fori(0, N) as i:
                        for u, (tile, b) in enumerate(units):
                            round_chunk(act, 2 * u + 1, i, per, tiles(2 * u + 1))
                            act.wait_ge(used.sem, after(used, 2 * u, i, per))
                            act.wait_ge(evicted2.sem, evicted2.at(u - 1, i, U))
                            col = branches[b][2]
                            bias = 0.0 if col is None else vec[:, bass.ds(merged_tile(i, col + tile), 1)]
                            act.activation(sig[:, u % 2], ps[2 * (u % 2)][:], ACT.Sigmoid, bias=bias).then_inc(evicted.sem, 1)
                            round_chunk(act, 2 * u + 2, i, per, tiles(2 * u + 2))

                @block.vector
                def _(dve):
                    if residual_gate is not None:
                        dve.wait_ge(side_loaded.sem, side_loaded.at(KT))
                        for k in range(KT):
                            x = residual_gate[:, k]
                            if k == 0:
                                dve.tensor_scalar(x, x, cond[:, k, 0:1], None, ALU.mult).then_inc(sq_ready.sem, 1)
                            else:
                                dve.wait_ge(sq_ready.sem, sq_ready.at(k))
                                dve.scalar_tensor_tensor(out=residual_gate[:, 0], in0=x, scalar=cond[:, k, 0:1],
                                                         in1=residual_gate[:, 0], op0=ALU.mult, op1=ALU.add).then_inc(sq_ready.sem, 1)
                    with dve.Fori(0, N) as i:
                        for u, (tile, b) in enumerate(units):
                            if beside:
                                beside(dve, i, u, 0)
                            dve.wait_ge(evicted.sem, evicted.at(u + 1, i, U))
                            dve.wait_ge(used.sem, after(used, 2 * u + 1, i, per))
                            if (u, b) not in adds:
                                to = acc[:, bass.ds(merged_tile(i, tile), 1)].rearrange("p a t -> p (a t)")
                                dve.tensor_tensor(to, sig[:, u % 2], ps[2 * (u % 2) + 1][:], ALU.mult).then_inc(evicted2.sem, 1)
                            else:
                                dve.wait_ge(o_evicted.sem, o_evicted.at(adds.index((u, b)), i, len(adds)))
                                dve.tensor_tensor(part[:], sig[:, u % 2], ps[2 * (u % 2) + 1][:], ALU.mult)\
                                   .then_inc(evicted2.sem, 1)
                            if beside:
                                beside(dve, i, u, 1)

                    if residual_gate is not None:
                        dve.wait_ge(sum_ready.sem, sum_ready.at(1))
                        dve.tensor_tensor(gate_t[:], ps[0][:, 0:KT], column("b_ada", 2 * KT, KT), ALU.add)

                @block.tensor
                def _(pe):
                    with pe.Fori(0, N) as i:
                        for u, (tile, b) in enumerate(units):
                            split_ready(pe, 2 * u, i, per)
                            pe.wait_ge(evicted.sem, evicted.at(u - 1, i, U))
                            product(pe, (2 * u, i, per), wide(ps[2 * (u % 2)])).then_inc(used.sem, 1)
                            split_ready(pe, 2 * u + 1, i, per)
                            pe.wait_ge(evicted2.sem, evicted2.at(u - 1, i, U))
                            product(pe, (2 * u + 1, i, per), halves(ps[2 * (u % 2) + 1], branches[b][5], branches[b][6]),
                                    branches[b][4]).then_inc(used.sem, 1)
                    if residual_gate is not None:
                        pe.wait_ge(sq_ready.sem, sq_ready.at(KT))
                        pe.wait_ge(evicted.sem, evicted.at(U * N - 1))
                        for d in range(KT):
                            last = pe.matmul(ps[0][:, d:d + 1], residual_gate[:, 0, d * P:d * P + P], ones[:, 0:1],
                                             start=True, stop=True)
                        last.then_inc(sum_ready.sem, 1)

            for s in (evicted, evicted2):
                s.passed(U * N)
            o_evicted.passed(len(adds) * N)
            if residual_gate is not None:
                side_loaded.passed(KT)
                sum_ready.passed(1)
                sq_ready.passed(KT)
            chunk_passed(per * N)

        def conv_source(i, m):
            return chunk_of(w_in, (A_X, A_C, A_B, A_Z)[m] + i * P)

        def convolution(y_hi_t, y_lo_t, following):
            N = WB // P
            b_in = COL["b_in"]
            with ExitStack() as sc, nc.Block() as block:
                ax = sb(sc, "ax", [P, T])
                u = sb(sc, "u", [P, T + 2])
                z = sb(sc, "z", [P, T])
                y = sb(sc, "y", [P, T])

                @block.sync
                def _(sp):
                    stream(sp, N, 4, conv_source, following)

                @block.gpsimd
                def _(pool):
                    pool.memset(u[:], 0.0).then_inc(aux.sem, 1)
                    with pool.Fori(0, N) as i:
                        for m in range(4):
                            rest_chunk(pool, m + 1, i, 4)
                        pool.wait_ge(y_hi.sem, y_hi.at(1, i, 1))
                        pool.tensor_tensor(y_lo_t[:, bass.ds(i, 1)], y[:].rearrange("p (a t) -> p a t", a=1),
                                           y_hi_t[:, bass.ds(i, 1)].bitcast(F32), ALU.subtract).then_inc(y_ready.sem, 1)

                @block.scalar
                def _(act):
                    with act.Fori(0, N) as i:
                        round_chunk(act, 1, i, 4)
                        act.wait_ge(used.sem, after(used, 0, i, 4))
                        act.wait_ge(evicted2.sem, evicted2.at(0, i, 2))
                        act.activation(ax[:], ps[0][:], ACT.Identity, bias=vec[:, bass.ds(i + (b_in + A_X // P), 1)])\
                           .then_inc(evicted.sem, 1)
                        round_chunk(act, 2, i, 4)
                        round_chunk(act, 3, i, 4)
                        round_chunk(act, 4, i, 4)
                        act.wait_ge(used.sem, after(used, 3, i, 4))
                        act.wait_ge(h_ready.sem, h_ready.at(0, i, 1))
                        act.activation(z[:], ps[3][:], ACT.Silu, bias=vec[:, bass.ds(i + (b_in + A_Z // P), 1)])\
                           .then_inc(evicted.sem, 1)
                        act.wait_ge(h_ready.sem, h_ready.at(1, i, 1))
                        act.activation(y_hi_t[:, bass.ds(i, 1)], y[:].rearrange("p (a t) -> p a t", a=1), ACT.Copy)\
                           .then_inc(y_hi.sem, 1)

                @block.vector
                def _(dve):
                    dve.wait_ge(aux.sem, aux.at(1))
                    with dve.Fori(0, N) as i:
                        dve_steps.open(i, 4)
                        dve.wait_ge(evicted.sem, evicted.at(1, i, 2))
                        dve.wait_ge(used.sem, after(used, 1, i, 4))
                        dve.scalar_tensor_tensor(out=u[:, 1:T + 1], in0=ps[1][:], scalar=vec[:, bass.ds(i + (b_in + A_C // P), 1)],
                                                 in1=ax[:], op0=ALU.add, op1=ALU.mult).then_inc(evicted2.sem, 1)
                        dve.wait_ge(evicted2.sem, evicted2.at(1, i, 2))
                        dve.wait_ge(y_ready.sem, y_ready.at(0, i, 1))
                        dve_steps.done(dve.tensor_scalar(y[:], u[:, 0:T], vec[:, bass.ds(i + COL["w_conv"], 1)],
                                                         vec[:, bass.ds(i + COL["b_conv"], 1)], ALU.mult, ALU.add))
                        for tap in (1, 2):
                            dve_steps.wait(dve)
                            dve_steps.done(dve.scalar_tensor_tensor(
                                out=y[:], in0=u[:, tap:tap + T], scalar=vec[:, bass.ds(i + (COL["w_conv"] + 4 * tap), 1)],
                                in1=y[:], op0=ALU.mult, op1=ALU.add))
                        dve_steps.wait(dve)
                        dve.wait_ge(used.sem, after(used, 2, i, 4))
                        dve_steps.done(dve.scalar_tensor_tensor(
                            out=y[:], in0=ps[2][:], scalar=vec[:, bass.ds(i + (b_in + A_B // P), 1)], in1=y[:],
                            op0=ALU.add, op1=ALU.mult))
                        dve_steps.wait(dve)
                        dve.wait_ge(evicted.sem, evicted.at(2, i, 2))
                        dve.tensor_tensor(y[:], y[:], z[:], ALU.mult).then_inc(h_ready.sem, 1)
                        dve.wait_ge(h_ready.sem, h_ready.at(1, i, 1))
                        carry_wait(0).then_inc(evicted2.sem, 1)

                @block.tensor
                def _(pe):
                    with pe.Fori(0, N) as i:
                        for m in range(4):
                            split_ready(pe, m, i, 4)
                            if m == 0:
                                pe.wait_ge(evicted.sem, evicted.at(0, i, 2))
                            else:
                                pe.wait_ge(h_ready.sem, h_ready.at(0, i, 1))
                            product(pe, (m, i, 4), wide(ps[m])).then_inc(used.sem, 1)

            dve_steps.close(N)
            for s, n in ((aux, 1), (evicted, 2 * N), (evicted2, 2 * N), (h_ready, N), (y_hi, N), (y_ready, N)):
                s.passed(n)
            chunk_passed(4 * N)

        def fourier_source(i, m):
            return chunk_of(w_in, (F_U, F_Z)[m] + i * P)

        def fourier(y_hi_t, y_lo_t, following):
            N = WB // P
            HT = HALF // P
            b_in = COL["b_in"]
            with ExitStack() as sc, nc.Block() as block:
                cos_t = sb(sc, "cos_t", [P, HT, HALF + 1])
                sin_t = sb(sc, "sin_t", [P, HT, HALF + 1])
                alt = sb(sc, "alt", [1, HALF + 1])
                chan = sb(sc, "chan", [P, 2, P])
                f = sb(sc, "f", [P, T])
                y = f
                even = sb(sc, "even", [P, HALF])
                odd = sb(sc, "odd", [P, HALF])
                parts = sb(sc, "parts", [P, 2 * HT, P])
                mid = sb(sc, "mid", [1, P])
                zc = sb(sc, "zc", [P, HALF + 1])
                zs = sb(sc, "zs", [P, HALF])
                big_a = sb(sc, "big_a", [P, HALF + 1])
                z = sb(sc, "z", [P, T])

                @block.sync
                def _(sp):
                    sp.dma_start(cos_t[:], a["k_cos"].rearrange("(t p) k -> p t k", p=P)).then_inc(side_loaded.sem, 16)
                    sp.dma_start(sin_t[:], a["k_sin"].rearrange("(t p) k -> p t k", p=P)).then_inc(side_loaded.sem, 16)
                    sp.dma_start(alt[:], a["k_alt"]).then_inc(side_loaded.sem, 16)
                    sp.dma_start(chan[:], a["k_chan"]).then_inc(side_loaded.sem, 16)
                    stream(sp, N, 2, fourier_source, following)

                @block.gpsimd
                def _(pool):
                    pool.memset(odd[:], 0.0).then_inc(aux.sem, 1)
                    with pool.Fori(0, N) as i:
                        for m in range(2):
                            rest_chunk(pool, m + 1, i, 2)
                        pool.wait_ge(y_hi.sem, y_hi.at(1, i, 1))
                        pool.tensor_tensor(y_lo_t[:, bass.ds(i, 1)], y[:].rearrange("p (a t) -> p a t", a=1),
                                           y_hi_t[:, bass.ds(i, 1)].bitcast(F32), ALU.subtract).then_inc(y_ready.sem, 1)

                @block.scalar
                def _(act):
                    with act.Fori(0, N) as i:
                        round_chunk(act, 1, i, 2)
                        act.wait_ge(used.sem, after(used, 0, i, 2))
                        act.wait_ge(y_ready.sem, y_ready.at(0, i, 1))
                        act.activation(f[:], ps[0][:], ACT.Identity, bias=vec[:, bass.ds(i + (b_in + F_U // P), 1)])\
                           .then_inc(evicted.sem, 1)
                        round_chunk(act, 2, i, 2)
                        act.wait_ge(transposed.sem, transposed.at(1, i, 1))
                        act.activation(parts[:], ps[2][:].rearrange("p (t c) -> p t c", c=P), ACT.Copy).then_inc(tr_evicted.sem, 1)
                        act.wait_ge(scores.sem, scores.at(1, i, 2))
                        act.activation(zc[:, 0:HALF], ps[2][:, 0:HALF], ACT.Copy)
                        act.activation(zc[:, HALF:HALF + 1], ps[3][:, HALF:HALF + 1], ACT.Copy).then_inc(exped.sem, 1)
                        act.wait_ge(used.sem, after(used, 1, i, 2))
                        act.wait_ge(h_ready.sem, h_ready.at(0, i, 1))
                        act.activation(z[:], ps[1][:], ACT.Silu, bias=vec[:, bass.ds(i + (b_in + F_Z // P), 1)])\
                           .then_inc(evicted2.sem, 1)
                        act.wait_ge(scores.sem, scores.at(2, i, 2))
                        act.activation(big_a[:, 0:HALF], ps[2][:, 0:HALF], ACT.Copy)
                        act.activation(big_a[:, HALF:HALF + 1], ps[3][:, HALF:HALF + 1], ACT.Copy).then_inc(exped.sem, 1)
                        act.wait_ge(h_ready.sem, h_ready.at(1, i, 1))
                        act.activation(y_hi_t[:, bass.ds(i, 1)], y[:].rearrange("p (a t) -> p a t", a=1), ACT.Copy)\
                           .then_inc(y_hi.sem, 1)

                @block.vector
                def _(dve):
                    dve.wait_ge(aux.sem, aux.at(1))
                    with dve.Fori(0, N) as i:
                        dve_steps.open(i, 3)
                        dve.wait_ge(evicted.sem, evicted.at(1, i, 1))
                        mirror = f[:, T - 1:HALF:-1]
                        dve.tensor_tensor(even[:, 1:HALF], f[:, 1:HALF], mirror, ALU.add)
                        dve.tensor_tensor(odd[:, 1:HALF], f[:, 1:HALF], mirror, ALU.subtract)
                        dve.tensor_copy(even[:, 0:1], f[:, 0:1]).then_inc(aux2.sem, 1)
                        dve.wait_ge(transposed.sem, transposed.at(1, i, 1))
                        dve.tensor_copy(mid[:], ps[3][0:1, 0:P]).then_inc(aux3.sem, 1)
                        dve.wait_ge(scores.sem, scores.at(1, i, 2))
                        dve.tensor_copy(zs[:], ps[2][:, HALF:2 * HALF]).then_inc(biased.sem, 1)
                        dve.wait_ge(exped.sem, exped.at(2, i, 2))
                        back = y[:, T - 1:HALF:-1]
                        dve.tensor_tensor(y[:, 0:HALF], big_a[:, 0:HALF], ps[2][:, HALF:2 * HALF], ALU.subtract)
                        dve_steps.done(dve.tensor_tensor(back, big_a[:, 1:HALF], ps[2][:, HALF + 1:2 * HALF], ALU.add))
                        dve_steps.done(dve.tensor_copy(y[:, HALF:HALF + 1], big_a[:, HALF:HALF + 1]))
                        dve_steps.wait(dve)
                        dve.wait_ge(evicted2.sem, evicted2.at(1, i, 1))
                        dve.tensor_tensor(y[:], y[:], z[:], ALU.mult).then_inc(h_ready.sem, 1)
                        dve.wait_ge(h_ready.sem, h_ready.at(1, i, 1))
                        dve_steps.done(carry_wait(0))

                @block.tensor
                def _(pe):
                    pe.wait_ge(side_loaded.sem, side_loaded.at(4))
                    with pe.Fori(0, N) as i:
                        split_ready(pe, 0, i, 2)
                        pe.wait_ge(evicted.sem, evicted.at(0, i, 1))
                        product(pe, (0, i, 2), wide(ps[0])).then_inc(used.sem, 1)
                        split_ready(pe, 1, i, 2)
                        pe.wait_ge(evicted2.sem, evicted2.at(0, i, 1))
                        for part in (0, 1):
                            product(pe, (1, i, 2), wide(ps[1]), part=(part, 4))
                        pe.wait_ge(aux2.sem, aux2.at(1, i, 1))
                        pe.wait_ge(h_ready.sem, h_ready.at(0, i, 1))
                        for n, src in enumerate((even, odd)):
                            for t in range(HT):
                                pe.transpose(ps[2][:, (n * HT + t) * P:(n * HT + t + 1) * P], src[:, t * P:t * P + P], ident[:])
                        pe.transpose(ps[3][0:1, 0:P], f[:, HALF:HALF + 1], ident[:]).then_inc(transposed.sem, 1)
                        product(pe, (1, i, 2), wide(ps[1]), part=(2, 4))
                        pe.wait_ge(tr_evicted.sem, tr_evicted.at(1, i, 1))
                        pe.wait_ge(aux3.sem, aux3.at(1, i, 1))
                        for dst, c0, c1 in ((ps[2][:, 0:HALF], 0, HALF), (ps[3][:, HALF:HALF + 1], HALF, HALF + 1)):
                            for t in range(HT):
                                pe.matmul(dst, parts[:, t], cos_t[:, t, c0:c1], start=(t == 0), stop=False)
                            pe.matmul(dst, mid[:], alt[:, c0:c1], start=False, stop=True)
                        for t in range(HT):
                            last = pe.matmul(ps[2][:, HALF:2 * HALF], parts[:, HT + t], sin_t[:, t, 0:HALF],
                                             start=(t == 0), stop=(t == HT - 1))
                        last.then_inc(scores.sem, 1)
                        product(pe, (1, i, 2), wide(ps[1]), part=(3, 4)).then_inc(used.sem, 1)
                        pe.wait_ge(exped.sem, exped.at(1, i, 2))
                        pe.wait_ge(biased.sem, biased.at(1, i, 1))
                        pe.matmul(ps[2][:, 0:HALF], chan[:, 0], zc[:, 0:HALF], start=True, stop=True)
                        pe.matmul(ps[3][:, HALF:HALF + 1], chan[:, 0], zc[:, HALF:HALF + 1], start=True, stop=True)
                        pe.matmul(ps[2][:, HALF:2 * HALF], chan[:, 1], zs[:], start=True, stop=True).then_inc(scores.sem, 1)

            dve_steps.close(N)
            side_loaded.passed(4)
            for s, n in ((aux, 1), (aux2, N), (aux3, N), (evicted, N), (evicted2, N), (transposed, N), (tr_evicted, N),
                         (scores, 2 * N), (exped, 2 * N), (biased, N), (h_ready, N), (y_hi, N), (y_ready, N)):
                s.passed(n)
            chunk_passed(2 * N)

        def project_source(w):
            return lambda i, m: chunk_of(w, m * P)

        def project(w, acc, res, first, gains, following, kept=None):
            with ExitStack() as sc, nc.Block() as block:
                xs = sb(sc, "xs", [P, 4, T])
                sq = xs[:, 2:4]
                ssq = sb(sc, "ssq", [P, T])
                inv = sb(sc, "inv", [P, T])

                def add_residual(engine, m):
                    engine.tensor_tensor(res[:, m], res[:, m], acc[:, m], ALU.add).then_inc((y_ready, y_ready2)[m % 2].sem, 1)

                def subtract(engine, m):
                    engine.wait_ge(hi_ready.sem, hi_ready.at(KT + m + 1))
                    engine.tensor_tensor(h_lo[:, m], xs[:, m % 4], h_hi[:, m].bitcast(F32), ALU.subtract)\
                        .then_inc((lo_ready2, lo_ready)[m % 2].sem, 1)

                def residual_ready(engine, m):
                    engine.wait_ge((y_ready, y_ready2)[m % 2].sem, (y_ready, y_ready2)[m % 2].at(m // 2 + 1))

                @block.sync
                def _(sp):
                    stream(sp, 1, KT, project_source(w), following)
                    if kept is not None:
                        for m in range(KT):
                            residual_ready(sp, m)
                            sp.dma_start(kept[:, m], res[:, m]).then_inc(stored.sem, 16)
                        sp.wait_ge(stored.sem, stored.at(KT))

                @block.gpsimd
                def _(pool):
                    for m in range(KT):
                        rest_chunk(pool, m + 1, 0, KT)
                    if not first:
                        pool.wait_ge(x_loaded.sem, x_loaded.at(1))
                        for m in range(0, KT, 2):
                            pool.wait_ge(biased.sem, biased.at(m + 1))
                            add_residual(pool, m)
                    for m in range(0, KT, 2):
                        subtract(pool, m)

                @block.scalar
                def _(act):
                    for k in range(KT):
                        act.activation(h_hi[:, k], acc[:, k], ACT.Copy).then_inc(hi_ready.sem, 1)
                        if k == 0:
                            round_chunk(act, 1, 0, KT)
                    def square(m):
                        act.wait_ge(evicted.sem, evicted.at(m + 1))
                        act.wait_ge(sum_ready.sem, sum_ready.at(m - 1))
                        act.activation(sq[:, m % 2], acc[:, m], ACT.Square).then_inc(sq_ready.sem, 1)

                    for m in range(KT):
                        if first:
                            act.wait_ge(transposed.sem, transposed.at(m + 1))
                            act.wait_ge(evicted.sem, evicted.at(m - 1))
                            act.activation(xs[:, m % 2], ps[2 + m % 2][:], ACT.Copy).then_inc(tr_evicted.sem, 1)
                        if m >= 1:
                            round_chunk(act, m + 1, 0, KT)
                            square(m - 1)
                    square(KT - 1)
                    act.wait_ge(stat_ready.sem, stat_ready.at(1))
                    act.activation(inv[:], inv[:], ACT.Sqrt).then_inc(norm_ready.sem, 1)
                    for m in range(KT):
                        residual_ready(act, m)
                        act.wait_ge(scores.sem, scores.at(1 + m - 1))
                        act.activation(sq[:, m % 2], res[:, m], ACT.Square).then_inc(sq_ready.sem, 1)
                    act.wait_ge(stat_ready.sem, stat_ready.at(2))
                    act.activation(inv[:], inv[:], ACT.Sqrt).then_inc(norm_ready.sem, 1)
                    for m in range(KT):
                        act.wait_ge(h_ready.sem, h_ready.at(m + 1))
                        act.activation(h_hi[:, m], xs[:, m % 4], ACT.Copy).then_inc(hi_ready.sem, 1)

                @block.vector
                def _(dve):
                    for k in range(KT):
                        dve.wait_ge(hi_ready.sem, hi_ready.at(k + 1))
                        dve.tensor_tensor(h_lo[:, k], acc[:, k], h_hi[:, k].bitcast(F32), ALU.subtract).then_inc(lo_ready.sem, 1)

                    def add_square(m):
                        dve.wait_ge(sq_ready.sem, sq_ready.at(m + 1))
                        if m == 0:
                            dve.tensor_copy(ssq[:], sq[:, 0]).then_inc(sum_ready.sem, 1)
                        else:
                            dve.wait_ge(sum_ready.sem, sum_ready.at(m))
                            dve.tensor_tensor(ssq[:], ssq[:], sq[:, m % 2], ALU.add).then_inc(sum_ready.sem, 1)

                    for m in range(KT):
                        dve.wait_ge(used.sem, after(used, m, 0, KT))
                        if first:
                            dve.wait_ge(tr_evicted.sem, tr_evicted.at(m + 1))
                            dve.scalar_tensor_tensor(out=acc[:, m], in0=ps[m % 2][:], scalar=gate_t[:, m:m + 1],
                                                     in1=xs[:, m % 2], op0=ALU.mult, op1=ALU.add).then_inc(evicted.sem, 1)
                        else:
                            dve.tensor_copy(acc[:, m], ps[m % 2][:]).then_inc(evicted.sem, 1)
                        if m >= 1:
                            add_square(m - 1)
                    add_square(KT - 1)

                    def inverse_rms(n, bank):
                        dve.wait_ge(scores.sem, scores.at((1, 1 + KT)[n]))
                        dve.tensor_scalar(inv[:], bank[:], 1.0 / D, EPS, ALU.mult, ALU.add).then_inc(stat_ready.sem, 1)
                        dve.wait_ge(norm_ready.sem, norm_ready.at(n + 1))
                        dve_steps.done(dve.reciprocal(inv[:], inv[:]))
                        dve_steps.wait(dve)

                    inverse_rms(0, ps[2])
                    if not first:
                        dve.wait_ge(x_loaded.sem, x_loaded.at(1))
                    for m in range(KT):
                        if first:
                            dve.scalar_tensor_tensor(out=res[:, m], in0=acc[:, m], scalar=column(gains[0], m), in1=inv[:],
                                                     op0=ALU.mult, op1=ALU.mult).then_inc((y_ready, y_ready2)[m % 2].sem, 1)
                        else:
                            dve.scalar_tensor_tensor(out=acc[:, m], in0=acc[:, m], scalar=column(gains[0], m), in1=inv[:],
                                                     op0=ALU.mult, op1=ALU.mult).then_inc(biased.sem, 1)
                            if m % 2:
                                dve.wait_ge(biased.sem, biased.at(m + 1))
                                add_residual(dve, m)
                    if not first:
                        residual_ready(dve, KT - 2)
                    inverse_rms(1, ps[3])
                    for m in range(KT):
                        if m >= 4:
                            half, n = (lo_ready2, m // 2 - 1) if m % 2 == 0 else (lo_ready, KT + m // 2 - 1)
                            dve.wait_ge(half.sem, half.at(n))
                        dve.scalar_tensor_tensor(out=xs[:, m % 4], in0=res[:, m], scalar=column(gains[1], m), in1=inv[:],
                                                 op0=ALU.mult, op1=ALU.mult).then_inc(h_ready.sem, 1)
                        if m >= 2 and m % 2 == 0:
                            subtract(dve, m - 1)
                    subtract(dve, KT - 1)

                @block.tensor
                def _(pe):
                    if first:
                        pe.wait_ge(x_loaded.sem, x_loaded.at(1))
                    for m in range(KT):
                        if first:
                            pe.wait_ge(tr_evicted.sem, tr_evicted.at(m - 1))
                            for t in range(TT):
                                last = pe.transpose(ps[2 + m % 2][:, t * P:t * P + P], res[:, t, m * P:m * P + P], ident[:])
                            last.then_inc(transposed.sem, 1)
                        split_ready(pe, m, 0, KT)
                        pe.wait_ge(evicted.sem, evicted.at(m - 1))
                        arrived = (lambda k: pe.wait_ge(lo_ready.sem, lo_ready.at(k + 1))) if m == 0 else None
                        product(pe, (m, 0, KT), wide(ps[m % 2]), KT, arrived).then_inc(used.sem, 1)
                    pe.wait_ge(sum_ready.sem, sum_ready.at(KT))
                    if first:
                        pe.wait_ge(tr_evicted.sem, tr_evicted.at(KT))
                    for c in (0, HALF):
                        last = pe.matmul(ps[2][:, c:c + HALF], ones[:], ssq[:, c:c + HALF], start=True, stop=True)
                    last.then_inc(scores.sem, 1)
                    for m in range(KT):
                        pe.wait_ge(sq_ready.sem, sq_ready.at(KT + m + 1))
                        for c in (0, HALF):
                            last = pe.matmul(ps[3][:, c:c + HALF], ones[:], sq[:, m % 2, c:c + HALF],
                                             start=(m == 0), stop=(m == KT - 1))
                        last.then_inc(scores.sem, 1)

            dve_steps.close()
            x_loaded.passed(1)
            if not first:
                biased.passed(KT)
            if first:
                transposed.passed(KT)
                tr_evicted.passed(KT)
            if kept is not None:
                stored.passed(KT)
            for s, n in ((hi_ready, 2 * KT), (lo_ready, KT + KT // 2), (lo_ready2, KT // 2), (evicted, KT), (sq_ready, 2 * KT), (sum_ready, KT),
                         (stat_ready, 2), (norm_ready, 2), (y_ready, KT // 2), (y_ready2, KT // 2), (scores, 1 + KT), (h_ready, KT)):
                s.passed(n)
            chunk_passed(KT)

        def hgrn_source(i, m):
            return (chunk_of(w_in2, (H_Q, H_F)[m % 2] + i * 2 * P + m // 2 * P) if m < 4 else
                    chunk_of(w_in2, (H_I, H_G)[m - 4] + i * P))

        def hgrn(y_hi_t, y_lo_t, following):
            N, NC, LEVELS = 2, T // CHUNK, 8
            SMALL = 2.0 ** -60
            with ExitStack() as sc, nc.Block() as block:
                masks = sb(sc, "masks", [P, LEVELS, CHUNK])
                blocks = sb(sc, "blocks", [P, P])
                reset = sb(sc, "reset", [P, T])
                q = sb(sc, "q", [P, 2, T])
                k = sb(sc, "k", [P, 2, T])
                b = sb(sc, "b", [P, 2, T])
                f = sb(sc, "f", [P, T])
                o_t = sb(sc, "o_t", [P, T])
                tiny = o_t
                e = sb(sc, "e", [P, 2, T])
                qe = sb(sc, "qe", [P, 2, T])
                ke = sb(sc, "ke", [P, 2, T])
                att = sb(sc, "att", [P, 2, NC, CHUNK])
                qx = sb(sc, "qx", [P, 2, T])
                kd = sb(sc, "kd", [P, 2, T])
                e_last = sb(sc, "e_last", [P, 2, NC])
                v_t = sb(sc, "v_t", [P, T])
                v_tok = sb(sc, "v_tok", [P, NC, P])
                g_silu = sb(sc, "g_silu", [P, T])
                kd_tok = ke[:, 0].rearrange("p (c t) -> p c t", t=CHUNK)
                state = qe[:, 0].rearrange("p (h c v) -> p h c v", h=2, v=64)

                def chunked(x):
                    return x.rearrange("p (c t) -> p c t", t=CHUNK)

                @block.sync
                def _(sp):
                    sp.dma_start(masks[:], a["k_levels"]).then_inc(side_loaded.sem, 16)
                    sp.dma_start(blocks[:], a["k_blocks"]).then_inc(side_loaded.sem, 16)
                    stream(sp, N, 6, hgrn_source, following)

                @block.gpsimd
                def _(pool):
                    pool.memset(reset[:], 1.0).then_inc(aux.sem, 1)
                    pool.wait_ge(aux.sem, aux.at(1))
                    pool.memset(chunked(reset[:])[:, :, 0:1], 0.0).then_inc(aux.sem, 1)
                    with pool.Fori(0, N) as i:
                        def decayed_keys(h):
                            pool.wait_ge(probs.sem, probs.at(h + 1, i, 2))
                            pool.tensor_tensor(kd[:, h], k[:, h], tiny[:], ALU.mult).then_inc(aux3.sem, 1)

                        for m in range(1, 5):
                            rest_chunk(pool, m, i, 6)
                        decayed_keys(0)
                        for h in range(2):
                            for n in range(7):
                                if h == 0 and n == 0:
                                    pool.wait_ge(o_ready.sem, o_ready.at(0, i, 1))
                                pool.wait_ge(exped.sem, exped.at(7 * h + n + 1, i, 14))
                                pool.wait_ge(scores.sem, scores.at(8 * h + n, i, 16))
                                pool.tensor_tensor(ke[:, n % 2], k[:, h], e[:, n % 2], ALU.mult).then_inc(y_ready.sem, 1)
                                if h == 0 and n == 0:
                                    rest_chunk(pool, 5, i, 6)
                                if h == 0 and n == 4:
                                    decayed_keys(1)
                                    rest_chunk(pool, 6, i, 6)
                        pool.wait_ge(y_hi.sem, y_hi.at(1, i, 1))
                        pool.tensor_tensor(y_lo_t[:, bass.ds(i, 1)], o_t[:].rearrange("p (a t) -> p a t", a=1),
                                           y_hi_t[:, bass.ds(i, 1)].bitcast(F32), ALU.subtract).then_inc(lo_ready.sem, 1)

                @block.scalar
                def _(act):
                    with act.Fori(0, N) as i:
                        def evict_q(h):
                            act.wait_ge(used.sem, after(used, 2 * h, i, 6))
                            act.wait_ge(evicted2.sem, evicted2.at(0, i, 16))
                            act.activation(q[:, h], ps[0][:], ACT.Silu).then_inc(evicted.sem, 1)

                        def evict_gates(h):
                            act.wait_ge(used.sem, after(used, 2 * h + 1, i, 6))
                            act.wait_ge(y_ready.sem, y_ready.at(0, i, 14))
                            act.wait_ge(o_evicted.sem, o_evicted.at(h, i, 2))
                            act.wait_ge(aux3.sem, aux3.at(h, i, 2))
                            act.wait_ge(lo_ready.sem, lo_ready.at(0, i, 1))
                            act.activation(k[:, h], ps[1][:], ACT.Sigmoid, scale=-1.0)
                            act.activation(f[:], ps[1][:], ACT.Sigmoid).then_inc(evicted.sem, 1)

                        def logarithms(h):
                            act.wait_ge(h_ready.sem, h_ready.at(h + 1, i, 2))
                            act.activation(f[:], f[:], ACT.Ln)
                            act.activation(tiny[:], tiny[:], ACT.Ln, scale=1.0 / SMALL).then_inc(mod_ready.sem, 1)

                        def decays(h):
                            act.wait_ge(aux4.sem, aux4.at(h + 1, i, 2))
                            act.activation(f[:], b[:, h], ACT.Exp)
                            act.activation(e_last[:, h], chunked(b[:, h])[:, :, CHUNK - 1], ACT.Exp)
                            act.activation(tiny[:], tiny[:], ACT.Exp).then_inc(probs.sem, 1)

                        def level(h, n):
                            act.wait_ge(biased.sem, biased.at(7 * h + n + 1, i, 14))
                            act_steps.open(i, 14)
                            act_steps.k = 7 * h + n
                            act_steps.done(act.activation(e[:, n % 2], e[:, n % 2], ACT.Abs))
                            act_steps.wait(act)
                            act.activation(e[:, n % 2], e[:, n % 2], ACT.Exp, scale=-1.0).then_inc(exped.sem, 1)

                        round_chunk(act, 1, i, 6)
                        evict_q(0)
                        round_chunk(act, 2, i, 6)
                        evict_gates(0)
                        round_chunk(act, 3, i, 6)
                        logarithms(0)
                        evict_q(1)
                        round_chunk(act, 4, i, 6)
                        decays(0)
                        level(0, 0)
                        evict_gates(1)
                        round_chunk(act, 5, i, 6)
                        level(0, 1)
                        level(0, 2)
                        logarithms(1)
                        level(0, 3)
                        level(0, 4)
                        decays(1)
                        act.wait_ge(used.sem, after(used, 4, i, 6))
                        act.activation(v_t[:], ps[0][:], ACT.Copy).then_inc(evicted.sem, 1)
                        round_chunk(act, 6, i, 6)
                        level(0, 5)
                        level(0, 6)
                        level(1, 0)
                        act.wait_ge(used.sem, after(used, 5, i, 6))
                        act.activation(g_silu[:], ps[1][:], ACT.Silu).then_inc(evicted.sem, 1)
                        act.wait_ge(transposed.sem, transposed.at(1, i, 3))
                        act.activation(v_tok[:], chunked(ps[0][:]), ACT.Copy).then_inc(tr_evicted.sem, 1)
                        for n in range(1, 7):
                            level(1, n)
                        for h in range(2):
                            act.wait_ge(transposed.sem, transposed.at(2 + h, i, 3))
                            if h == 1:
                                act.wait_ge(pt_ready.sem, pt_ready.at(1, i, 2))
                            act.activation(kd_tok[:], chunked(ps[2][:]), ACT.Copy).then_inc(tr_evicted.sem, 1)
                        act.wait_ge(o_ready.sem, o_ready.at(1, i, 1))
                        act.activation(o_t[:], ps[3][:], ACT.Copy)
                        act.activation(e[:, 0], ps[3][:], ACT.Square).then_inc(sq_ready.sem, 1)
                        act.wait_ge(stat_ready.sem, stat_ready.at(1, i, 2))
                        act.activation(e[:, 1], e[:, 1], ACT.Sqrt).then_inc(norm_ready.sem, 1)
                        act.wait_ge(stat_ready.sem, stat_ready.at(2, i, 2))
                        act.activation(y_hi_t[:, bass.ds(i, 1)], o_t[:].rearrange("p (a t) -> p a t", a=1), ACT.Copy)\
                           .then_inc(y_hi.sem, 1)

                @block.vector
                def _(dve):
                    dve.wait_ge(aux.sem, aux.at(2))
                    dve.wait_ge(side_loaded.sem, side_loaded.at(2))
                    with dve.Fori(0, N) as i:
                        dve_steps.open(i, 2 * 4 + 3)

                        def gates(h):
                            one_minus, low = lb[:, bass.ds(i * 2 + (4 + h), 1)], lb[:, bass.ds(i * 2 + h, 1)]
                            dve.wait_ge(evicted.sem, evicted.at(2 * h + 2, i, 6))
                            dve_steps.done(dve.tensor_scalar(k[:, h], k[:, h], one_minus, None, ALU.mult))
                            dve_steps.done(dve.tensor_scalar(f[:], f[:], one_minus, low, ALU.mult, ALU.add))
                            dve_steps.wait(dve)
                            dve_steps.done(dve.tensor_scalar(tiny[:], f[:], 1e-30, SMALL, ALU.max, ALU.min))
                            dve_steps.wait(dve)
                            dve.tensor_scalar(f[:], f[:], SMALL, None, ALU.max).then_inc(h_ready.sem, 1)

                        def minus_reference(h, dst, size, at, flip):
                            x = b[:, h].rearrange("p (c t) -> p c t", t=size)
                            r = x[:, :, at:at + 1].broadcast_to([P, T // size, size])
                            y = dst.rearrange("p (c t) -> p c t", t=size)
                            return dve.tensor_tensor(y, r if flip else x, x if flip else r, ALU.subtract)

                        def running_sum(h):
                            dve.wait_ge(mod_ready.sem, mod_ready.at(h + 1, i, 2))
                            dve_steps.done(dve.tensor_tensor(f[:], f[:], tiny[:], ALU.add))
                            dve_steps.wait(dve)
                            dve.tensor_tensor_scan(b[:, h], reset[:], f[:], 0.0, ALU.mult, ALU.add).then_inc(aux2.sem, 1)
                            dve.wait_ge(aux2.sem, aux2.at(h + 1, i, 2))
                            minus_reference(h, tiny[:], CHUNK, CHUNK - 1, True).then_inc(aux4.sem, 1)

                        def decayed_queries(h):
                            dve.wait_ge(probs.sem, probs.at(h + 1, i, 2))
                            dve.tensor_tensor(qx[:, h], q[:, h], f[:], ALU.mult).then_inc(o_evicted.sem, 1)

                        def difference(h, n):
                            half = CHUNK >> (n + 1)
                            dve.wait_ge(lo_ready2.sem, lo_ready2.at(7 * h + n - 1, i, 14))
                            dve.wait_ge(y_ready.sem, y_ready.at(7 * h + n - 1, i, 14))
                            minus_reference(h, e[:, n % 2], 2 * half, half - 1, False).then_inc(biased.sem, 1)

                        def take(h, n):
                            dve.wait_ge(evicted2.sem, evicted2.at(8 * h + n, i, 16))
                            dve.wait_ge(scores.sem, scores.at(8 * h + n + 1, i, 16))
                            mask = masks[:, (n - 1) % LEVELS:(n - 1) % LEVELS + 1].broadcast_to([P, NC, CHUNK])
                            if n == 0:
                                dve.tensor_tensor(att[:, h], mask, chunked(ps[2][:]), ALU.mult).then_inc(evicted2.sem, 1)
                            else:
                                carry_wait(0)
                                dve.copy_predicated(att[:, h], mask.bitcast(U32), chunked(ps[2 + n % 2][:])).then_inc(evicted2.sem, 1)

                        gates(0)
                        running_sum(0)
                        difference(0, 0)
                        decayed_queries(0)
                        for h in range(2):
                            if h == 1:
                                difference(1, 0)
                            for n in range(7):
                                if n < 6:
                                    difference(h, n + 1)
                                dve.wait_ge(exped.sem, exped.at(7 * h + n + 1, i, 14))
                                if n == 0:
                                    dve.wait_ge(o_ready.sem, o_ready.at(0, i, 1))
                                dve.wait_ge(scores.sem, scores.at(8 * h + n, i, 16))
                                dve.tensor_tensor(qe[:, n % 2], q[:, h], e[:, n % 2], ALU.mult).then_inc(lo_ready2.sem, 1)
                                take(h, n)
                                if h == 0 and n == 1:
                                    gates(1)
                                if h == 0 and n == 3:
                                    running_sum(1)
                                if h == 0 and n == 5:
                                    decayed_queries(1)
                            take(h, 7)
                        for h in range(2):
                            dve.wait_ge(pt_ready.sem, pt_ready.at(h + 1, i, 2))
                            for c in range(NC - 1):
                                add = ps[1][:, h * HALF + c * 64:h * HALF + c * 64 + 64]
                                if c == 0:
                                    dve.tensor_copy(state[:, h, 1], add).then_inc(pt_evicted.sem, 1)
                                else:
                                    dve.wait_ge(pt_evicted.sem, pt_evicted.at(7 * h + c, i, 14))
                                    dve.scalar_tensor_tensor(out=state[:, h, c + 1], in0=state[:, h, c],
                                                             scalar=e_last[:, h, c:c + 1], in1=add, op0=ALU.mult,
                                                             op1=ALU.add).then_inc(pt_evicted.sem, 1)
                        dve.wait_ge(sum_ready.sem, sum_ready.at(1, i, 1))
                        dve.tensor_scalar(e[:, 1], ps[2][:], 1.0 / 64, EPS, ALU.mult, ALU.add).then_inc(stat_ready.sem, 1)
                        dve.wait_ge(norm_ready.sem, norm_ready.at(1, i, 1))
                        dve_steps.done(dve.reciprocal(e[:, 1], e[:, 1]))
                        dve_steps.wait(dve)
                        dve_steps.done(dve.scalar_tensor_tensor(
                            out=o_t[:], in0=o_t[:], scalar=vec[:, bass.ds(i + COL["hgrn_norm_2"], 1)], in1=e[:, 1],
                            op0=ALU.mult, op1=ALU.mult))
                        dve_steps.wait(dve)
                        dve.tensor_tensor(o_t[:], o_t[:], g_silu[:], ALU.mult).then_inc(stat_ready.sem, 1)
                        dve.wait_ge(stat_ready.sem, stat_ready.at(2, i, 2))
                        dve_steps.done(carry_wait(2))

                @block.tensor
                def _(pe):
                    pe.wait_ge(side_loaded.sem, side_loaded.at(2))
                    with pe.Fori(0, N) as i:
                        for m in range(4):
                            split_ready(pe, m, i, 6)
                            pe.wait_ge(evicted.sem, evicted.at(max(0, m - 1), i, 6))
                            if m == 0:
                                pe.wait_ge(tr_evicted.sem, tr_evicted.at(0, i, 3))
                            product(pe, (m, i, 6), wide(ps[m % 2])).then_inc(used.sem, 1)
                        for h in range(2):
                            pe.wait_ge(h_ready.sem, h_ready.at(h + 1, i, 2))
                            if h == 0:
                                pe.wait_ge(stat_ready.sem, stat_ready.at(0, i, 2))
                            for n in range(8):
                                if n >= 1:
                                    pe.wait_ge(y_ready.sem, y_ready.at(7 * h + n, i, 14))
                                    pe.wait_ge(lo_ready2.sem, lo_ready2.at(7 * h + n, i, 14))
                                pe.wait_ge(evicted2.sem, evicted2.at(8 * h + n - 1, i, 16))
                                for c in range(NC):
                                    cut = slice(c * CHUNK, c * CHUNK + CHUNK)
                                    ks, qs = (k[:, h, cut], q[:, h, cut]) if n == 0 else (ke[:, (n - 1) % 2, cut], qe[:, (n - 1) % 2, cut])
                                    last = pe.matmul(ps[2 + n % 2][:, cut], ks, qs, start=True, stop=True)
                                last.then_inc(scores.sem, 1)
                                if h == 0:
                                    m = 4 + n // 4
                                    if n % 4 == 0:
                                        split_ready(pe, m, i, 6)
                                        pe.wait_ge(evicted.sem, evicted.at(3 + n // 4, i, 6))
                                    last = product(pe, (m, i, 6), wide(ps[m % 2]), part=(n % 4, 4))
                                    if n % 4 == 3:
                                        last.then_inc(used.sem, 1)
                                if h == 1 and n == 0:
                                    pe.wait_ge(evicted.sem, evicted.at(5, i, 6))
                                    for c in range(NC):
                                        last = pe.transpose(ps[0][:, c * P:c * P + P], v_t[:, c * P:c * P + P], ident[:])
                                    last.then_inc(transposed.sem, 1)
                        pe.wait_ge(evicted.sem, evicted.at(6, i, 6))
                        pe.wait_ge(evicted2.sem, evicted2.at(16, i, 16))
                        for h in range(2):
                            if h == 1:
                                pe.wait_ge(tr_evicted.sem, tr_evicted.at(2, i, 3))
                            for c in range(NC):
                                last = pe.transpose(ps[2][:, c * P:c * P + P], kd[:, h, c * P:c * P + P], ident[:])
                            last.then_inc(transposed.sem, 1)
                            pe.wait_ge(tr_evicted.sem, tr_evicted.at(2 + h, i, 3))
                            for c in range(NC - 1):
                                last = pe.matmul(ps[1][:, h * HALF + c * 64:h * HALF + c * 64 + 64], kd_tok[:, c],
                                                 v_tok[:, c, h * 64:h * 64 + 64], start=True, stop=True)
                            last.then_inc(pt_ready.sem, 1)
                        for h in range(2):
                            rows = slice(h * 64, h * 64 + 64)
                            for c in range(NC):
                                cut = slice(c * CHUNK, c * CHUNK + CHUNK)
                                if c >= 1:
                                    pe.wait_ge(pt_evicted.sem, pt_evicted.at(7 * h + c, i, 14))
                                last = pe.matmul(ps[3][rows, cut], v_tok[:, c, rows], att[:, h, c], start=True, stop=(c == 0))
                                if c >= 1:
                                    last = pe.matmul(ps[3][rows, cut], state[:, h, c], qx[:, h, cut], start=False, stop=True)
                        last.then_inc(o_ready.sem, 1)
                        pe.wait_ge(sq_ready.sem, sq_ready.at(1, i, 1))
                        for c in (0, HALF):
                            last = pe.matmul(ps[2][:, c:c + HALF], blocks[:], e[:, 0, c:c + HALF], start=True, stop=True)
                        last.then_inc(sum_ready.sem, 1)

            act_steps.close(0)
            act_steps.counted.passed(14 * N)
            dve_steps.close(N)
            side_loaded.passed(2)
            for s, n in ((aux, 2), (aux2, 2 * N), (aux3, 2 * N), (aux4, 2 * N), (evicted, 6 * N), (evicted2, 16 * N), (h_ready, 2 * N),
                         (mod_ready, 2 * N), (exped, 14 * N), (biased, 14 * N), (scores, 16 * N), (y_ready, 14 * N),
                         (lo_ready2, 14 * N), (probs, 2 * N), (o_evicted, 2 * N),
                         (transposed, 3 * N), (tr_evicted, 3 * N), (pt_ready, 2 * N), (pt_evicted, 14 * N), (o_ready, N),
                         (sq_ready, N), (sum_ready, N), (stat_ready, 2 * N), (norm_ready, N), (y_hi, N), (lo_ready, N)):
                s.passed(n)
            chunk_passed(6 * N)

        def memory_source(i, m):
            return chunk_of(w_in2, m * P + M_Q) if m < 2 else chunk_of(a["w_mem_kv_2"][0], (m - 2) * P)

        def memory_attention(y_hi_t, y_lo_t, following):
            H = BW // DH
            with ExitStack() as sc, nc.Block() as block:
                mem_tok = sb(sc, "mem_tok", [P, 2, D])
                mem32 = sb(sc, "mem32", [P, KT, NMEM])
                mem_hi = sb(sc, "mem_hi", [P, KT, NMEM], F32R)
                mem_lo = sb(sc, "mem_lo", [P, KT, NMEM], F32R)
                power = sb(sc, "power", [P, 2])
                sums = sb(sc, "sums", [P, 2])
                rstd = sb(sc, "rstd", [P, 2])
                q_t = sb(sc, "q_t", [P, 2, T])
                k_t = sb(sc, "k_t", [P, 2, NMEM])
                v_t = sb(sc, "v_t", [P, 2, NMEM])
                v_tok = sb(sc, "v_tok", [P, 2, BW])
                prob = sb(sc, "prob", [P, 2, H, NMEM])
                prob_t = sb(sc, "prob_t", [P, 2, 2 * H, P])
                stat = sb(sc, "stat", [P, 2, 4, H])

                def place(h):
                    return h % 2 * 2 + h // 2

                @block.sync
                def _(sp):
                    sp.dma_start(mem_tok[:], a["mem_2"][0].rearrange("(t p) d -> p t d", p=P)).then_inc(side_loaded.sem, 16)
                    stream(sp, 1, 6, memory_source, following)

                @block.gpsimd
                def _(pool):
                    pool.memset(power[:], -0.5).then_inc(aux.sem, 1)
                    rest_chunk(pool, 1, 0, 6)
                    pool.wait_ge(aux.sem, aux.at(1))
                    pool.wait_ge(stat_ready.sem, stat_ready.at(1))
                    pool.tensor_tensor(rstd[:], sums[:], power[:], ALU.pow).then_inc(norm_ready.sem, 1)
                    for m in range(2, 7):
                        rest_chunk(pool, m, 0, 6)

                @block.scalar
                def _(act):
                    round_chunk(act, 1, 0, 6)
                    act.wait_ge(side_loaded.sem, side_loaded.at(1))
                    for t in range(2):
                        act.activation(prob[:, t].rearrange("p h k -> p (h k)"), mem_tok[:, t], ACT.Square,
                                       accum_out=sums[:, t:t + 1]).then_inc(sq_ready.sem, 1)
                    act.wait_ge(used.sem, after(used, 0, 0, 6))
                    act.activation(q_t[:, 0], ps[0][:], ACT.Copy).then_inc(evicted.sem, 1)
                    round_chunk(act, 2, 0, 6)
                    act.wait_ge(h_ready.sem, h_ready.at(KT))
                    act.activation(mem_hi[:], mem32[:], ACT.Copy).then_inc(hi_ready.sem, 1)
                    act.wait_ge(used.sem, after(used, 1, 0, 6))
                    act.activation(q_t[:, 1], ps[1][:], ACT.Copy).then_inc(evicted.sem, 1)
                    for m in range(3, 7):
                        round_chunk(act, m, 0, 6)
                    act.wait_ge(transposed.sem, transposed.at(3))
                    act.activation(v_tok[:], ps[2][:, 0:2 * BW].rearrange("p (t c) -> p t c", c=BW), ACT.Copy)\
                       .then_inc(tr_evicted.sem, 1)

                    def exps(b):
                        act.wait_ge(biased.sem, biased.at(b + 1))
                        act.wait_ge(pt_ready.sem, pt_ready.at(b - 1))
                        for h in range(H):
                            last = act.activation(prob[:, b % 2, h], ps[b % 2][:, h * NMEM:h * NMEM + NMEM], ACT.Exp,
                                                  bias=stat[:, b % 2, 1, h:h + 1], scale=DH ** -0.5,
                                                  accum_out=stat[:, b % 2, 2, h:h + 1])
                        last.then_inc(exped.sem, 1)

                    def evict_probs(b):
                        act.wait_ge(pt_ready.sem, pt_ready.at(b + 1))
                        act.wait_ge(o_ready.sem, o_ready.at(b - 1))
                        act.activation(prob_t[:, b % 2], ps[2][:].rearrange("p (j c) -> p j c", c=P), ACT.Copy)\
                           .then_inc(pt_evicted.sem, 1)

                    def evict_o(b):
                        act.wait_ge(o_ready.sem, o_ready.at(b + 1))
                        at = b % 2 * HALF
                        act.activation(y_hi_t[:, :, b * P:b * P + P], ps[3][:, at:at + 2 * P].rearrange("p (t c) -> p t c", c=P),
                                       ACT.Copy).then_inc(y_hi.sem, 1)

                    exps(0)
                    for b in range(TT):
                        if b + 1 < TT:
                            exps(b + 1)
                        evict_probs(b)
                        if b >= 1:
                            evict_o(b - 1)
                    evict_o(TT - 1)

                @block.vector
                def _(dve):
                    dve.wait_ge(sq_ready.sem, sq_ready.at(2))
                    dve.tensor_scalar(sums[:], sums[:], 1.0 / D, EPS, ALU.mult, ALU.add).then_inc(stat_ready.sem, 1)
                    dve.wait_ge(norm_ready.sem, norm_ready.at(1))
                    for t in range(2):
                        dve.tensor_scalar(mem_tok[:, t], mem_tok[:, t], rstd[:, t:t + 1], None, ALU.mult).then_inc(sum_ready.sem, 1)
                    for d in range(KT):
                        dve.wait_ge(transposed.sem, transposed.at(1 + d // 4))
                        dve.tensor_scalar(mem32[:, d], ps[2 + d // 4][:, d % 4 * NMEM:(d % 4 + 1) * NMEM],
                                          column("norm_mem_2", d), None, ALU.mult).then_inc(h_ready.sem, 1)
                    dve.wait_ge(hi_ready.sem, hi_ready.at(1))
                    dve.tensor_tensor(mem_lo[:], mem32[:], mem_hi[:].bitcast(F32), ALU.subtract).then_inc(lo_ready.sem, 1)
                    for m in range(4):
                        dve.wait_ge(used.sem, after(used, 2 + m, 0, 6))
                        dve.tensor_copy((k_t, v_t)[m // 2][:, m % 2], ps[2 + m // 2][:, m % 2 * HALF:m % 2 * HALF + NMEM])\
                           .then_inc(evicted2.sem, 1)

                    def maxima(b):
                        dve.wait_ge(scores.sem, scores.at(b + 1))
                        st = stat[:, b % 2]
                        dve_steps.done(dve.reduce_max(st[:, 0], ps[b % 2][:].rearrange("p (h k) -> p h k", k=NMEM), AX))
                        dve_steps.wait(dve)
                        dve.tensor_scalar(st[:, 1], st[:, 0], -DH ** -0.5, None, ALU.mult).then_inc(biased.sem, 1)

                    def normalise(b):
                        st = stat[:, b % 2]
                        dve.wait_ge(exped.sem, exped.at(b + 1))
                        dve_steps.done(dve.reciprocal(st[:, 3], st[:, 2]))
                        dve_steps.wait(dve)
                        dve.tensor_tensor(prob[:, b % 2], prob[:, b % 2],
                                          st[:, 3].rearrange("p (h k) -> p h k", k=1).broadcast_to([P, H, NMEM]),
                                          ALU.mult).then_inc(probs.sem, 1)

                    def rest_o(b):
                        dve.wait_ge(y_hi.sem, y_hi.at(b + 1))
                        at = b % 2 * HALF
                        cols = slice(b * P, b * P + P)
                        dve.tensor_tensor(y_lo_t[:, :, cols], ps[3][:, at:at + 2 * P].rearrange("p (t c) -> p t c", c=P),
                                          y_hi_t[:, :, cols].bitcast(F32), ALU.subtract).then_inc(o_evicted.sem, 1)

                    maxima(0)
                    for b in range(TT):
                        if b + 1 < TT:
                            maxima(b + 1)
                        normalise(b)
                        if b >= 2:
                            rest_o(b - 2)
                    rest_o(TT - 2)
                    rest_o(TT - 1)

                @block.tensor
                def _(pe):
                    split_ready(pe, 0, 0, 6)
                    product(pe, (0, 0, 6), wide(ps[0])).then_inc(used.sem, 1)
                    split_ready(pe, 1, 0, 6)
                    product(pe, (1, 0, 6), wide(ps[1])).then_inc(used.sem, 1)
                    pe.wait_ge(sum_ready.sem, sum_ready.at(2))
                    for d in range(KT):
                        for t in range(2):
                            c = d % 4 * NMEM + t * P
                            last = pe.transpose(ps[2 + d // 4][:, c:c + P], mem_tok[:, t, d * P:d * P + P], ident[:])
                        if d % 4 == 3:
                            last.then_inc(transposed.sem, 1)
                    pe.wait_ge(lo_ready.sem, lo_ready.at(1))
                    for m in range(2, 6):
                        split_ready(pe, m, 0, 6)
                        c = m % 2 * HALF
                        product(pe, (m, 0, 6), [(ps[1 + m // 2][:, c:c + NMEM], lambda k: mem_hi[:, k], lambda k: mem_lo[:, k])])\
                            .then_inc(used.sem, 1)
                    pe.wait_ge(evicted2.sem, evicted2.at(4))
                    for t in range(2):
                        for ft in range(2):
                            c = t * BW + ft * P
                            last = pe.transpose(ps[2][:, c:c + P], v_t[:, ft, t * P:t * P + P], ident[:])
                    last.then_inc(transposed.sem, 1)
                    pe.wait_ge(evicted.sem, evicted.at(2))

                    def score(b):
                        pe.wait_ge(exped.sem, exped.at(b - 1))
                        for h in range(H):
                            rows, c = slice(h % 2 * 64, h % 2 * 64 + 64), place(h) * NMEM
                            last = pe.matmul(ps[b % 2][:, c:c + NMEM], q_t[rows, h // 2, b * P:b * P + P],
                                             k_t[rows, h // 2], start=True, stop=True)
                        last.then_inc(scores.sem, 1)

                    def turn(b):
                        pe.wait_ge(probs.sem, probs.at(b + 1))
                        pe.wait_ge(pt_evicted.sem, pt_evicted.at(b))
                        for j in range(2 * H):
                            last = pe.transpose(ps[2][:, j * P:j * P + P], prob[:, b % 2, j // 2, j % 2 * P:j % 2 * P + P], ident[:])
                        last.then_inc(pt_ready.sem, 1)

                    def weigh(b):
                        pe.wait_ge(pt_evicted.sem, pt_evicted.at(b + 1))
                        pe.wait_ge(o_evicted.sem, o_evicted.at(b - 1))
                        for h in range(H):
                            rows = slice(h % 2 * 64, h % 2 * 64 + 64)
                            c = b % 2 * HALF + h // 2 * P
                            for t in range(2):
                                last = pe.matmul(ps[3][rows, c:c + P], v_tok[:, t, h * DH:h * DH + DH], prob_t[:, b % 2, 2 * place(h) + t],
                                                 start=(t == 0), stop=(t == 1))
                        last.then_inc(o_ready.sem, 1)

                    score(0)
                    score(1)
                    pe.wait_ge(tr_evicted.sem, tr_evicted.at(1))
                    for b in range(TT):
                        if b + 2 < TT:
                            score(b + 2)
                        if b >= 1:
                            weigh(b - 1)
                        turn(b)
                    weigh(TT - 1)

            dve_steps.close()
            side_loaded.passed(1)
            for s, n in ((aux, 1), (sq_ready, 2), (stat_ready, 1), (norm_ready, 1), (sum_ready, 2), (h_ready, KT), (hi_ready, 1),
                         (lo_ready, 1), (evicted, 2), (evicted2, 4), (transposed, 3), (tr_evicted, 1), (scores, TT), (biased, TT),
                         (exped, TT), (probs, TT), (pt_ready, TT), (pt_evicted, TT), (o_ready, TT), (o_evicted, TT), (y_hi, TT)):
                s.passed(n)
            chunk_passed(6)

        SCORED = range(TOPK // P, TT)

        def keys_of(b):
            return (b + 1) * P

        def score_at(b):
            return sum(keys_of(c) for c in SCORED if c < b)

        def indexer_source(i, m):
            return chunk_of(w_in2, (P_Z, P_Z + P, I_Q, I_Q + P, I_Q + 2 * P, I_Q + 3 * P, I_K, S_K)[m])

        def indexer(y_hi_t, y_lo_t, score, kv_t, following):
            H = 8
            PAD = 16
            Z, SUM_A, SUM_B = (0, 3), 1, 2
            IQ = range(2, 6)
            UNSCORED = SCORED[0] * P
            units = [(b, h) for b in SCORED for h in range(H)]
            n_y = len(units)
            with ExitStack() as sc, nc.Block() as block:
                pad = sb(sc, "pad", [P, 4, PAD + T])
                inv_n = sb(sc, "inv_n", [P, 2, PAD])
                iq_parts = sb(sc, "iq_parts", [P, H, T - UNSCORED], F32R)
                kw_t = score[:, 0:T]
                map_w = score[:, T:T + 2 * P].rearrange("p (t c) -> p t c", c=P)
                ik_hi = sb(sc, "ik_hi", [P, T], F32R)
                ik_lo = sb(sc, "ik_lo", [P, T], F32R)
                head_w = sb(sc, "head_w", [P, TT, H])

                @block.sync
                def _(sp):
                    sp.wait_ge(aux.sem, aux.at(1))
                    for g in range(4):
                        half = g % 2 * 64
                        sp.dma_start(map_w[half:half + 64, g // 2, half:half + 64], a["pool_w_2"][0, g]).then_inc(side_loaded.sem, 16)
                    sp.dma_start(inv_n[:], a["k_pool"]).then_inc(side_loaded.sem, 16)
                    stream(sp, 1, 8, indexer_source, following)

                @block.gpsimd
                def _(pool):
                    pool.memset(map_w, 0.0).then_inc(aux.sem, 1)
                    pool.memset(pad[:, :, 0:PAD], 0.0).then_inc(aux.sem, 1)
                    for m in range(8):
                        rest_chunk(pool, m + 1, 0, 8)
                    for t in range(2):
                        pool.wait_ge(y_hi.sem, y_hi.at(t + 1))
                        pool.tensor_tensor(y_lo_t[:, t], pad[:, (SUM_A, SUM_B)[t], PAD:], y_hi_t[:, t].bitcast(F32), ALU.subtract)\
                            .then_inc(lo_ready.sem, 1)

                @block.scalar
                def _(act):
                    targets = {0: pad[:, Z[0], PAD:], 1: pad[:, Z[1], PAD:], 6: kw_t, 7: kv_t[:]}
                    for m in range(8):
                        round_chunk(act, m + 1, 0, 8)
                        act.wait_ge(used.sem, after(used, m, 0, 8))
                        if m in IQ:
                            for odd in range(2):
                                rows = slice(odd * 64, odd * 64 + 64)
                                last = act.activation(iq_parts[rows, 2 * (m - IQ[0]) + odd], ps[m % 4][rows, UNSCORED:], ACT.Copy)
                            last.then_inc(evicted.sem, 1)
                        else:
                            act.activation(targets[m], ps[m % 4][:], ACT.Copy).then_inc(evicted.sem, 1)
                    act.wait_ge(pt_ready.sem, pt_ready.at(1))
                    act.activation(ik_hi[:], ps[2][:], ACT.Copy).then_inc(pt_evicted.sem, 1)
                    for t in range(2):
                        act.wait_ge(y_ready.sem, y_ready.at(t + 1))
                        act.activation(y_hi_t[:, t], pad[:, (SUM_A, SUM_B)[t], PAD:], ACT.Copy).then_inc(y_hi.sem, 1)
                    act.wait_ge(lo_ready.sem, lo_ready.at(2))
                    for n, (b, h) in enumerate(units):
                        act.wait_ge(scores.sem, scores.at(n + 1))
                        act.wait_ge(biased.sem, biased.at(n - 3))
                        act.activation(pad[:, n % 4, 0:keys_of(b)], ps[n % 4][:, 0:keys_of(b)], ACT.Relu).then_inc(exped.sem, 1)

                @block.vector
                def _(dve):
                    dve.wait_ge(side_loaded.sem, side_loaded.at(5))
                    dve.wait_ge(aux.sem, aux.at(2))

                    def doubled(dst, src, shift, rows):
                        dve_steps.wait(dve)
                        dve_steps.done(dve.tensor_tensor(pad[rows, dst, PAD:], pad[rows, src, PAD:],
                                                         pad[rows, src, PAD - shift:PAD + T - shift], ALU.add))

                    every, lower, upper = slice(0, P), slice(0, 64), slice(64, P)
                    for t in range(2):
                        dve.wait_ge(evicted.sem, evicted.at(t + 1))
                        doubled(SUM_A, Z[t], 1, every)
                        if t == 0:
                            doubled(SUM_B, SUM_A, 2, upper)
                        else:
                            doubled(SUM_B, SUM_A, 2, every)
                            doubled(SUM_A, SUM_B, 4, every)
                            doubled(SUM_B, SUM_A, 8, upper)
                        dve_steps.wait(dve)
                        for rows, s in ((lower, SUM_A), (upper, SUM_B)):
                            first, rest = slice(PAD, 2 * PAD), slice(2 * PAD, PAD + T)
                            dve_steps.done(dve.scalar_tensor_tensor(out=pad[rows, Z[t], rest], in0=pad[rows, s, rest],
                                                                    scalar=inv_n[rows, t, PAD - 1:PAD], in1=pad[rows, Z[t], rest],
                                                                    op0=ALU.mult, op1=ALU.subtract))
                            dve_steps.done(dve.tensor_tensor(pad[rows, s, first], pad[rows, s, first], inv_n[rows, t], ALU.mult))
                            dve_steps.wait(dve)
                            last = dve.tensor_tensor(pad[rows, Z[t], first], pad[rows, s, first], pad[rows, Z[t], first], ALU.subtract)
                            if s == SUM_A:
                                dve_steps.done(last)
                            else:
                                last.then_inc(h_ready.sem, 1)
                    for m in IQ:
                        dve.wait_ge(evicted.sem, evicted.at(m + 1))
                        for odd in range(2):
                            rows, other, h = slice(odd * 64, odd * 64 + 64), slice(64 - odd * 64, P - odd * 64), 2 * (m - IQ[0]) + odd
                            last = dve.tensor_tensor(iq_parts[other, h], ps[m % 4][rows, UNSCORED:], iq_parts[rows, h].bitcast(F32),
                                                     ALU.subtract)
                        last.then_inc(aux2.sem, 1)
                    dve.wait_ge(pt_evicted.sem, pt_evicted.at(1))
                    dve.tensor_tensor(ik_lo[:], ps[2][:], ik_hi[:].bitcast(F32), ALU.subtract).then_inc(aux3.sem, 1)
                    for t in range(2):
                        dve.wait_ge(o_ready.sem, o_ready.at(t + 1))
                        dve.tensor_scalar(pad[:, (SUM_A, SUM_B)[t], PAD:], ps[t][:], column("pool_scale_2", t), None, ALU.mult)\
                           .then_inc(y_ready.sem, 1)
                    dve.wait_ge(transposed.sem, transposed.at(1))
                    dve.tensor_scalar(head_w[:], ps[3][:].rearrange("p (t c) -> p t c", c=P)[:, :, 64:64 + H],
                                      DH ** -0.5 * H ** -0.5, None, ALU.mult).then_inc(tr_evicted.sem, 1)
                    dve.wait_ge(tr_evicted.sem, tr_evicted.at(1))
                    for n, (b, h) in enumerate(units):
                        dve.wait_ge(exped.sem, exped.at(n + 1))
                        to, r = score[:, score_at(b):score_at(b) + keys_of(b)], pad[:, n % 4, 0:keys_of(b)]
                        if h == 0:
                            dve.tensor_scalar(to, r, head_w[:, b, 0:1], None, ALU.mult).then_inc(biased.sem, 1)
                        else:
                            dve.wait_ge(biased.sem, biased.at(n))
                            dve.scalar_tensor_tensor(out=to, in0=r, scalar=head_w[:, b, h:h + 1], in1=to,
                                                     op0=ALU.mult, op1=ALU.add).then_inc(biased.sem, 1)
                    dve.wait_ge(biased.sem, biased.at(n_y))
                    for b in SCORED:
                        end = score_at(b) + keys_of(b)
                        dve_steps.done(dve.memset(score[0:64, end - 64:end], NEG))

                @block.tensor
                def _(pe):
                    for m in range(8):
                        split_ready(pe, m, 0, 8)
                        pe.wait_ge(evicted.sem, evicted.at(m - 3))
                        if m - 4 in IQ:
                            pe.wait_ge(aux2.sem, aux2.at(m - 4 - IQ[0] + 1))
                        product(pe, (m, 0, 8), wide(ps[m % 4])).then_inc(used.sem, 1)
                    pe.wait_ge(evicted.sem, evicted.at(7))
                    for c in (0, HALF):
                        for half in (0, 64):
                            last = pe.matmul(ps[2][half:half + 64, c:c + HALF], ident[0:64, 0:64], kw_t[0:64, c:c + HALF],
                                             start=True, stop=True)
                    last.then_inc(pt_ready.sem, 1)
                    pe.wait_ge(evicted.sem, evicted.at(8))
                    for t in range(TT):
                        last = pe.transpose(ps[3][:, t * P:t * P + P], kw_t[:, t * P:t * P + P], ident[:])
                    last.then_inc(transposed.sem, 1)
                    pe.wait_ge(aux2.sem, aux2.at(len(IQ)))
                    for t in range(2):
                        pe.wait_ge(h_ready.sem, h_ready.at(t + 1))
                        for c in (0, HALF):
                            last = pe.matmul(ps[t][:, c:c + HALF], map_w[:, t], pad[:, Z[t], PAD + c:PAD + c + HALF],
                                             start=True, stop=True)
                        last.then_inc(o_ready.sem, 1)
                    pe.wait_ge(y_ready.sem, y_ready.at(2))
                    pe.wait_ge(aux3.sem, aux3.at(1))
                    pe.wait_ge(tr_evicted.sem, tr_evicted.at(1))
                    for n, (b, h) in enumerate(units):
                        pe.wait_ge(exped.sem, exped.at(n - 3))
                        n_keys = keys_of(b)
                        for c in range(0, n_keys, HALF):
                            to = min(c + HALF, n_keys)
                            for part in (ik_hi, ik_lo):
                                last = pe.matmul(ps[n % 4][:, c:to], iq_parts[:, h, b * P - UNSCORED:b * P + P - UNSCORED], part[:, c:to],
                                                 start=part is ik_hi, stop=part is ik_lo)
                        last.then_inc(scores.sem, 1)

            dve_steps.close()
            side_loaded.passed(5)
            for s, n in ((aux, 2), (aux2, len(IQ)), (aux3, 1), (evicted, 8), (pt_ready, 1), (pt_evicted, 1), (transposed, 1), (tr_evicted, 1), (h_ready, 2),
                         (o_ready, 2), (y_ready, 2), (y_hi, 2), (lo_ready, 2), (scores, n_y), (exped, n_y), (biased, n_y)):
                s.passed(n)
            chunk_passed(8)

        def top_rounds(score, best, halves_of):
            per = (len(SCORED) + 1) * sum(n for unit in halves_of for n in unit)

            def part(b):
                return score[:, score_at(b):score_at(b) + keys_of(b)]

            def beside(dve, i, u, place):
                if u == 0 and place == 0:
                    top_steps.open(i, per)
                for _ in range(halves_of[u][place]):
                    marking = top_steps.k // (len(SCORED) + 1) % 2
                    top_steps.wait(dve)
                    top_steps.done(carry_wait(marking))
                    for j, b in enumerate(SCORED):
                        top_steps.done(dve.match_replace(part(b), best[:, j], part(b), TAKEN) if marking else
                                       dve.max(best[:, j], part(b)))
            return beside

        def sparse_source(i, m):
            return chunk_of(w_in2, m * P + S_Q)

        def sparse_attention(y_hi_t, y_lo_t, score, kv_t, following):
            H = BW // DH
            order = (0, 7, 1, 6, 2, 5, 3, 4)
            turns = [(n, j) for n, b in enumerate(order) for j in range(b + 1)]
            with ExitStack() as sc, nc.Block() as block:
                q_parts = sb(sc, "q_parts", [P, H, T], F32R)
                k_hi = sb(sc, "k_hi", [P, T], F32R)
                k_lo = sb(sc, "k_lo", [P, T], F32R)
                v_two = kv_t[:].rearrange("p (t a c) -> p t a c", a=2, c=DH)
                edge = y_lo_t[:, 0, 3 * P:3 * P + keys_of(1)].bitcast(F32)
                prob_n = max(keys_of(b) + keys_of(c) for b, c in zip(order, order[1:]))
                prob = sb(sc, "prob", [P, H, prob_n])
                prob_t = sb(sc, "prob_t", [P, 2, H * P])
                stat = sb(sc, "stat", [P, 2, 4, H])

                def place(h):
                    return h % 2 * 2 + h // 2

                def out_of(n, half):
                    c = n % 2 * HALF + half * 2 * P
                    return ps[3][half * 64:half * 64 + 64, c:c + 2 * P].rearrange("p (t c) -> p t c", c=P)

                def pieces(n):
                    cuts = [*range(0, order[n], 2), order[n] + 1]
                    return list(zip(cuts, cuts[1:])) if order[n] else [(0, 1)]

                def prob_of(n):
                    first = 0 if n % 2 else prob_n - keys_of(order[n])
                    return prob[:, :, first:first + keys_of(order[n])]

                @block.sync
                def _(sp):
                    stream(sp, 1, 2, sparse_source, following)

                @block.gpsimd
                def _(pool):
                    pool.memset(edge, 0.0).then_inc(aux.sem, 1)
                    pool.wait_ge(aux.sem, aux.at(1))
                    pool.memset(edge[0:64, keys_of(1) - 64:], NEG).then_inc(aux.sem, 1)
                    for m in range(2):
                        rest_chunk(pool, m + 1, 0, 2)

                @block.scalar
                def _(act):
                    act.wait_ge(transposed.sem, transposed.at(1))
                    act.activation(k_hi[:], ps[2][:], ACT.Copy).then_inc(tr_evicted.sem, 1)
                    v = ps[3][:].rearrange("p (t c) -> p t c", c=P)[:, :, DH:]
                    for n in range(2):
                        last = act.activation(v_two[:, :, n], v, ACT.Copy)
                    last.then_inc(tr_evicted.sem, 1)
                    for m in range(2):
                        round_chunk(act, m + 1, 0, 2)
                        act.wait_ge(used.sem, after(used, m, 0, 2))
                        for odd in range(2):
                            rows = slice(odd * 64, odd * 64 + 64)
                            last = act.activation(q_parts[rows, 2 * m + odd], ps[m][rows], ACT.Copy)
                        last.then_inc(evicted.sem, 1)

                    def exps(n, h):
                        act.wait_ge(mod_ready.sem, mod_ready.at(n * H + h + 1))
                        x = prob_of(n)[:, h]
                        act.activation(x, x, ACT.Exp, bias=stat[:, n % 2, 1, h:h + 1],
                                       accum_out=stat[:, n % 2, 2, h:h + 1]).then_inc(exped.sem, 1)

                    for h in range(H):
                        exps(0, h)
                    for n, b in enumerate(order):
                        heads = list(range(H)) if n + 1 < TT else []
                        for j in range(b + 1):
                            if j >= 2 and heads:
                                exps(n + 1, heads.pop(0))
                            x = turns.index((n, j))
                            act.wait_ge(pt_ready.sem, pt_ready.at(x + 1))
                            act.wait_ge(o_ready.sem, o_ready.at(x - 1))
                            act.activation(prob_t[:, x % 2], ps[2][:, x % 2 * HALF:x % 2 * HALF + HALF], ACT.Copy)\
                               .then_inc(pt_evicted.sem, 1)
                        for h in heads:
                            exps(n + 1, h)
                        act.wait_ge(o_ready.sem, o_ready.at(turns.index((n, b)) + 1))
                        for half in range(2):
                            rows = slice(half * 64, half * 64 + 64)
                            last = act.activation(y_hi_t[rows, :, b * P:b * P + P], out_of(n, half), ACT.Copy)
                        last.then_inc(y_hi.sem, 1)

                @block.vector
                def _(dve):
                    dve.wait_ge(tr_evicted.sem, tr_evicted.at(1))
                    dve.tensor_tensor(k_lo[:], ps[2][:], k_hi[:].bitcast(F32), ALU.subtract).then_inc(aux2.sem, 1)
                    dve.wait_ge(aux.sem, aux.at(2))
                    for b in SCORED:
                        x = score[:, score_at(b):score_at(b) + keys_of(b)]
                        dve_steps.done(dve.tensor_scalar(x, x, TAKEN, NEG, ALU.not_equal, ALU.mult))
                    for m in range(2):
                        dve.wait_ge(evicted.sem, evicted.at(m + 1))
                        for odd in range(2):
                            rows, other, h = slice(odd * 64, odd * 64 + 64), slice(64 - odd * 64, P - odd * 64), 2 * m + odd
                            last = dve.tensor_tensor(q_parts[other, h], ps[m][rows], q_parts[rows, h].bitcast(F32), ALU.subtract)
                        last.then_inc(aux3.sem, 1)
                    dve_steps.wait(dve)

                    def mask(b):
                        if b in SCORED:
                            return score[:, score_at(b):score_at(b) + keys_of(b)]
                        return edge[:, keys_of(1) - keys_of(b):]

                    def bias_scores(n, heads):
                        b = order[n]
                        if n >= 2:
                            dve.wait_ge(pt_ready.sem, pt_ready.at(turns.index((n - 1, 0))))
                        for h in heads:
                            x = n * H + h
                            dve.wait_ge(scores.sem, scores.at(x + 1))
                            dve.tensor_tensor_reduce(prob_of(n)[:, h], ps[x % 2][:, 0:keys_of(b)], mask(b), DH ** -0.5, -3e38,
                                                     ALU.add, ALU.max, stat[:, n % 2, 0, h:h + 1]).then_inc(biased.sem, 1)
                            dve.wait_ge(biased.sem, biased.at(x + 1))
                            dve.tensor_scalar(stat[:, n % 2, 1, h:h + 1], stat[:, n % 2, 0, h:h + 1], -1.0, None, ALU.mult)\
                               .then_inc(mod_ready.sem, 1)

                    def normalise(n):
                        dve.wait_ge(exped.sem, exped.at(n * H + H))
                        dve_steps.done(dve.reciprocal(stat[:, n % 2, 3], stat[:, n % 2, 2]))
                        dve_steps.wait(dve)
                        for first, to in pieces(n):
                            x = prob_of(n)[:, :, first * P:to * P]
                            dve.tensor_tensor(x, x, stat[:, n % 2, 3].rearrange("p (h k) -> p h k", k=1).broadcast_to(list(x.shape)),
                                              ALU.mult).then_inc(probs.sem, 1)

                    def rest_o(n):
                        dve.wait_ge(y_hi.sem, y_hi.at(n + 1))
                        b = order[n]
                        for half in range(2):
                            rows = slice(half * 64, half * 64 + 64)
                            last = dve.tensor_tensor(y_lo_t[rows, :, b * P:b * P + P], out_of(n, half),
                                                     y_hi_t[rows, :, b * P:b * P + P].bitcast(F32), ALU.subtract)
                        last.then_inc(o_evicted.sem, 1)

                    bias_scores(0, range(H))
                    for n in range(TT):
                        if n + 1 < TT:
                            bias_scores(n + 1, (0, 1))
                        normalise(n)
                        if n + 1 < TT:
                            bias_scores(n + 1, (2, 3))
                        if n >= 1:
                            rest_o(n - 1)
                    rest_o(TT - 1)

                @block.tensor
                def _(pe):
                    for c in (0, HALF):
                        for half in (0, 64):
                            pe.matmul(ps[2][half:half + 64, c:c + HALF], ident[0:64, 0:64], kv_t[0:64, c:c + HALF],
                                      start=True, stop=True)
                    for t in range(TT):
                        last = pe.transpose(ps[3][:, t * P:t * P + P], kv_t[:, t * P:t * P + P], ident[:])
                    last.then_inc(transposed.sem, 1)
                    for m in range(2):
                        split_ready(pe, m, 0, 2)
                        product(pe, (m, 0, 2), wide(ps[m])).then_inc(used.sem, 1)
                    pe.wait_ge(aux3.sem, aux3.at(2))
                    pe.wait_ge(aux2.sem, aux2.at(1))
                    pe.wait_ge(tr_evicted.sem, tr_evicted.at(2))

                    def score_heads(n, h0):
                        n_keys = keys_of(order[n])
                        for odd in range(2):
                            pe.wait_ge(biased.sem, biased.at(n * H + h0 + odd - 1))
                            for c in range(0, n_keys, HALF):
                                to = min(c + HALF, n_keys)
                                for part in (k_hi, k_lo):
                                    last = pe.matmul(ps[odd][:, c:to], q_parts[:, h0 + odd, order[n] * P:order[n] * P + P], part[:, c:to],
                                                     start=part is k_hi, stop=part is k_lo)
                            last.then_inc(scores.sem, 1)

                    def turn(n, j):
                        x = turns.index((n, j))
                        pe.wait_ge(pt_evicted.sem, pt_evicted.at(x - 1))
                        for h in range(H):
                            c = x % 2 * HALF + place(h) * P
                            last = pe.transpose(ps[2][:, c:c + P], prob_of(n)[:, h, j * P:j * P + P], ident[:])
                        last.then_inc(pt_ready.sem, 1)

                    def weigh(n, j):
                        x = turns.index((n, j))
                        pe.wait_ge(pt_evicted.sem, pt_evicted.at(x + 1))
                        if j == 0:
                            pe.wait_ge(o_evicted.sem, o_evicted.at(n - 1))
                        pe.matmul(ps[3][:, n % 2 * HALF:n % 2 * HALF + HALF], v_two[:, j].rearrange("p a c -> p (a c)"), prob_t[:, x % 2],
                                  start=(j == 0), stop=(j == order[n])).then_inc(o_ready.sem, 1)

                    score_heads(0, 0)
                    score_heads(0, 2)
                    for n in range(TT):
                        if n + 1 < TT:
                            score_heads(n + 1, 0)
                        normed = sum(len(pieces(o)) for o in range(n))
                        for j in range(order[n] + 1):
                            if j in [first for first, _ in pieces(n)]:
                                normed += 1
                                pe.wait_ge(probs.sem, probs.at(normed))
                            turn(n, j)
                            if j >= 1:
                                weigh(n, j - 1)
                            if j == min(2, order[n]) and n + 1 < TT:
                                score_heads(n + 1, 2)
                        weigh(n, order[n])

            dve_steps.close()
            X = len(turns)
            for s, n in ((aux, 2), (aux2, 1), (aux3, 2), (transposed, 1), (tr_evicted, 2), (evicted, 2), (scores, TT * H), (biased, TT * H), (mod_ready, TT * H),
                         (exped, TT * H), (probs, sum(len(pieces(n)) for n in range(TT))), (pt_ready, X), (pt_evicted, X), (o_ready, X), (o_evicted, TT), (y_hi, TT)):
                s.passed(n)
            chunk_passed(2)

        w_gate_up, w_down = a["w_ffn_gate_up_2"][0], a["w_ffn_down_2"][0]

        def down_rows(f):
            src = w_down.rearrange("(f p) n -> p f n", p=P)[:, bass.ds(f, 1)]
            return lambda slot: (slot.rearrange("p k n -> p (k n)").rearrange("p (a n) -> p a n", a=1), src)

        def ffn_source(i, m):
            return chunk_of(w_gate_up, m * DFF)

        def ffn(acc, following):
            N = (FT - 2) // 2

            def loop_source(i, m):
                tile = i * (2 * P) + (1 + m // 3) * P
                return down_rows(i * 2 + m // 3) if m % 3 == 2 else chunk_of(w_gate_up, tile + m % 3 * DFF)

            def end_source(i, m):
                return chunk_of(w_gate_up, (FT - 1) * P + m * DFF) if m < 2 else down_rows(FT - 2 + m - 2)

            begin = chunks[0]

            def sections(engine, body):
                chunks[0] = begin
                body(0, 2, 0, (("gate", 0), ("up", 0)))
                chunks[0] = begin + 2
                with engine.Fori(0, N) as i:
                    body(i, 6, 2, (("gate", 1), ("up", 1), ("down", 0), ("gate", 2), ("up", 2), ("down", 1)))
                chunks[0] = begin + 2 + 6 * N
                body(0, 4, 0, (("gate", FT - 1), ("up", FT - 1), ("down", FT - 2), ("down", FT - 1)))
                chunks[0] = begin

            with ExitStack() as sc, nc.Block() as block:
                outs = [ps[n] for n in (2, 3, 0, 2, 3, 0, 2, 3)]
                gate = sb(sc, "gate", [P, T])
                act32 = sb(sc, "act32", [P, T])
                act_hi = sb(sc, "act_hi", [P, 2, T], F32R)
                act_lo = sb(sc, "act_lo", [P, 2, T], F32R)

                @block.sync
                def _(sp):
                    stream(sp, 1, 2, ffn_source, loop_source)
                    chunks[0] = begin + 2
                    stream(sp, N, 6, loop_source, end_source)
                    chunks[0] = begin + 2 + 6 * N
                    stream(sp, 1, 4, end_source, following)
                    chunks[0] = begin

                @block.gpsimd
                def _(pool):
                    pool.memset(acc[:], 0.0).then_inc(aux.sem, 1)

                    def body(i, per, n, parts):
                        for m, (part, f) in enumerate(parts):
                            if following or parts[-1] != ("down", FT - 1) or m + 1 < per:
                                rest_chunk(pool, m + 1, i, per)
                            if part == "up":
                                pool.wait_ge(y_hi.sem, y_hi.at(f + 1, i, n))
                                pool.tensor_tensor(act_lo[:, f % 2], act32[:], act_hi[:, f % 2].bitcast(F32), ALU.subtract)\
                                    .then_inc(lo_ready.sem, 1)
                    sections(pool, body)

                @block.scalar
                def _(act):
                    def body(i, per, n, parts):
                        for m, (part, f) in enumerate(parts):
                            if following or parts[-1] != ("down", FT - 1) or m + 1 < per:
                                round_chunk(act, m + 1, i, per)
                            if part == "gate":
                                act.wait_ge(used.sem, after(used, m, i, per))
                                act.wait_ge(h_ready.sem, h_ready.at(f, i, n))
                                act.activation(gate[:], ps[0][:], ACT.Silu).then_inc(evicted.sem, 1)
                            if part == "up":
                                act.wait_ge(h_ready.sem, h_ready.at(f + 1, i, n))
                                act.wait_ge(used.sem, after(used, m - 2, i, per))
                                act.activation(act_hi[:, f % 2], act32[:], ACT.Copy).then_inc(y_hi.sem, 1)
                    sections(act, body)

                @block.vector
                def _(dve):
                    dve.wait_ge(aux.sem, aux.at(1))

                    def body(i, per, n, parts):
                        for m, (part, f) in enumerate(parts):
                            if part == "up":
                                dve.wait_ge(evicted.sem, evicted.at(f + 1, i, n))
                                dve.wait_ge(used.sem, after(used, m, i, per))
                                dve.wait_ge(lo_ready.sem, lo_ready.at(f, i, n))
                                dve.tensor_tensor(act32[:], gate[:], ps[1][:], ALU.mult).then_inc(h_ready.sem, 1)
                            if part == "down":
                                for o in range(KT):
                                    if o < KT - 1:
                                        dve.wait_ge(o_ready.sem, o_ready.at((KT - 1) * f + o + 1, i, (KT - 1) * n))
                                    else:
                                        dve.wait_ge(used.sem, after(used, m, i, per))
                                    dve.wait_ge(o_evicted.sem, o_evicted.at(8 * f + o - 7 if f or n else 0, i, 8 * n))
                                    dve.tensor_tensor(acc[:, o], acc[:, o], outs[o][:], ALU.add).then_inc(o_evicted.sem, 1)
                    sections(dve, body)

                @block.tensor
                def _(pe):
                    def body(i, per, n, parts):
                        for m, (part, f) in enumerate(parts):
                            split_ready(pe, m, i, per)
                            if part == "gate":
                                pe.wait_ge(evicted.sem, evicted.at(f, i, n))
                                if f >= 1:
                                    pe.wait_ge(o_evicted.sem, o_evicted.at(8 * (f - 2) + 6, i, 8 * n))
                                product(pe, (m, i, per), wide(ps[0])).then_inc(used.sem, 1)
                            if part == "up":
                                pe.wait_ge(h_ready.sem, h_ready.at(f, i, n))
                                product(pe, (m, i, per), wide(ps[1])).then_inc(used.sem, 1)
                            if part == "down":
                                pe.wait_ge(lo_ready.sem, lo_ready.at(f + 1, i, n))
                                for o in range(KT):
                                    if o == KT // 2:
                                        split_ready(pe, m, i, per, half=1)
                                    if o == 2:
                                        pe.wait_ge(evicted.sem, evicted.at(min(f + 2, FT), i, n))
                                    else:
                                        pe.wait_ge(o_evicted.sem, o_evicted.at(8 * f + (o - 1 if o < 2 else o - 2), i, 8 * n))
                                    for w, x in ((w_hi, act_hi), (w_hi, act_lo), (w_lo, act_hi)):
                                        for c in (0, HALF):
                                            last = pe.matmul(outs[o][:, c:c + HALF], w[:, m % 2, o], x[:, f % 2, c:c + HALF],
                                                             start=(w is w_hi and x is act_hi), stop=(w is w_lo))
                                    last.then_inc(o_ready.sem if o < KT - 1 else used.sem, 1)
                    sections(pe, body)

            aux.passed(1)
            for s, n in ((evicted, FT), (h_ready, FT), (y_hi, FT), (lo_ready, FT), (o_ready, (KT - 1) * FT), (o_evicted, KT * FT)):
                s.passed(n)
            chunk_passed(3 * FT)

        def finish(acc, res):
            with ExitStack() as sc, nc.Block() as block:
                sq = sb(sc, "sq", [P, 2, T])
                inv = sb(sc, "inv", [P, T])

                @block.sync
                def _(sp):
                    for d in range(KT):
                        sp.wait_ge(tr_evicted.sem, tr_evicted.at(d + 1))
                        sp.dma_start(out.rearrange("(t p) d -> p t d", p=P)[:, :, d * P:d * P + P],
                                     res[:, d].rearrange("p (t c) -> p t c", c=P)).then_inc(stored.sem, 16)
                    sp.wait_ge(stored.sem, stored.at(KT))

                def add_residual(engine, d):
                    engine.wait_ge(biased.sem, biased.at(d + 1))
                    engine.tensor_tensor(acc[:, d], acc[:, d], res[:, d], ALU.add).then_inc((y_ready, y_ready2)[d % 2].sem, 1)

                @block.gpsimd
                def _(pool):
                    for d in range(0, KT, 2):
                        add_residual(pool, d)

                @block.scalar
                def _(act):
                    for d in range(KT):
                        act.wait_ge(sum_ready.sem, sum_ready.at(d - 1))
                        act.activation(sq[:, d % 2], acc[:, d], ACT.Square).then_inc(sq_ready.sem, 1)
                    act.wait_ge(stat_ready.sem, stat_ready.at(1))
                    act.activation(inv[:], inv[:], ACT.Sqrt).then_inc(norm_ready.sem, 1)
                    for d in range(KT):
                        act.wait_ge(transposed.sem, transposed.at(d + 1))
                        act.activation(res[:, d], ps[d % 2][:], ACT.Copy).then_inc(tr_evicted.sem, 1)

                @block.vector
                def _(dve):
                    dve.wait_ge(sum_ready.sem, sum_ready.at(KT))
                    dve.tensor_scalar(inv[:], ps[3][:], 1.0 / D, EPS, ALU.mult, ALU.add).then_inc(stat_ready.sem, 1)
                    dve.wait_ge(norm_ready.sem, norm_ready.at(1))
                    dve_steps.done(dve.reciprocal(inv[:], inv[:]))
                    dve_steps.wait(dve)
                    for d in range(KT):
                        dve.scalar_tensor_tensor(out=acc[:, d], in0=acc[:, d], scalar=column("norm_ffn_post_2", d),
                                                 in1=inv[:], op0=ALU.mult, op1=ALU.mult).then_inc(biased.sem, 1)
                        if d % 2:
                            add_residual(dve, d)

                @block.tensor
                def _(pe):
                    for d in range(KT):
                        pe.wait_ge(sq_ready.sem, sq_ready.at(d + 1))
                        for c in (0, HALF):
                            last = pe.matmul(ps[3][:, c:c + HALF], ones[:], sq[:, d % 2, c:c + HALF], start=(d == 0), stop=(d == KT - 1))
                        last.then_inc(sum_ready.sem, 1)
                    for d in range(KT):
                        half = (y_ready, y_ready2)[d % 2]
                        pe.wait_ge(half.sem, half.at(d // 2 + 1))
                        pe.wait_ge(tr_evicted.sem, tr_evicted.at(d - 1))
                        for t in range(TT):
                            last = pe.transpose(ps[d % 2][:, t * P:t * P + P], acc[:, d, t * P:t * P + P], ident[:])
                        last.then_inc(transposed.sem, 1)

        rpb_rows = nc.dram_tensor("rpb_rows", [8 * N_DR, P], F32, kind="Internal").ap()
        x2_kept = nc.dram_tensor("x2_kept", [P, KT, T], F32, kind="Internal").ap()
        w_out1, w_out2 = a["w_out"][0], a["w_out_2"][0]
        with ExitStack() as first:
            with ExitStack() as branch:
                y_hi_t = sb(branch, "y_hi_t", [P, WB // P, T], F32R)
                y_lo_t = sb(branch, "y_lo_t", [P, WB // P, T], F32R)
                b_in = COL["b_in"]
                from_c, from_a, from_f = (
                    [(w_in, col, b_in + col // P, a[name][0], WB // P, y_hi_t, y_lo_t)]
                    for name, col in (("w_br_c", G_C), ("w_br_a", G_A), ("w_br_f", G_F)))
                with ExitStack() as attended:
                    hc_hi = sb(attended, "hc_hi", [P, KT, CTX], F32R)
                    hc_lo = sb(attended, "hc_lo", [P, KT, CTX], F32R)
                    setup(hc_hi, hc_lo, rpb_rows)
                    attention(hc_hi, hc_lo, rpb_rows, y_hi_t, y_lo_t, merge_source(from_c))
                acc = sb(first, "acc", [P, KT, T], side="right")
                with ExitStack() as gated:
                    residual_gate = sb(gated, "residual_gate", [P, KT, D])
                    merge(acc, from_c, False, conv_source, residual_gate=residual_gate)
                convolution(y_hi_t, y_lo_t, merge_source(from_a))
                merge(acc, from_a, True, fourier_source)
                fourier(y_hi_t, y_lo_t, merge_source(from_f))
                res = sb(first, "res", [P, KT, T], side="right")

                def load_x(sp):
                    sp.dma_start(res[:], a["x"][0].rearrange("(t p) d -> p t d", p=P)).then_inc(x_loaded.sem, 16)

                merge(acc, from_f, True, project_source(w_out1), early=load_x)
            project(w_out1, acc, res, True, ("final_g", "norm_mix_pre_2"), hgrn_source, x2_kept)
        with ExitStack() as second:
            with ExitStack() as early3:
                def pair(n):
                    return [sb(early3, f"y{n}_{part}", [P, BW // P, T], F32R, side="right") for part in ("hi", "lo")]

                ya_hi, ya_lo = pair("a")
                hgrn(ya_hi, ya_lo, memory_source)
                ym_hi, ym_lo = pair("m")
                memory_attention(ym_hi, ym_lo, indexer_source)
                yb_hi, yb_lo = pair("b")

                def branch2(n, y_hi, y_lo):
                    return (w_gate2[n], 0, None, w_branch2[n], BW // P, y_hi, y_lo)

                from_abm = [branch2(0, ya_hi, ya_lo), branch2(1, yb_hi, yb_lo), branch2(3, ym_hi, ym_lo)]
                score = sb(second, "score", [P, score_at(TT)])
                kv_t = sb(second, "kv_t", [P, T])
                indexer(yb_hi, yb_lo, score, kv_t, merge_source(from_abm))
                acc = sb(second, "acc", [P, KT, T])
                best = sb(second, "best", [P, len(SCORED), 8])
                merge(acc, from_abm, False, sparse_source, beside=top_rounds(score, best, ((1, 2), (1, 2), (1, 1)) * 2))
                top_steps.close(KT // 2)
            with ExitStack() as late:
                yc_hi, yc_lo = (sb(late, f"yc_{part}", [P, BW // P, T], F32R, side="right") for part in ("hi", "lo"))
                from_y = [branch2(2, yc_hi, yc_lo)]
                sparse_attention(yc_hi, yc_lo, score, kv_t, merge_source(from_y))
                res = sb(second, "res", [P, KT, T])

                def load_x2(sp):
                    sp.dma_start(res[:], x2_kept).then_inc(x_loaded.sem, 16)

                merge(acc, from_y, True, project_source(w_out2), early=load_x2)
            project(w_out2, acc, res, False, ("norm_mix_post_2", "norm_ffn_pre_2"), ffn_source)
            ffn(acc, None)
            finish(acc, res)


_INS = ["x", "c", "ctx", "c_ctx", "norm_g", "w_ada", "b_ada", "w_in", "b_in", "w_conv", "b_conv", "rpb", "w_br_a",
        "w_br_f", "w_br_c", "w_out", "final_g", "mem_2", "lb_logits_2", "w_in_2", "w_gate_2", "w_branch_2", "w_out_2",
        "hgrn_norm_2", "pool_w_2", "pool_scale_2", "w_mem_kv_2", "norm_mem_2", "norm_mix_pre_2", "norm_mix_post_2",
        "norm_ffn_pre_2", "norm_ffn_post_2", "w_ffn_gate_up_2", "w_ffn_down_2"]


def kernel(**inputs):
    import concourse.bacc as _bacc
    from concourse.bass_utils import run_bass_kernel_spmd as _run

    nc = _bacc.Bacc("TRN2", target_bir_lowering=False, num_devices=1)
    arrays, args = {}, {}
    for name in _INS:
        arrays[f"in_{name}"] = np.ascontiguousarray(inputs[name])
    arrays.update(constants())
    for name, x in arrays.items():
        ap = nc.dram_tensor(name, x.shape, mybir.dt.from_np(x.dtype), kind="ExternalInput").ap()
        args[name.removeprefix("in_")] = ap
    out = nc.dram_tensor("out", [T, D], F32, kind="ExternalOutput").ap()
    first_then_second_block(nc, args, out)
    r = _run(nc, [arrays], core_ids=[0])
    return r.results[0]["out"].reshape(1, T, D)
```
